# Optimizing a Trainium2 kernel written in Bass

```python
import jax
import jax.numpy as jnp
from jax import lax
import numpy as np

D_MODEL = 1024
BATCH = 1
SEQ = 512
DEPTH = 2

HEAD_DIM = 64
MIX_WIDTH = D_MODEL // 4
N_BRANCH = 4
NORM_EPS = 1e-6
MASK_VALUE = -1e9
EXP_CLIP = 60.0

HG_HEADS = MIX_WIDTH // HEAD_DIM
GLA_HEADS = 4
GLA_DV = MIX_WIDTH // GLA_HEADS
GLA_DK = GLA_DV // 2
GLA_RANK = 16
GLA_TAU = 16.0
CHUNK = 64
RW_HEADS = MIX_WIDTH // HEAD_DIM
RW_DECAY_LORA = 32
RW_AAA_LORA = 32
RW_MV_LORA = 32
RW_GATE_LORA = 64
RW_GN_EPS = 64e-5
DIL_PAIRS = ((128, 1), (512, 4), (2048, 16))
N_DIL = 3
AT_HEADS = MIX_WIDTH // HEAD_DIM
AT_WIDTH = N_DIL * AT_HEADS * HEAD_DIM
Q_BLOCK = 128
ROPE_THETA = 10000.0
D_FF = 11 * D_MODEL // 4
CONV_W = 3

HG_WIDTH = 4 * MIX_WIDTH
GLA_WIDTH = 2 * GLA_HEADS * GLA_DK + 2 * MIX_WIDTH + GLA_RANK
RW_WIDTH = 3 * MIX_WIDTH + RW_DECAY_LORA + RW_AAA_LORA + RW_GATE_LORA
GATE_WIDTH = N_BRANCH * D_MODEL
N_IN = HG_WIDTH + GLA_WIDTH + RW_WIDTH + 3 * AT_WIDTH + GATE_WIDTH

kernel_name = "hybrid_hgrn2_gla_rwkv7_dilated_gated_merge"

F32 = jnp.float32

def _split(z, widths):
    out, off = [], 0
    for w in widths:
        out.append(z[..., off:off + w])
        off += w
    return out

def rmsnorm(x, w):
    xf = x.astype(F32)
    y = xf * lax.rsqrt(jnp.mean(xf * xf, axis=-1, keepdims=True) + NORM_EPS)
    return (y * w).astype(x.dtype)

def head_rmsnorm(o, n_heads, w):
    B, S, W = o.shape
    of = o.astype(F32).reshape(B, S, n_heads, W // n_heads)
    of = of * lax.rsqrt(jnp.mean(of * of, axis=-1, keepdims=True) + NORM_EPS)
    return (of.reshape(B, S, W) * w).astype(o.dtype)

def to_heads(t, n_heads):
    B, S, W = t.shape
    return t.reshape(B, S, n_heads, W // n_heads).transpose(0, 2, 1, 3)

def from_heads(t):
    B, H, S, Dh = t.shape
    return t.transpose(0, 2, 1, 3).reshape(B, S, H * Dh)

def chunk_gated_linear_attn(q, k, v, log_g):
    B, H, S, Dk = q.shape
    Dv = v.shape[-1]
    nc = S // CHUNK

    def to_chunks(t):
        return jnp.moveaxis(t.astype(F32).reshape(B, H, nc, CHUNK, t.shape[-1]), 2, 0)

    xs = (to_chunks(q), to_chunks(k), to_chunks(v), to_chunks(log_g))
    causal = jnp.tril(jnp.ones((CHUNK, CHUNK), dtype=bool))[:, :, None]

    def step(state, inp):
        qb, kb, vb, gb = inp
        b = jnp.cumsum(gb, axis=2)
        diff = b[:, :, :, None, :] - b[:, :, None, :, :]
        decay = jnp.where(causal, jnp.exp(jnp.where(causal, diff, 0.0)), 0.0)
        scores = jnp.einsum('bhtd,bhsd,bhtsd->bhts', qb, kb, decay)
        o = jnp.einsum('bhts,bhsv->bhtv', scores, vb) + jnp.einsum('bhtk,bhkv->bhtv', qb * jnp.exp(b), state)
        b_last = b[:, :, -1:, :]
        k_dec = kb * jnp.exp(b_last - b)
        state = jnp.exp(b_last[:, :, 0, :, None]) * state + jnp.einsum('bhsk,bhsv->bhkv', k_dec, vb)
        return state, o

    s0 = jnp.zeros((B, H, Dk, Dv), F32)
    _, o = lax.scan(step, s0, xs)
    return jnp.moveaxis(o, 0, 2).reshape(B, H, S, Dv).astype(v.dtype)

def hgrn2_mixer(z, lb, norm_w):
    q_raw, f_raw, i_raw, g_raw = _split(z, (MIX_WIDTH,) * 4)
    fz = f_raw.astype(F32)
    log_f = jax.nn.log_sigmoid(fz) + jnp.log1p(lb * jnp.exp(jnp.minimum(-fz, EXP_CLIP)))
    k = (1.0 - lb) * jax.nn.sigmoid(-fz)
    q = jax.nn.silu(q_raw)
    o = chunk_gated_linear_attn(to_heads(q, HG_HEADS), to_heads(k, HG_HEADS),
                                to_heads(i_raw, HG_HEADS), to_heads(log_f, HG_HEADS))
    return head_rmsnorm(from_heads(o), HG_HEADS, norm_w) * jax.nn.sigmoid(g_raw)

def gla_mixer(z, a_w2, a_b, norm_w):
    q, k, v, g, a_low = _split(z, (GLA_HEADS * GLA_DK, GLA_HEADS * GLA_DK, MIX_WIDTH, MIX_WIDTH, GLA_RANK))
    log_alpha = jax.nn.log_sigmoid((a_low @ a_w2 + a_b).astype(F32)) / GLA_TAU
    o = chunk_gated_linear_attn(to_heads(q, GLA_HEADS) * (GLA_DK ** -0.5), to_heads(k, GLA_HEADS),
                                to_heads(v, GLA_HEADS), to_heads(log_alpha, GLA_HEADS))
    return head_rmsnorm(from_heads(o), GLA_HEADS, norm_w) * jax.nn.silu(g)

def rwkv7_scan(r, w, k, v, kk, a):
    B, S, H, Dh = r.shape

    def step(state, inp):
        r_t, w_t, k_t, v_t, kk_t, a_t = inp
        sa = jnp.einsum('bhvk,bhk->bhv', state, -kk_t)
        state = (state * w_t[:, :, None, :] + sa[..., None] * (kk_t * a_t)[:, :, None, :]
                 + v_t[..., None] * k_t[:, :, None, :])
        return state, jnp.einsum('bhvk,bhk->bhv', state, r_t)

    xs = tuple(jnp.moveaxis(t, 1, 0) for t in (r, w, k, v, kk, a))
    s0 = jnp.zeros((B, H, Dh, Dh), F32)
    _, ys = lax.scan(step, s0, xs)
    return jnp.moveaxis(ys, 0, 1)

def rwkv7_mixer(z, mu, w0, w2, a0, a2, g2, k_k, k_a, r_k, ln_w, ln_b, v_first, v0, v1, v2):
    B, S, _ = z.shape
    z_prev = jnp.pad(z, ((0, 0), (1, 0), (0, 0)))[:, :-1]
    zs = z + mu * (z_prev - z)
    r, wl, k, v, al, gl = _split(zs, (MIX_WIDTH, RW_DECAY_LORA, MIX_WIDTH, MIX_WIDTH, RW_AAA_LORA, RW_GATE_LORA))
    w = -jax.nn.softplus(-(w0 + jnp.tanh(wl) @ w2)) - 0.5
    decay = jnp.exp(-jnp.exp(w.astype(F32)))
    a = jax.nn.sigmoid(a0 + al @ a2)
    g = jax.nn.sigmoid(gl) @ g2
    if v_first is not None:
        v = v + (v_first - v) * jax.nn.sigmoid(v0 + (v @ v1) @ v2)

    def hs(t):
        return t.astype(F32).reshape(B, S, RW_HEADS, HEAD_DIM)

    kk = hs(k * k_k)
    kk = kk / jnp.maximum(jnp.sqrt(jnp.sum(kk * kk, axis=-1, keepdims=True)), 1e-12)
    k_mod = hs(k * (1.0 + (a - 1.0) * k_a))
    rh, vh = hs(r), hs(v)
    y = rwkv7_scan(rh, hs(decay), k_mod, vh, kk, hs(a))
    mean = jnp.mean(y, axis=-1, keepdims=True)
    var = jnp.mean(jnp.square(y - mean), axis=-1, keepdims=True)
    yn = ((y - mean) * lax.rsqrt(var + RW_GN_EPS)).reshape(B, S, MIX_WIDTH) * ln_w + ln_b
    bonus = (jnp.sum(rh * k_mod * r_k.reshape(RW_HEADS, HEAD_DIM), axis=-1, keepdims=True) * vh).reshape(B, S, MIX_WIDTH)
    return ((yn + bonus) * g).astype(z.dtype), v

def rope(x, pos):
    half = HEAD_DIM // 2
    inv = ROPE_THETA ** (-jnp.arange(half, dtype=F32) / half)
    ang = pos.astype(F32)[:, None] * inv[None, :]
    cos, sin = jnp.cos(ang), jnp.sin(ang)
    xf = x.astype(F32)
    x1, x2 = xf[..., :half], xf[..., half:]
    return jnp.concatenate([x1 * cos - x2 * sin, x1 * sin + x2 * cos], axis=-1).astype(x.dtype)

def dilated_window_attention(q, k, v):
    B, G, H, S, Dh = q.shape
    nb = S // Q_BLOCK
    scale = Dh ** -0.5

    def block(start):
        t = start + jnp.arange(Q_BLOCK)
        outs, lses = [], []
        for g, (window, dil) in enumerate(DIL_PAIRS):
            n_keys = window // dil + 1
            idx = t[:, None] - dil * jnp.arange(n_keys)[None, :]
            valid = idx >= 0
            idx = jnp.maximum(idx, 0)
            qb = lax.dynamic_slice_in_dim(q[:, g], start, Q_BLOCK, axis=2)
            kg = jnp.take(k[:, g], idx, axis=2)
            vg = jnp.take(v[:, g], idx, axis=2)
            s = jnp.einsum('bhqd,bhqnd->bhqn', qb, kg).astype(F32) * scale
            s = jnp.where(valid, s, MASK_VALUE)
            lse = jax.nn.logsumexp(s, axis=-1)
            p = jnp.exp(s - lse[..., None])
            outs.append(jnp.einsum('bhqn,bhqnd->bhqd', p, vg.astype(F32)))
            lses.append(lse)
        wts = jax.nn.softmax(jnp.stack(lses, axis=0), axis=0)
        return jnp.sum(wts[..., None] * jnp.stack(outs, axis=0), axis=0)

    ob = lax.map(block, jnp.arange(nb) * Q_BLOCK)
    return jnp.moveaxis(ob, 0, 2).reshape(B, H, S, Dh).astype(q.dtype)

def dilated_mixer(z, pos):
    B, S, _ = z.shape
    q, k, v = _split(z, (AT_WIDTH,) * 3)

    def gh(t):
        return t.reshape(B, S, N_DIL, AT_HEADS, HEAD_DIM).transpose(0, 2, 3, 1, 4)

    o = dilated_window_attention(rope(gh(q), pos), rope(gh(k), pos), gh(v))
    return from_heads(o)

def causal_dwconv(a, w, b):
    S = a.shape[1]
    ap = jnp.pad(a, ((0, 0), (CONV_W - 1, 0), (0, 0)))
    out = b + w[0] * a
    for j in range(1, CONV_W):
        out = out + w[j] * ap[:, CONV_W - 1 - j:CONV_W - 1 - j + S]
    return out

def setup_inputs(seed: int = 0) -> dict:
    key = jax.random.key(seed)
    ks = jax.random.split(key, 32)
    n = lambda i, shape, s: jax.random.normal(ks[i], shape, F32) * s
    one = lambda i, shape: 1.0 + 0.02 * jax.random.normal(ks[i], shape, F32)
    L, W = DEPTH, MIX_WIDTH
    return {
        "x": n(0, (BATCH, SEQ, D_MODEL), 1.0),
        "norm_mix_w": one(1, (L, D_MODEL)),
        "norm_ffn_w": one(2, (L, D_MODEL)),
        "norm_final_w": one(3, (D_MODEL,)),
        "w_in": n(4, (L, D_MODEL, N_IN), D_MODEL ** -0.5),
        "hg_lb_table": n(5, (L, W), 0.5),
        "hg_norm_w": one(6, (L, W)),
        "gla_a_w2": n(7, (L, GLA_RANK, GLA_HEADS * GLA_DK), GLA_RANK ** -0.5),
        "gla_a_b": n(8, (L, GLA_HEADS * GLA_DK), 0.1),
        "gla_norm_w": one(9, (L, W)),
        "rw_mu": jax.random.uniform(ks[10], (L, RW_WIDTH), F32),
        "rw_w0": jax.random.uniform(ks[11], (L, W), F32, minval=-5.0, maxval=0.0),
        "rw_w2": n(12, (L, RW_DECAY_LORA, W), 0.5 * RW_DECAY_LORA ** -0.5),
        "rw_a0": n(13, (L, W), 0.1),
        "rw_a2": n(14, (L, RW_AAA_LORA, W), RW_AAA_LORA ** -0.5),
        "rw_g2": n(15, (L, RW_GATE_LORA, W), RW_GATE_LORA ** -0.5),
        "rw_k_k": 0.85 + n(16, (L, W), 0.1),
        "rw_k_a": 1.0 + n(17, (L, W), 0.1),
        "rw_r_k": n(18, (L, W), 0.1),
        "rw_ln_w": one(19, (L, W)),
        "rw_ln_b": n(20, (L, W), 0.02),
        "rw_v0": n(21, (L - 1, W), 0.1),
        "rw_v1": n(22, (L - 1, W, RW_MV_LORA), W ** -0.5),
        "rw_v2": n(23, (L - 1, RW_MV_LORA, W), RW_MV_LORA ** -0.5),
        "w_branch": n(24, (L, N_BRANCH, W, D_MODEL), W ** -0.5),
        "w_out": n(25, (L, D_MODEL, D_MODEL), D_MODEL ** -0.5),
        "ffn_w_up": n(26, (L, D_MODEL, 2 * D_FF), D_MODEL ** -0.5),
        "ffn_conv_w": n(27, (L, CONV_W, D_FF), CONV_W ** -0.5),
        "ffn_conv_b": n(28, (L, D_FF), 0.02),
        "ffn_w_down": n(29, (L, D_FF, D_MODEL), D_FF ** -0.5),
    }

def reference(x, norm_mix_w, norm_ffn_w, norm_final_w, w_in, hg_lb_table, hg_norm_w, gla_a_w2, gla_a_b,
              gla_norm_w, rw_mu, rw_w0, rw_w2, rw_a0, rw_a2, rw_g2, rw_k_k, rw_k_a, rw_r_k, rw_ln_w, rw_ln_b,
              rw_v0, rw_v1, rw_v2, w_branch, w_out, ffn_w_up, ffn_conv_w, ffn_conv_b, ffn_w_down):
    B, S, _ = x.shape
    pos = jnp.arange(S, dtype=jnp.int32)
    p_lb = jax.nn.softmax(hg_lb_table.astype(F32), axis=0)
    lower_bounds = jnp.cumsum(p_lb, axis=0) - p_lb[0:1]
    v_first = None
    for layer in range(DEPTH):
        h = rmsnorm(x, norm_mix_w[layer])
        z = h @ w_in[layer]
        z_hg, z_gla, z_rw, z_at, z_gate = _split(z, (HG_WIDTH, GLA_WIDTH, RW_WIDTH, 3 * AT_WIDTH, GATE_WIDTH))
        o_a = hgrn2_mixer(z_hg, lower_bounds[layer], hg_norm_w[layer])
        o_b = gla_mixer(z_gla, gla_a_w2[layer], gla_a_b[layer], gla_norm_w[layer])
        if layer == 0:
            o_c, v_first = rwkv7_mixer(z_rw, rw_mu[layer], rw_w0[layer], rw_w2[layer], rw_a0[layer], rw_a2[layer],
                                       rw_g2[layer], rw_k_k[layer], rw_k_a[layer], rw_r_k[layer], rw_ln_w[layer],
                                       rw_ln_b[layer], None, None, None, None)
        else:
            o_c, _ = rwkv7_mixer(z_rw, rw_mu[layer], rw_w0[layer], rw_w2[layer], rw_a0[layer], rw_a2[layer],
                                 rw_g2[layer], rw_k_k[layer], rw_k_a[layer], rw_r_k[layer], rw_ln_w[layer],
                                 rw_ln_b[layer], v_first, rw_v0[layer - 1], rw_v1[layer - 1], rw_v2[layer - 1])
        o_d = dilated_mixer(z_at, pos)
        branches = jnp.stack([o_a, o_b, o_c, o_d], axis=2)
        proj = jnp.einsum('bsnw,nwd->bsnd', branches, w_branch[layer])
        gates = jax.nn.sigmoid(z_gate.reshape(B, S, N_BRANCH, D_MODEL))
        x = x + jnp.sum(gates * proj, axis=2) @ w_out[layer]
        h2 = rmsnorm(x, norm_ffn_w[layer])
        up, gate_ff = _split(h2 @ ffn_w_up[layer], (D_FF, D_FF))
        up = causal_dwconv(up, ffn_conv_w[layer], ffn_conv_b[layer])
        x = x + (jax.nn.silu(up) * gate_ff) @ ffn_w_down[layer]
    return rmsnorm(x, norm_final_w)


_drawn_inputs = setup_inputs


def setup_inputs(seed=0):
    import zlib

    import numpy as np

    out = dict(_drawn_inputs(seed))
    spreads = {}
    factors = {'norm_ffn_w': 2.69,
     'norm_final_w': 9.017,
     'hg_norm_w': 6.287,
     'gla_a_b': 2.896,
     'gla_norm_w': 6.076,
     'rw_w2': 4.181,
     'rw_a0': 3.33,
     'rw_ln_w': 6.955,
     'rw_ln_b': 18.71,
     'rw_v0': 6.453,
     'ffn_conv_b': 4.058}
    for name, (base, spread) in spreads.items():
        noise = np.random.default_rng([zlib.crc32(name.encode()), seed]).standard_normal(out[name].shape)
        drawn = base * np.exp(spread * noise) if base else spread * noise
        out[name] = jnp.asarray(drawn.astype(out[name].dtype))
    for name, factor in factors.items():
        out[name] = (out[name] * factor).astype(out[name].dtype)
    return out
```

```python
import numpy as np

import concourse.bass as bass
from concourse import mybir

F32 = mybir.dt.float32
U32 = mybir.dt.uint32
ALU = mybir.AluOpType
ACT = mybir.ActivationFunctionType
AX = mybir.AxisListType

P = 128
D = 1024
S = 512
L = 2
KT = D // P
W = D // 4
HD = 64
NH = W // HD
NBR = 4
DFF = 11 * D // 4
FT = DFF // P
GDK = 32
GRANK = 16
TAU = 16.0
N_DIL = 3
DILS = (1, 4, 16)
ORDER = (1, 4, 4)
TB = S // P
RC = 64
NRC = S // RC

HG0 = 0
GL0 = 4 * W
GLW = 2 * NH * GDK + 2 * W + GRANK
RW0 = GL0 + GLW
RWW = 3 * W + 32 + 32 + 64
AT0 = RW0 + RWW
GT0 = AT0 + 9 * W
N_IN = GT0 + NBR * D

LEVELS = (64, 32, 16, 8, 4, 2, 1)
RING = 4
NPJ = 2
NMX = 6
BIG = 8.0e9

C_ONE, C_EPS, C_GN, C_LOG, C_SM = range(5)
LOG_SHIFT = 20


def _rows(*items):
    at, n = {}, 0
    for name, rows in items:
        at[name] = n
        n += rows
    return at, n


PA, NPA = _rows(("norm_mix", 8), ("norm_ffn", 8), ("hg_norm", 2), ("gla_norm", 2), ("gla_b", 1), ("w0", 2), ("a0", 2),
                ("k_k", 2), ("k_a", 2), ("r_k", 2), ("ln_w", 2), ("ln_b", 2), ("v0", 2), ("mu_r", 2), ("mu_k", 2),
                ("mu_v", 2), ("mu_sm", 1), ("lb", 4), ("final", 8))
PB, NPB = _rows(("conv_w", 3 * FT), ("conv_b", FT))


def strips():
    out, at = [], {}

    def add(name, *pieces):
        at[name] = len(out)
        out.append(pieces)

    def win(name, col, width=2 * P):
        add(name, (0, "w_in", col, width, 0, KT))

    win("rw_r", RW0)
    win("rw_k", RW0 + W + 32)
    win("rw_v", RW0 + 2 * W + 32)
    add("rw_sm", (0, "w_in", RW0 + W, 32, 0, KT), (32, "w_in", RW0 + 3 * W + 32, 32, 0, KT),
        (64, "w_in", RW0 + 3 * W + 64, 64, 0, KT))
    for n, nm in enumerate(("hg_q", "hg_f", "hg_i", "hg_g")):
        win(nm, HG0 + n * W)
    win("gl_qk", GL0)
    win("gl_v", GL0 + W)
    win("gl_g", GL0 + 2 * W)
    win("gl_a", GL0 + 3 * W, GRANK)
    for g in range(N_DIL):
        win(("at_q", g), AT0 + g * W)
        win(("at_k", g), AT0 + (N_DIL + g) * W)
        win(("at_v", g), AT0 + (2 * N_DIL + g) * W)
    for d in range(D // (2 * P)):
        for n in range(NBR):
            win(("gate", d, n), GT0 + n * D + d * 2 * P)
    for d in range(D // (2 * P)):
        add(("out", d), (0, "w_out", d * 2 * P, 2 * P, 0, KT))
    for c in range(FT // 2):
        add(("up", c), (0, "ffn_up", c * 2 * P, 2 * P, 0, KT))
        add(("gf", c), (0, "ffn_up", DFF + c * 2 * P, 2 * P, 0, KT))
    for d in range(D // (2 * P)):
        for j, k0 in enumerate(range(0, FT, KT)):
            add(("down", d, j), (0, "ffn_down", d * 2 * P, 2 * P, k0, min(KT, FT - k0)))
    return out, at


STRIPS, STRIP_AT = strips()


def tiles():
    t = []
    for nm in ("rw_r", "rw_k", "rw_v"):
        t += [((nm, m), "a") for m in range(2)]
    t.append((("rw_sm", 0), "a"))
    for nm in ("hg_q", "hg_f", "hg_i", "hg_g", "gl_qk", "gl_v", "gl_g"):
        t += [((nm, m), "a") for m in range(2)]
    t.append((("gl_a", 0), "a"))
    for g in range(N_DIL):
        for nm in ("at_q", "at_k", "at_v"):
            t += [((nm, g, m), "a") for m in range(2)]
    for d in range(D // (2 * P)):
        for n in range(NBR):
            for m in range(2):
                t += [(("gate", d, n, m), "a"), (("br", d, n, m), "d")]
    for d in range(D // P):
        t.append((("out", d), "d"))
    for c in range(FT):
        t += [(("up", c), "a"), (("gf", c), "d")]
    for d in range(D // P):
        t.append((("down", d), "d"))
    return t


TILES = tiles()
TILE_AT = {n: i for i, (n, _) in enumerate(TILES)}


def taken(i):
    return sum(1 for _, e in TILES[:i + 1] if e == TILES[i][1])


def last_tile(name):
    if isinstance(name, str):
        return TILE_AT[(name, 0 if name in ("rw_sm", "gl_a") else 1)]
    if name[0] in ("out", "up", "gf", "down"):
        return TILE_AT[(name[0], 2 * name[1] + 1)]
    return TILE_AT[(*name, 1)]


class Sems:

    def __init__(self, nc, n):
        self.pool, self.made = [nc.alloc_semaphore(f"sem{i}") for i in range(n)], {}
        nums = [s.num for s in self.pool]
        assert nums == list(range(nums[0], nums[0] + n)), nums
        self.range = range(nums[0], nums[-1] + 1)

    def __getitem__(self, name):
        if name not in self.made:
            self.made[name] = self.pool[len(self.made)]
        return self.made[name]


class Chain:

    def __init__(self, eng, sems, own):
        self.eng, self.sems, self.own, self.n = eng, sems, own, {}

    def __call__(self, ins, name=None):
        name = name or self.own
        self.n[name] = self.n.get(name, 0) + 1
        ins.then_inc(self.sems[name], 1)
        self.eng.wait_ge(self.sems[name], self.n[name])


def build(nc, t, out):
    sems = Sems(nc, 145)

    def sb(name, *shape):
        return nc.alloc_sbuf_tensor(name, [P, *shape], F32)

    X = sb("x_fm", KT, S)
    H = sb("h_fm", KT, S)
    RG = [sb(f"ring{i}", KT, 2 * P) for i in range(RING)]
    BRG = [sb(f"brring{i}", 2, 2 * P) for i in range(2)]
    OB = sb("branch_out", KT, S)
    VF = sb("v_first", 2, S)
    CC = sb("consts", t["consts"].shape[1])
    CST = sb("const_cols", 8)
    ROW = sb("param_rows", 2, P)
    PC_ = sb("param_cols", NPA + NPB)
    LORA = sb("lora", 2 * P)
    V1 = sb("v1", 2, 32)
    V2 = sb("v2", 2 * P)
    AW2 = sb("gla_w2", P)
    FLAG = sb("layer_flag", 2)
    LB = sb("lower_bound", 2)
    OMLB = sb("one_minus_lb", 2)
    LBT = sb("lb_tmp", 16)
    arena = sb("arena", 24900)
    PS = [nc.alloc_psum_tensor(f"ps{i}", [P, 512], F32) for i in range(8)]
    pj, mx = PS[:NPJ], PS[NPJ:]

    ccat = {}
    at = 0
    for nm, n in CONSTS:
        ccat[nm] = at
        at += n
    cc = lambda nm: CC[:, ccat[nm]:ccat[nm] + dict(CONSTS)[nm]]
    ident, ones, oblk, rot = cc("ident"), cc("ones"), cc("oblk"), cc("rot")
    lmask = cc("lmask").rearrange("p (l t) -> p l t", l=8)
    amask, rmask = cc("amask"), cc("rmask")
    cosT, sinT, rst64, rst128 = cc("cos"), cc("sin"), cc("rst64"), cc("rst128")

    def pa(name, i=0):
        return PC_[:, PA[name] + i:PA[name] + i + 1]

    def pb_(name, i=0):
        return PC_[:, NPA + PB[name] + i:NPA + PB[name] + i + 1]

    def cst(i):
        return CST[:, i:i + 1]

    class Arena:
        def __init__(self):
            self.at = 0

        def __call__(self, *shape):
            n = int(np.prod(shape))
            v = arena[:, self.at:self.at + n]
            self.at += n
            assert self.at <= 24900, self.at
            if len(shape) == 2:
                v = v.rearrange("p (a b) -> p a b", a=shape[0])
            elif len(shape) == 3:
                v = v.rearrange("p (a b c) -> p a b c", a=shape[0], b=shape[1])
            return v

    a = Arena()
    ZT, RS = a(2, S + 1), a(7, S)
    RA, RLW, RB, RG_, RBN, RKT = (a(2, S) for _ in range(6))
    AR = a(2, 2, S)
    RT1, RT2 = a(2, S), a(2, S)
    PCH = a(2, NRC)
    mark = a.at
    TOK = a(4, TB, P)
    G = a(8, 4 * P)
    TM, TTM = a(8, P), a(8, P)
    SH = a(NRC + 1, HD)
    SPR = a(HD)
    as_tiles = lambda v, n: v.rearrange("p (a b) -> p a b", a=n)
    CM = as_tiles(RB.rearrange("p a b -> p (a b)"), 8)
    YM = as_tiles(RS[:, 2:4, :].rearrange("p a b -> p (a b)"), 8)
    W1, TV, U = (as_tiles(RS[:, i, :], 8) for i in (0, 1, 6))
    TAT = RT1[:, 0, :]
    VT = G[:, 0, :]
    YF = RLW

    def lin_buffers(nt):
        a = Arena()
        b = {}
        for nm in ("q", "k", "b", "t1", "t2", "t3"):
            b[nm] = a(nt, S)
        for nm in ("g", "o", "u1", "u2"):
            b[nm] = a(2, S)
        b["v"] = a(TB, 2 * P)
        b["x"] = [a(nt, S) for _ in range(2)]
        b["d"] = [a(nt, S) for _ in range(2)]
        b["a"] = a(NH, TB, P)
        b["kdt"] = a(nt, TB, P)
        b["sh"] = a(TB, nt, HD)
        b["ebl"] = a(nt, TB)
        b["al"] = a(S)
        b["f"] = a(nt, S)
        return b

    HB, GB = lin_buffers(2), lin_buffers(1)

    a = Arena()
    QR, KR = a(6, S), a(6, S)
    VA = a(N_DIL * TB, 2 * P)
    TZ, TC, TR = a(2, S), a(S), a(S)
    SMX = a(2, 4 * P)
    PT = a(2, 4 * P)
    PE_ = a(2, 4 * P)
    ST = a(3 * 2 * 2 * TB)
    STR = a(P)
    NM = a(4)
    MN = a(3, S)
    CN = a(3, S)
    MG, DN, NU, TP = a(S), a(S), a(S), a(S)

    a = Arena()
    MT = a(KT, S)
    SG = [a(S) for _ in range(4)]
    MTMP = [a(S) for _ in range(2)]
    a = Arena()
    HFF = a(FT, S)
    UP = [a(S + 2) for _ in range(2)]
    FC = [a(S) for _ in range(3)]
    FS = [a(S) for _ in range(2)]
    SQN = a(2, S)
    RSTD = a(S)
    NTMP = a(S)

    with nc.Block() as block:
        @block.sync
        def _(sp):
            sp.dma_start(CC[:, :], t["consts"]).then_inc(sems["c_in"], 16)
            sp.dma_start(CST[:, :], t["const_cols"]).then_inc(sems["c_in"], 16)
            for tb in range(TB):
                sp.dma_start(arena[:, tb * D:(tb + 1) * D], t["x"][0, tb * P:(tb + 1) * P, :]).then_inc(sems["x_in"], 16)

        @block.tensor
        def _(pe):
            pe.wait_ge(sems["c_in"], 32)
            pe.wait_ge(sems["x_in"], 16 * TB)
            for k in range(KT):
                if k >= 2:
                    pe.wait_ge(sems["x_out"], k - 1)
                for tb in range(TB):
                    ins = nc.tensor.transpose(pj[k % 2][:, tb * P:(tb + 1) * P],
                                              arena[:, tb * D + k * P:tb * D + (k + 1) * P], ident)
                ins.then_inc(sems["x_t"], 1)

        @block.vector
        def _(dve):
            nc.vector.memset(VF[:, :, :], 0.0)
            nc.vector.memset(ROW[:, :, :], 0.0).then_inc(sems["row0"], 1)
            for k in range(KT):
                dve.wait_ge(sems["x_t"], k + 1)
                nc.vector.tensor_copy(X[:, k, :], pj[k % 2][:, :]).then_inc(sems["x_out"], 1)

    def clear():
        nc.sync.sem_clear(sems.range)
        nc.all_engine_barrier()

    clear()

    def norm_pe(pe, tag):
        for k in range(KT):
            pe.wait_ge(sems[tag + "_sq"], k + 1)
            ins = nc.tensor.matmul(mx[0][:, :], ones, SQN[:, k % 2, :], start=k == 0, stop=k == KT - 1)
            ins.then_inc(sems[tag + "_ss"], 1)

    def norm_act(act, ch, tag):
        for k in range(KT):
            if k >= 2:
                act.wait_ge(sems[tag + "_ss"], k - 1)
            nc.scalar.activation(SQN[:, k % 2, :], X[:, k, :], ACT.Square).then_inc(sems[tag + "_sq"], 1)
        act.wait_ge(sems[tag + "_ss"], KT)
        ch(nc.scalar.activation(NTMP[:, :], mx[0][:, :], ACT.Ln, bias=cst(C_EPS), scale=1.0 / D))
        ch(nc.scalar.activation(RSTD[:, :], NTMP[:, :], ACT.Exp, scale=-0.5), tag + "_rstd")

    def norm_dve(dve, tag, wname):
        dve.wait_ge(sems[tag + "_rstd"], 1)
        for k in range(KT):
            ins = nc.vector.scalar_tensor_tensor(H[:, k, :], X[:, k, :], pa(wname, k), RSTD[:, :], ALU.mult, ALU.mult)
        ins.then_inc(sems[tag + "_h"], 1)

    def sig_act(ch, xs, tmp, src, bias=0.0, scale=1.0, name=None):
        nc.scalar.activation(xs, src, ACT.Identity, bias=bias, scale=scale)
        ch(nc.scalar.activation(tmp, src, ACT.Abs, bias=bias, scale=scale))
        ch(nc.scalar.activation(tmp, tmp, ACT.Exp, scale=-1.0))
        ch(nc.scalar.activation(tmp, tmp, ACT.Ln, bias=cst(C_ONE), scale=1.0), name)

    def sig_dve(ch, dst, xs, tmp, name=None):
        ch(nc.vector.scalar_tensor_tensor(dst, xs, 0.0, tmp, ALU.min, ALU.subtract), name)

    flat = lambda v: v.rearrange("p a b -> p (a b)")

    mm = nc.tensor.matmul
    tr = nc.tensor.transpose
    V, A = nc.vector, nc.scalar
    TOKN = ("a", "b", "k", "v")
    half = lambda hh: slice(HD * hh, HD * hh + HD)

    def rwkv_pe(pe):
        w = lambda nm, v: pe.wait_ge(sems[nm], v)
        w("rw_smx", 1)
        w("rw_shift", 7)
        for m in range(2):
            mm(mx[m][:, :], LORA[0:32, m * P:(m + 1) * P], RA[0:32, 0, :], start=True, stop=True)
        for m in range(2):
            mm(mx[2 + m][:, :], LORA[32:64, m * P:(m + 1) * P], RA[32:64, 0, :], start=True, stop=True)
        for m in range(2):
            ins = mm(mx[4][0:32, :], V1[:, m, :], RS[:, 4 + m, :], start=m == 0, stop=m == 1)
        ins.then_inc(sems["rw_lora"], 1)
        w("rw_sig1", 1)
        for m in range(2):
            mm(mx[m][:, :], V2[0:32, m * P:(m + 1) * P], VT[0:32, :], start=True, stop=True)
        for m in range(2):
            ins = mm(mx[2 + m][:, :], LORA[64:128, m * P:(m + 1) * P], RBN[64:128, 0, :], start=True, stop=True)
        ins.then_inc(sems["rw_lora2"], 1)
        w("rw_sq", 1)
        for m in range(2):
            ins = mm(mx[4 + m][:, :], oblk, RT1[:, m, :], start=True, stop=True)
        ins.then_inc(sems["rw_ss"], 1)
        w("rw_bp", 1)
        for m in range(2):
            ins = mm(mx[m][:, :], oblk, RT1[:, m, :], start=True, stop=True)
        ins.then_inc(sems["rw_bs"], 1)
        w("rw_ready", 1)
        for p in range(2):
            src = (AR[:, p, 0, :], RA[:, p, :], RKT[:, p, :], RS[:, 4 + p, :])
            for q in range(4):
                for tb in range(TB):
                    ins = tr(mx[q][:, tb * P:(tb + 1) * P], src[q][:, tb * P:(tb + 1) * P], ident)
                ins.then_inc(sems["rw_tr"], 1)
            w("rw_tok", 4 * (p + 1))
            for hh in range(2):
                for tb in range(TB):
                    i = hh * TB + tb
                    if i >= 2:
                        w("rw_g", 8 * p + i - 1)
                    ts = slice(tb * P, (tb + 1) * P)
                    mm(mx[i % 2][:, 0:256], RA[half(hh), p, ts], AR[half(hh), p, :, ts], start=True, stop=True)
                    mm(mx[i % 2][:, 256:512], RKT[half(hh), p, ts], AR[half(hh), p, :, ts], start=True, stop=True)\
                        .then_inc(sems["rw_gp"], 1)
            w("rw_g", 8 * p + 8)
            for l in range(6):
                for g in range(2):
                    n = (p * 6 + l) * 2 + g
                    y, z, zt = mx[3 * g:3 * g + 3]
                    w("rw_cm", n + 1)
                    for j in range(4):
                        ins = mm(y[:, j * P:(j + 1) * P], CM[:, 4 * g + j, :], TM[:, 4 * g + j, :], start=True, stop=True)
                    ins.then_inc(sems["rw_y1"], 1)
                for g in range(2):
                    n = (p * 6 + l) * 2 + g
                    y, z, zt = mx[3 * g:3 * g + 3]
                    w("rw_ym", n + 1)
                    for j in range(4):
                        mm(z[:, j * P:(j + 1) * P], TTM[:, 4 * g + j, :], YM[:, 4 * g + j, :], start=True, stop=True)
                    for j in range(4):
                        ins = mm(zt[:, j * P:(j + 1) * P], YM[:, 4 * g + j, :], TTM[:, 4 * g + j, :], start=True, stop=True)
                    ins.then_inc(sems["rw_z"], 1)
            w("rw_t", (p + 1) * 12)
            for hh in range(2):
                for tb in range(TB):
                    i = hh * TB + tb
                    ins = mm(mx[0][:, i * HD:(i + 1) * HD], G[:, i, 256:384], TOK[:, 3, tb, half(hh)], start=True, stop=True)
            ins.then_inc(sems["rw_w1p"], 1)
            w("rw_w1", p + 1)
            for hh in range(2):
                for tb in range(TB):
                    i = hh * TB + tb
                    mm(mx[1][:, i * HD:(i + 1) * HD], TTM[:, i, :], W1[:, i, :], start=True, stop=True)
            for hh in range(2):
                for tb in range(TB):
                    i = hh * TB + tb
                    ins = mm(mx[2][half(hh), tb * P:(tb + 1) * P], TOK[:, 0, tb, half(hh)], TTM[:, i, :], start=True, stop=True)
            ins.then_inc(sems["rw_tvp"], 1)
            w("rw_tv", 2 * (p + 1))
            for c in range(NRC):
                tb, par = divmod(c, 2)
                rows = slice(RC * par, RC * par + RC)
                w("rw_s", p * NRC + c + 1)
                for hh in range(2):
                    ins = mm(mx[3 + hh][rows, 0:HD], TAT[half(hh), c * RC:(c + 1) * RC], SH[half(hh), c, :],
                             start=True, stop=True)
                ins.then_inc(sems["rw_up"], 1)
                w("rw_u", p * NRC + c + 1)
                if c < NRC - 1:
                    for hh in range(2):
                        mm(mx[5][half(hh), 0:HD], TOK[rows, 1, tb, half(hh)], U[rows, hh * TB + tb, :],
                           start=True, stop=False)
                        ins = mm(mx[5][half(hh), 0:HD], TOK[rows, 2, tb, half(hh)], TOK[rows, 3, tb, half(hh)],
                                 start=False, stop=True)
                    ins.then_inc(sems["rw_sp"], 1)
            for hh in range(2):
                for tb in range(TB):
                    i = hh * TB + tb
                    o = mx[0][half(hh), tb * P:(tb + 1) * P]
                    mm(o, U[:, i, :], G[:, i, 128:256], start=True, stop=False)
                    mm(o, TOK[:, 3, tb, half(hh)], G[:, i, 384:512], start=False, stop=False)
                    for par in range(2):
                        c = 2 * tb + par
                        ins = mm(mx[0][half(hh), c * RC:(c + 1) * RC], SH[half(hh), c, :],
                                 AR[half(hh), p, 1, c * RC:(c + 1) * RC], start=False, stop=par == 1)
            ins.then_inc(sems["rw_yp"], 1)
            w("rw_yf", p + 1)
        for m in range(2):
            ins = mm(mx[m][:, :], oblk, YF[:, m, :], start=True, stop=True)
        ins.then_inc(sems["rw_mean"], 1)
        w("rw_yc", 1)
        for m in range(2):
            ins = mm(mx[2 + m][:, :], oblk, RT1[:, m, :], start=True, stop=True)
        ins.then_inc(sems["rw_var"], 1)
        w("rw_done", 1)

    def rwkv_act(act, ch):
        w = lambda nm, v: act.wait_ge(sems[nm], v)
        sm_scale = cst(C_SM)
        i = 0
        for nm, m in [(n, m) for n in ("rw_r", "rw_k", "rw_v") for m in range(2)] + [("rw_sm", 0)]:
            take_act(act, (nm, m))
            w("rw_zpad", 1)
            if i >= 2:
                w("rw_shift", i - 1)
            ch(A.activation(ZT[:, i % 2, 1:S + 1], pj[TILE_AT[(nm, m)] % NPJ][:, :], ACT.Copy), "out_act")
            i += 1
        w("rw_shift", 7)
        sig_act(ch, RBN[:, 0, :], RT1[:, 0, :], RS[:, 6, :], scale=sm_scale, name="rw_sm1")
        w("rw_sm2", 1)
        ch(A.activation(RBN[:, 0, :], RBN[:, 0, :], ACT.Exp), "rw_sg")
        w("rw_lora", 1)
        ch(A.activation(VT[0:32, :], mx[4][0:32, :], ACT.Copy))
        w("rw_smx", 1)
        for m in range(2):
            sig_act(ch, RLW[:, m, :], RT1[:, m, :], mx[m][:, :], bias=pa("w0", m))
        for m in range(2):
            sig_act(ch, RKT[:, m, :], RT2[:, m, :], mx[2 + m][:, :], bias=pa("a0", m), name="rw_sig1" if m else None)
        w("rw_sig2", 1)
        A.activation(flat(RLW), flat(RLW), ACT.Exp)
        ch(A.activation(flat(RA), flat(RKT), ACT.Exp), "rw_sig3")
        w("rw_lora2", 1)
        for m in range(2):
            A.activation(RG_[:, m, :], mx[2 + m][:, :], ACT.Copy)
            sig_act(ch, RT2[:, m, :], RT1[:, m, :], mx[m][:, :], bias=pa("v0", m), name="rw_vm1")
        w("rw_vm2", 1)
        ch(A.activation(flat(RT2), flat(RT2), ACT.Exp), "rw_vm3")
        w("rw_ss2", 1)
        ch(A.activation(flat(RT1), flat(RT1), ACT.Ln, scale=float(2 ** LOG_SHIFT)))
        ch(A.activation(flat(RT1), flat(RT1), ACT.Exp, scale=-0.5, bias=cst(C_LOG)), "rw_kn")
        w("rw_cum", 1)
        ch(A.activation(flat(RT2), flat(RT2), ACT.Exp), "rw_em")
        w("rw_em2", 1)
        ch(A.activation(flat(RT2), flat(RB), ACT.Exp), "rw_eb")
        w("rw_eb2", 1)
        ch(A.activation(flat(RT2), flat(RB), ACT.Exp, scale=-1.0), "rw_en")
        for p in range(2):
            for q in (2, 3):
                w("rw_tr", 4 * p + q + 1)
                ch(A.activation(flat(TOK[:, q]), mx[q][:, :], ACT.Copy), "rw_tokx")
            for n in range(12):
                w("rw_y1", p * 12 + n + 1)
                g = n % 2
                ch(A.activation(flat(YM[:, 4 * g:4 * g + 4]), mx[3 * g][:, :], ACT.Copy), "rw_ym")
            w("rw_w1p", p + 1)
            ch(A.activation(flat(W1), mx[0][:, :], ACT.Copy), "rw_w1")
            w("rw_tvp", p + 1)
            ch(A.activation(flat(TV), mx[1][:, :], ACT.Copy), "rw_tv")
            ch(A.activation(TAT[:, :], mx[2][:, :], ACT.Copy), "rw_tv")
            w("rw_yp", p + 1)
            ch(A.activation(YF[:, p, :], mx[0][:, :], ACT.Copy), "rw_yf")
        w("rw_var", 1)
        for m in range(2):
            ch(A.activation(RT2[:, m, :], mx[2 + m][:, :], ACT.Ln, scale=1.0 / HD, bias=cst(C_GN)))
        ch(A.activation(flat(RT2), flat(RT2), ACT.Exp, scale=-0.5), "rw_rstd")

    def rwkv_dve(dve, ch):
        w = lambda nm, v: dve.wait_ge(sems[nm], v)
        ch(V.memset(ZT[:, :, 0:1], 0.0), "rw_zpad")
        mus = [("mu_r", 0), ("mu_r", 1), ("mu_k", 0), ("mu_k", 1), ("mu_v", 0), ("mu_v", 1), ("mu_sm", 0)]
        for i in range(7):
            w("out_act", i + 1)
            z = ZT[:, i % 2, 1:S + 1]
            ch(V.tensor_tensor(RT1[:, i % 2, :], ZT[:, i % 2, 0:S], z, ALU.subtract))
            ch(V.scalar_tensor_tensor(RS[:, i, :], RT1[:, i % 2, :], pa(*mus[i]), z, ALU.mult, ALU.add), "rw_shift")
        w("rw_sm1", 1)
        sig_dve(ch, RBN[:, 0, :], RBN[:, 0, :], RT1[:, 0, :], "rw_sm2")
        w("rw_sg", 1)
        V.tensor_scalar(RA[0:32, 0, :], RBN[0:32, 0, :], 2.0, -1.0, ALU.mult, ALU.add)
        ch(V.tensor_copy(RA[32:64, 0, :], RS[32:64, 6, :]), "rw_smx")
        w("rw_sig1", 1)
        sig_dve(ch, flat(RLW), flat(RLW), flat(RT1))
        sig_dve(ch, flat(RKT), flat(RKT), flat(RT2), "rw_sig2")
        w("rw_vm1", 2)
        sig_dve(ch, flat(RT2), flat(RT2), flat(RT1), "rw_vm2")
        w("rw_sig3", 1)
        ch(V.tensor_scalar_mul(flat(RLW), flat(RLW), -float(np.exp(np.float64(-0.5)))))
        r, k, v = RS[:, 0:2, :], RS[:, 2:4, :], RS[:, 4:6, :]
        ch(V.tensor_scalar(flat(RT1), flat(v), FLAG[:, 1:2], None, ALU.mult))
        ch(V.scalar_tensor_tensor(flat(VF), flat(VF), FLAG[:, 0:1], flat(RT1), ALU.mult, ALU.add))
        ch(V.tensor_tensor(flat(RT1), flat(VF), flat(v), ALU.subtract))
        w("rw_vm3", 1)
        ch(V.tensor_tensor(flat(RT1), flat(RT1), flat(RT2), ALU.mult))
        ch(V.tensor_tensor(flat(v), flat(v), flat(RT1), ALU.add))
        w("rw_lora2", 1)
        kk = AR[:, :, 0, :]
        for m in range(2):
            ch(V.tensor_scalar(AR[:, m, 0, :], k[:, m, :], pa("k_k", m), None, ALU.mult))
        ch(V.tensor_tensor(RT1, kk, kk, ALU.mult), "rw_sq")
        for m in range(2):
            V.tensor_tensor_scan(RB[:, m, :], rst64, RLW[:, m, :], 0.0, ALU.mult, ALU.add)
        for m in range(2):
            ch(V.tensor_scalar(RT2[:, m, :], RA[:, m, :], -1.0, pa("k_a", m), ALU.add, ALU.mult))
        ch(V.scalar_tensor_tensor(flat(RKT), flat(RT2), 1.0, flat(k), ALU.add, ALU.mult))
        w("rw_ss", 1)
        for m in range(2):
            ins = V.tensor_scalar_max(RT1[:, m, :], mx[4 + m][:, :], 1e-24)
        ch(ins, "rw_ss2")
        ch(V.tensor_tensor(flat(RT2), flat(RB), flat(RLW), ALU.subtract), "rw_cum")
        w("rw_kn", 1)
        ch(V.tensor_tensor(kk, kk, RT1, ALU.mult))
        ch(V.tensor_tensor(RA, RA, kk, ALU.mult))
        ch(V.tensor_tensor(RT1, r, RKT, ALU.mult))
        for m in range(2):
            ins = V.tensor_scalar(RT1[:, m, :], RT1[:, m, :], pa("r_k", m), None, ALU.mult)
        ch(ins, "rw_bp")
        w("rw_bs", 1)
        for m in range(2):
            ins = V.tensor_tensor(RBN[:, m, :], mx[m][:, :], v[:, m, :], ALU.mult)
        ch(ins)
        w("rw_em", 1)
        ch(V.tensor_tensor(kk, kk, RT2, ALU.mult), "rw_em2")
        w("rw_eb", 1)
        V.tensor_copy(PCH, RT2.rearrange("p m (c t) -> p m c t", t=RC)[:, :, :, RC - 1])
        ch(V.tensor_tensor(AR[:, :, 1, :], r, RT2, ALU.mult), "rw_eb2")
        w("rw_en", 1)
        V.tensor_tensor(RA, RA, RT2, ALU.mult)
        ch(V.tensor_tensor(RKT, RKT, RT2, ALU.mult), "rw_ready")
        for p in range(2):
            for q in range(2):
                w("rw_tr", 4 * p + q + 1)
                ch(V.tensor_copy(flat(TOK[:, q]), mx[q][:, :]), "rw_tok")
            w("rw_tokx", 2 * p + 2)
            ch(V.memset(SH[:, 0, :], 0.0), "rw_tok")
            for j in range(8):
                ins = V.tensor_copy(TM[:, j, :], ident)
            for j in range(8):
                ins = V.tensor_copy(TTM[:, j, :], ident)
            ch(ins, "rw_tok")
            for i in range(8):
                w("rw_gp", 8 * p + i + 1)
                ch(V.tensor_tensor(G[:, i, :], mx[i % 2][:, :], rmask, ALU.mult), "rw_g")
            for l in range(6):
                mask = lmask[:, 6 - l, :]
                for g in range(2):
                    gs = slice(4 * g, 4 * g + 4)
                    ch(V.tensor_tensor(CM[:, gs, :], G[:, gs, 0:P], bc(mask, 4), ALU.mult), "rw_cm")
                for g in range(2):
                    gs = slice(4 * g, 4 * g + 4)
                    w("rw_z", (p * 6 + l) * 2 + g + 1)
                    V.tensor_tensor(flat(TM[:, gs, :]), flat(TM[:, gs, :]), mx[3 * g + 1][:, :], ALU.subtract)
                    ch(V.tensor_tensor(flat(TTM[:, gs, :]), flat(TTM[:, gs, :]), mx[3 * g + 2][:, :], ALU.subtract), "rw_t")
            w("rw_tv", 2 * (p + 1))
            ch(V.memset(SH[:, 0, :], 0.0), "rw_s")
            for c in range(NRC):
                tb, par = divmod(c, 2)
                rows = slice(RC * par, RC * par + RC)
                pc = PCH[:, p, c:c + 1]
                w("rw_up", p * NRC + c + 1)
                for hh in range(2):
                    i = hh * TB + tb
                    ins = V.scalar_tensor_tensor(U[rows, i, :], mx[3 + hh][rows, 0:HD], -1.0, TV[rows, i, :],
                                                 ALU.mult, ALU.subtract)
                ch(ins, "rw_u")
                if c < NRC - 1:
                    ch(V.tensor_scalar(SPR[:, :], SH[:, c, :], pc, None, ALU.mult))
                    w("rw_sp", p * (NRC - 1) + c + 1)
                    ch(V.scalar_tensor_tensor(SH[:, c + 1, :], mx[5][:, 0:HD], pc, SPR[:, :], ALU.mult, ALU.add), "rw_s")
        w("rw_mean", 1)
        for m in range(2):
            ins = V.scalar_tensor_tensor(YF[:, m, :], mx[m][:, :], -1.0 / HD, YF[:, m, :], ALU.mult, ALU.add)
        ch(ins)
        ch(V.tensor_tensor(RT1, YF, YF, ALU.mult), "rw_yc")
        w("rw_rstd", 1)
        ch(V.tensor_tensor(YF, YF, RT2, ALU.mult))
        for m in range(2):
            ins = V.tensor_scalar(YF[:, m, :], YF[:, m, :], pa("ln_w", m), pa("ln_b", m), ALU.mult, ALU.add)
        ch(ins)
        ch(V.tensor_tensor(YF, YF, RBN, ALU.add))
        ch(V.tensor_tensor(OB[:, 4:6, :], YF, RG_, ALU.mult), "rw_done")

    def bc(v, n):
        return v.unsqueeze(1).to_broadcast([v.shape[0], n, v.shape[1]])

    def take_act(act, name):
        act.wait_ge(sems["tile"], TILE_AT[name] + 1)

    NL = len(LEVELS)
    HG_LEAVES = dict(d=NL, e=NL, x=NL, sc=(NL + 1) * NH, cp=(NL + 1) * NH, kdt=2)

    def lin_wait(eng, pre, nm, v):
        eng.wait_ge(sems["lin_" + nm], v + (HG_LEAVES.get(nm, 1) if pre == "gl" else 0))

    def linear_pe(pe, pre, b, nt, dk):
        w = lambda nm, v: lin_wait(pe, pre, nm, v)
        hpt = P // dk
        for l in range(len(LEVELS) + 1):
            if l < len(LEVELS):
                w("x", l + 1)
                kx = qx = b["x"][l % 2]
            else:
                w("qk", 1)
                kx, qx = b["k"], b["q"]
            for h in range(NH):
                ti, r = divmod(h, hpt)
                rows = slice(dk * r, dk * r + dk)
                if l >= 1:
                    w("cp", (l - 1) * NH + h + 1)
                for c in range(TB):
                    ts = slice(c * P, (c + 1) * P)
                    ins = mm(mx[h][:, ts], kx[rows, ti, ts], qx[rows, ti, ts], start=True, stop=True)
                ins.then_inc(sems["lin_sc"], 1)
        w("kd", 1)
        for ti in range(nt):
            for c in range(TB):
                ins = tr(mx[4 + ti][:, c * P:(c + 1) * P], b["t1"][:, ti, c * P:(c + 1) * P], ident)
        ins.then_inc(sems["lin_kdp"], 1)
        w("kdt", nt)
        for h in range(NH):
            ti, r = divmod(h, hpt)
            rows = slice(dk * r, dk * r + dk)
            for c in range(TB - 1):
                at_ = (ti * (TB - 1) + c) * HD
                ins = mm(mx[4][rows, at_:at_ + HD], b["kdt"][:, ti, c, rows], b["v"][:, c, h * HD:(h + 1) * HD],
                         start=True, stop=True)
        ins.then_inc(sems["lin_kv"], 1)
        w("sh", 1)
        w("qb", 1)
        w("cp", (len(LEVELS) + 1) * NH)
        for h in range(NH):
            ti, r = divmod(h, hpt)
            rows = slice(dk * r, dk * r + dk)
            for c in range(TB):
                o = mx[h // 2][half(h % 2), c * P:(c + 1) * P]
                mm(o, b["v"][:, c, h * HD:(h + 1) * HD], b["a"][:, h, c, :], start=True, stop=False)
                ins = mm(o, b["sh"][rows, c, ti, :], b["t2"][rows, ti, c * P:(c + 1) * P], start=False, stop=True)
        ins.then_inc(sems["lin_op"], 1)
        w("osq", 1)
        for m in range(2):
            ins = mm(mx[2 + m][:, :], oblk, b["u1"][:, m, :], start=True, stop=True)
        ins.then_inc(sems["lin_oss"], 1)
        w("done", 1)

    def blocks(v, n):
        return flat(v).rearrange("p (b h n) -> p b h n", h=2, n=n)

    def linear_act(act, ch, pre, b, nt):
        w = lambda nm, v: lin_wait(act, pre, nm, v)
        for l, n in enumerate(LEVELS):
            w("d", l + 1)
            d = blocks(b["d"][l % 2], n)
            A.activation(d[:, :, 0, :], d[:, :, 0, :], ACT.Exp, scale=-1.0)
            ch(A.activation(d[:, :, 1, :], d[:, :, 1, :], ACT.Exp), "lin_e")
        w("db", 1)
        ch(A.activation(flat(b["t1"]), flat(b["t1"]), ACT.Exp, scale=-1.0), "lin_ed")
        ch(A.activation(flat(b["t2"]), flat(b["b"]), ACT.Exp), "lin_eb")
        w("kdp", 1)
        for ti in range(nt):
            ch(A.activation(flat(b["kdt"][:, ti]), mx[4 + ti][:, :], ACT.Copy), "lin_kdt")
        w("op", 1)
        for m in range(2):
            ins = A.activation(b["o"][:, m, :], mx[m][:, :], ACT.Copy)
        ch(ins)
        ch(A.activation(flat(b["u1"]), flat(b["o"]), ACT.Square), "lin_osq")
        w("oss", 1)
        for m in range(2):
            ins = A.activation(b["u2"][:, m, :], mx[2 + m][:, :], ACT.Ln, scale=1.0 / HD, bias=cst(C_EPS))
        ch(ins)
        ch(A.activation(flat(b["u2"]), flat(b["u2"]), ACT.Exp, scale=-0.5), "lin_rs")

    def linear_dve(dve, ch, pre, b, nt, norm, ob):
        w = lambda nm, v: lin_wait(dve, pre, nm, v)
        ch(V.memset(b["a"].rearrange("p a b c -> p (a b c)"), 0.0))
        V.memset(b["sh"][:, 0, :, :], 0.0)
        for m in range(nt):
            ins = V.tensor_tensor_scan(b["b"][:, m, :], rst128, b["f"][:, m, :], 0.0, ALU.mult, ALU.add)
        ch(ins)
        bb = flat(b["b"])

        def diff(l):
            n = LEVELS[l]
            v = bb.rearrange("p (b m) -> p b m", m=2 * n)
            if l >= 2:
                w("x", l - 1)
            ch(V.tensor_tensor(flat(b["d"][l % 2]).rearrange("p (b m) -> p b m", m=2 * n), v,
                               v[:, :, n - 1:n].to_broadcast([P, v.shape[1], 2 * n]), ALU.subtract), "lin_d")

        diff(0)
        for l, n in enumerate(LEVELS):
            if l + 1 < len(LEVELS):
                diff(l + 1)
            w("e", l + 1)
            if l >= 2:
                w("sc", (l - 1) * NH)
            d, x, k, q = (blocks(v, n) for v in (b["d"][l % 2], b["x"][l % 2], b["k"], b["q"]))
            V.tensor_tensor(x[:, :, 0, :], k[:, :, 0, :], d[:, :, 0, :], ALU.mult)
            ch(V.tensor_tensor(x[:, :, 1, :], q[:, :, 1, :], d[:, :, 1, :], ALU.mult), "lin_x")
            if l == 0:
                continue
            copy_scores(dve, ch, pre, b, l - 1)
        copy_scores(dve, ch, pre, b, len(LEVELS) - 1)
        copy_scores(dve, ch, pre, b, len(LEVELS))
        v = bb.rearrange("p (b m) -> p b m", m=P)
        ch(V.tensor_tensor(flat(b["t1"]).rearrange("p (b m) -> p b m", m=P), v,
                           v[:, :, P - 1:P].to_broadcast([P, v.shape[1], P]), ALU.subtract), "lin_db")
        w("ed", 1)
        ch(V.tensor_tensor(flat(b["t1"]), flat(b["t1"]), flat(b["k"]), ALU.mult), "lin_kd")
        w("eb", 1)
        ch(V.tensor_copy(b["ebl"], b["t2"].rearrange("p m (c t) -> p m c t", t=P)[:, :, :, P - 1]))
        ch(V.tensor_tensor(flat(b["t2"]), flat(b["t2"]), flat(b["q"]), ALU.mult), "lin_qb")
        w("kv", 1)
        for c in range(TB - 1):
            for ti in range(nt):
                at_ = (ti * (TB - 1) + c) * HD
                ins = V.scalar_tensor_tensor(b["sh"][:, c + 1, ti, :], b["sh"][:, c, ti, :], b["ebl"][:, ti, c:c + 1],
                                             mx[4][:, at_:at_ + HD], ALU.mult, ALU.add)
            ch(ins, "lin_sh" if c == TB - 2 else None)
        w("rs", 1)
        ch(V.tensor_tensor(flat(b["o"]), flat(b["o"]), flat(b["u2"]), ALU.mult))
        for m in range(2):
            ins = V.scalar_tensor_tensor(OB[:, ob + m, :], b["o"][:, m, :], pa(norm, m), b["g"][:, m, :], ALU.mult, ALU.mult)
        ch(ins, "lin_done")

    def copy_scores(dve, ch, pre, b, l):
        for h in range(NH):
            lin_wait(dve, pre, "sc", l * NH + h + 1)
            ch(V.copy_predicated(b["a"][:, h, :, :], bc(lmask[:, l, :], TB).bitcast(U32),
                                 mx[h][:, :].rearrange("p (c t) -> p c t", c=TB)), "lin_cp")

    def out_tile(act, ch, name, dst, bank=None, **kw):
        take_act(act, name)
        ch(A.activation(dst, pj[TILE_AT[name] % NPJ][:, :], ACT.Copy, **kw), "out_act")

    def hg_act(act, ch):
        b = HB
        w = lambda nm, v: act.wait_ge(sems["hg_" + nm], v)
        act.wait_ge(sems["rw_done"], 1)
        for m in range(2):
            out_tile(act, ch, ("hg_q", m), b["q"][:, m, :])
        for m in range(2):
            out_tile(act, ch, ("hg_f", m), b["f"][:, m, :])
        for m in range(2):
            out_tile(act, ch, ("hg_i", m), flat(b["v"][:, 2 * m:2 * m + 2, :]))
        for m in range(2):
            out_tile(act, ch, ("hg_g", m), b["g"][:, m, :])
        sig_act(ch, flat(b["t1"]), flat(b["t2"]), flat(b["q"]), name="hg_s1")
        w("s2", 1)
        ch(A.activation(flat(b["t1"]), flat(b["t1"]), ACT.Exp), "hg_s3")
        sig_act(ch, flat(b["u1"]), flat(b["u2"]), flat(b["g"]), name="hg_g1")
        w("g2", 1)
        ch(A.activation(flat(b["g"]), flat(b["u1"]), ACT.Exp), "hg_g3")
        w("s4", 1)
        sig_act(ch, flat(b["t1"]), flat(b["t2"]), flat(b["f"]), name="hg_f1")
        w("f2", 1)
        ch(A.activation(flat(b["t2"]), flat(b["t2"]), ACT.Exp), "hg_f3")
        w("f4", 1)
        A.activation(flat(b["t2"]), flat(b["t2"]), ACT.Ln, bias=cst(C_ONE), scale=1.0)
        ch(A.activation(flat(b["t3"]), flat(b["t3"]), ACT.Ln, scale=1e-9), "hg_f5")
        ch(A.activation(flat(b["k"]), flat(b["k"]), ACT.Exp), "hg_k1")
        linear_act(act, ch, "hg", b, 2)

    def hg_dve(dve, ch):
        b = HB
        w = lambda nm, v: dve.wait_ge(sems["hg_" + nm], v)
        w("s1", 1)
        sig_dve(ch, flat(b["t1"]), flat(b["t1"]), flat(b["t2"]), "hg_s2")
        w("s3", 1)
        ch(V.tensor_tensor(flat(b["q"]), flat(b["q"]), flat(b["t1"]), ALU.mult), "hg_s4")
        w("g1", 1)
        sig_dve(ch, flat(b["u1"]), flat(b["u1"]), flat(b["u2"]), "hg_g2")
        w("f1", 1)
        sig_dve(ch, flat(b["t1"]), flat(b["t1"]), flat(b["t2"]))
        ch(V.tensor_tensor(flat(b["k"]), flat(b["t1"]), flat(b["f"]), ALU.subtract))
        ch(V.tensor_scalar(flat(b["t2"]), flat(b["f"]), -1.0, 60.0, ALU.mult, ALU.min), "hg_f2")
        w("f3", 1)
        for m in range(2):
            ins = V.tensor_scalar(b["t2"][:, m, :], b["t2"][:, m, :], LB[:, m:m + 1], None, ALU.mult)
        ch(ins)
        V.tensor_scalar_max(flat(b["t3"]), flat(b["t2"]), 1e9)
        ch(V.tensor_scalar_min(flat(b["x"][0]), flat(b["t2"]), 1e9))
        ch(V.tensor_copy(flat(b["t2"]), flat(b["x"][0])), "hg_f4")
        w("f5", 1)
        ch(V.tensor_tensor(flat(b["f"]), flat(b["t1"]), flat(b["t2"]), ALU.add))
        ch(V.tensor_tensor(flat(b["f"]), flat(b["f"]), flat(b["t3"]), ALU.add))
        w("k1", 1)
        for m in range(2):
            ins = V.tensor_scalar(b["k"][:, m, :], b["k"][:, m, :], OMLB[:, m:m + 1], None, ALU.mult)
        ch(ins, "lin_qk")
        linear_dve(dve, ch, "hg", b, 2, "hg_norm", 0)

    def gl_act(act, ch):
        b = GB
        w = lambda nm, v: act.wait_ge(sems["gl_" + nm], v)
        act.wait_ge(sems["lin_done"], 1)
        out_tile(act, ch, ("gl_qk", 0), b["q"][:, 0, :], scale=float(GDK) ** -0.5)
        out_tile(act, ch, ("gl_qk", 1), b["k"][:, 0, :])
        for m in range(2):
            out_tile(act, ch, ("gl_v", m), flat(b["v"][:, 2 * m:2 * m + 2, :]))
        for m in range(2):
            out_tile(act, ch, ("gl_g", m), b["g"][:, m, :])
        take_act(act, ("gl_a", 0))
        ch(A.activation(b["al"][0:GRANK, :], pj[TILE_AT[("gl_a", 0)] % NPJ][0:GRANK, :], ACT.Copy), "out_act")
        sig_act(ch, flat(b["u1"]), flat(b["u2"]), flat(b["g"]), name="gl_g1")
        w("g2", 1)
        ch(A.activation(flat(b["u1"]), flat(b["u1"]), ACT.Exp), "gl_g3")
        w("u", 1)
        sig_act(ch, flat(b["t1"]), flat(b["t2"]), mx[5][:, :], bias=pa("gla_b"), name="gl_f1")
        linear_act(act, ch, "gl", b, 1)

    def gl_dve(dve, ch):
        b = GB
        w = lambda nm, v: dve.wait_ge(sems["gl_" + nm], v)
        w("g1", 1)
        sig_dve(ch, flat(b["u1"]), flat(b["u1"]), flat(b["u2"]), "gl_g2")
        w("g3", 1)
        ch(V.tensor_tensor(flat(b["g"]), flat(b["g"]), flat(b["u1"]), ALU.mult))
        w("f1", 1)
        sig_dve(ch, flat(b["f"]), flat(b["t1"]), flat(b["t2"]))
        ch(V.tensor_scalar_mul(flat(b["f"]), flat(b["f"]), 1.0 / TAU), "lin_qk")
        linear_dve(dve, ch, "gl", b, 1, "gla_norm", 2)

    def attention_pe(pe):
        w = lambda nm, v: pe.wait_ge(sems[nm], v)
        w("at_rope", 12)
        n = 0
        for pr in range(2):
            for hh in range(2):
                for blk in range(TB):
                    bs = slice(blk * P, (blk + 1) * P)
                    if n >= 1:
                        w("at_sm", n)
                    s = mx[0]
                    q = lambda g: QR[half(hh), 2 * g + pr, bs]
                    if blk:
                        mm(s[:, 0:256], q(0), KR[half(hh), pr, (blk - 1) * P:(blk + 1) * P], start=True, stop=True)
                    else:
                        mm(s[:, 128:256], q(0), KR[half(hh), pr, bs], start=True, stop=True)
                    mm(s[:, 256:384], q(1), KR[half(hh), 2 + pr, bs], start=True, stop=True)
                    mm(s[:, 384:512], q(2), KR[half(hh), 4 + pr, bs], start=True, stop=True)\
                        .then_inc(sems["at_s"], 1)
                    w("at_p", n + 1)
                    for j in range(0 if blk else 1, 4):
                        ins = tr(mx[1][:, j * P:(j + 1) * P], PE_[:, n % 2, j * P:(j + 1) * P], ident)
                    ins.then_inc(sems["at_pt"], 1)
                    w("at_ptc", n + 1)
                    if n == 8:
                        w("at_num", 1)
                    vs = slice((2 * pr + hh) * HD, (2 * pr + hh + 1) * HD)
                    pt = PT[:, n % 2, :]
                    for g in range(N_DIL):
                        o = mx[2 + g][half(hh), bs]
                        if g == 0 and blk:
                            mm(o, VA[:, blk - 1, vs], pt[:, 0:P], start=True, stop=False)
                        ins = mm(o, VA[:, g * TB + blk, vs], pt[:, (1 + g) * P:(2 + g) * P], start=not (g == 0 and blk),
                                 stop=True)
                    ins.then_inc(sems["at_n"], 1)
                    n += 1
            w("at_st", pr + 1)
            tr(mx[5][0:48, 0:P], ST[:, :], ident).then_inc(sems["at_str"], 1)
            w("at_strc", pr + 1)
            for q in range(2):
                for g in range(N_DIL):
                    k = q * N_DIL + g
                    if k:
                        w("at_bca" if k <= 3 else "at_bcd", pr * 3 + (k if k <= 3 else k - 3))
                    for hh in range(2):
                        for blk in range(TB):
                            row = ((g * 2 + q) * 2 + hh) * TB + blk
                            ins = mm(mx[5][half(hh), blk * P:(blk + 1) * P], ident[0:48, row:row + 1].to_broadcast([48, HD]),
                                     STR[0:48, :], start=True, stop=True)
                    ins.then_inc(sems["at_bcp"], 1)

    def nat(v, g):
        if g == 0:
            return v
        return v.rearrange("p (r j) -> p j r", r=ORDER[g])

    def perm(v, g):
        if g == 0:
            return v
        return v.rearrange("p (j r) -> p j r", r=ORDER[g])

    def at_act(act, ch):
        w = lambda nm, v: act.wait_ge(sems[nm], v)
        w("lin_done", 2)
        n = 0
        for g in range(N_DIL):
            for nm in ("at_q", "at_k"):
                for m in range(2):
                    take_act(act, (nm, g, m))
                    if n >= 2:
                        w("at_rope", n - 1)
                    ch(A.activation(TZ[:, n % 2, :], pj[TILE_AT[(nm, g, m)] % NPJ][:, :], ACT.Copy), "out_act")
                    n += 1
            for m in range(2):
                out_tile(act, ch, ("at_v", g, m), flat(VA[:, g * TB + 2 * m:g * TB + 2 * m + 2, :]))
        n = 0
        scale = float(HD) ** -0.5
        for pr in range(2):
            for hh in range(2):
                for blk in range(TB):
                    w("at_sm", n + 1)
                    if n >= 2:
                        w("at_pt", n - 1)
                    x, e = SMX[:, n % 2, :], PE_[:, n % 2, :]
                    c = hh * TB + blk
                    lo = 0 if blk else P
                    for g, (a0, a1) in enumerate(((lo, 256), (256, 384), (384, 512))):
                        ins = A.activation(e[:, a0:a1], x[:, a0:a1], ACT.Exp, bias=NM[:, g:g + 1], scale=scale,
                                           accum_out=ST[:, ((g * 2 + 1) * 2) * TB + c:((g * 2 + 1) * 2) * TB + c + 1])
                    ch(ins, "at_p")
                    w("at_pt", n + 1)
                    ch(A.activation(PT[:, n % 2, lo:], mx[1][:, lo:], ACT.Copy), "at_ptc")
                    n += 1
            w("at_str", pr + 1)
            ch(A.activation(STR[0:48, :], mx[5][0:48, 0:P], ACT.Copy), "at_strc")
            for g in range(N_DIL):
                w("at_bcp", pr * 6 + g + 1)
                ch(A.activation(perm(MN[:, g, :], g), nat(mx[5][:, :], g), ACT.Copy), "at_bca")
            w("at_c1", pr + 1)
            ch(A.activation(flat(CN), flat(CN), ACT.Exp, scale=scale), "at_c2")
            w("at_den", pr + 1)
            ch(A.activation(TP[:, :], DN[:, :], ACT.Ln))
            ch(A.activation(TP[:, :], TP[:, :], ACT.Exp, scale=-1.0), "at_rd")

    def at_dve(dve, ch):
        w = lambda nm, v: dve.wait_ge(sems[nm], v)
        n = 0
        for g in range(N_DIL):
            for dst in (QR, KR):
                for m in range(2):
                    w("at_rot", n + 1)
                    V.tensor_tensor(TC[:, :], TZ[:, n % 2, :], cosT, ALU.mult)
                    ch(V.tensor_tensor(TR[:, :], mx[n % 2][:, :], sinT, ALU.mult))
                    ch(V.tensor_tensor(nat(dst[:, 2 * g + m, :], g), perm(TC[:, :], g), perm(TR[:, :], g), ALU.add),
                       "at_rope")
                    n += 1
        n = 0
        scale = float(HD) ** -0.5
        for pr in range(2):
            if pr:
                w("at_str", pr)
            for hh in range(2):
                for blk in range(TB):
                    lo = 0 if blk else P
                    c = hh * TB + blk
                    x = SMX[:, n % 2, :]
                    w("at_s", n + 1)
                    if n >= 1:
                        w("at_p", n)
                    ch(V.tensor_tensor(x[:, lo:], mx[0][:, lo:], amask[:, lo:], ALU.add))
                    st = ST[:, :].rearrange("p (g q c) -> p g q c", g=3, q=2)
                    V.tensor_reduce(st[:, 0, 0, c:c + 1], x[:, lo:256], AX.X, ALU.max)
                    ch(V.tensor_reduce(st[:, 1:3, 0, c], x[:, 256:512].rearrange("p (g t) -> p g t", g=2), AX.X, ALU.max))
                    ch(V.tensor_scalar_mul(NM[:, 0:3], st[:, :, 0, c], -scale), "at_sm")
                    n += 1
            w("at_p", n)
            w("at_n", n)
            ch(V.tensor_copy(NM[:, 3:4], NM[:, 0:1]), "at_st")
            w("at_bca", pr * 3 + 3)
            ch(V.tensor_tensor(MG[:, :], MN[:, 0, :], MN[:, 1, :], ALU.max))
            ch(V.tensor_tensor(MG[:, :], MG[:, :], MN[:, 2, :], ALU.max))
            ch(V.tensor_tensor(CN, MN, bc(MG, 3), ALU.subtract), "at_c1")
            w("at_c2", pr + 1)
            for g in range(N_DIL):
                w("at_bcp", pr * 6 + 4 + g)
                o = DN if g == 0 else TC
                ch(V.tensor_tensor(perm(o[:, :], g), nat(mx[5][:, :], g), perm(CN[:, g, :], g), ALU.mult), "at_bcd")
                if g:
                    ch(V.tensor_tensor(DN[:, :], DN[:, :], TC[:, :], ALU.add), "at_den" if g == 2 else None)
            for g in range(N_DIL):
                o = NU if g == 0 else TC
                ch(V.tensor_tensor(perm(o[:, :], g), nat(mx[2 + g][:, :], g), perm(CN[:, g, :], g), ALU.mult),
                   "at_num" if g == 2 else None)
                if g:
                    ch(V.tensor_tensor(NU[:, :], NU[:, :], TC[:, :], ALU.add))
            w("at_rd", pr + 1)
            ch(V.tensor_tensor(OB[:, 6 + pr, :], NU[:, :], TP[:, :], ALU.mult), "at_done")

    with nc.Fori(0, L) as li:
        with nc.Block() as block:
            def load_parameters(q):
                def row(half, r, src, n):
                    q.dma_start(ROW[r:r + n, half, :], src.rearrange("(a p) -> a p", p=P)).then_inc(sems["par"], 16)
                for nm, src in (("norm_mix", "norm_mix_w"), ("norm_ffn", "norm_ffn_w"), ("hg_norm", "hg_norm_w"),
                                ("gla_norm", "gla_norm_w"), ("gla_b", "gla_a_b"), ("w0", "rw_w0"), ("a0", "rw_a0"),
                                ("k_k", "rw_k_k"), ("k_a", "rw_k_a"), ("r_k", "rw_r_k"), ("ln_w", "rw_ln_w"),
                                ("ln_b", "rw_ln_b")):
                    n = t[src].shape[1] // P
                    row(0, PA[nm], t[src][li], n)
                row(0, PA["v0"], t["rw_v0"][0], 2)
                mu = t["rw_mu"][li]
                row(0, PA["mu_r"], mu[0:W], 2)
                row(0, PA["mu_k"], mu[W + 32:2 * W + 32], 2)
                row(0, PA["mu_v"], mu[2 * W + 32:3 * W + 32], 2)
                r = PA["mu_sm"]
                one = lambda v: v.rearrange("(a p) -> a p", a=1)
                q.dma_start(ROW[r:r + 1, 0, 0:32], one(mu[W:W + 32])).then_inc(sems["par"], 16)
                q.dma_start(ROW[r:r + 1, 0, 32:64], one(mu[3 * W + 32:3 * W + 64])).then_inc(sems["par"], 16)
                q.dma_start(ROW[r:r + 1, 0, 64:128], one(mu[3 * W + 64:3 * W + 128])).then_inc(sems["par"], 16)
                for l in range(L):
                    row(0, PA["lb"] + 2 * l, t["hg_lb_table"][l], 2)
                row(0, PA["final"], t["norm_final_w"], 8)
                for j in range(3):
                    row(1, PB["conv_w"] + j * FT, t["ffn_conv_w"][li, j], FT)
                row(1, PB["conv_b"], t["ffn_conv_b"][li], FT)
                q.dma_start(LORA[0:32, :], t["rw_w2"][li]).then_inc(sems["par2"], 16)
                q.dma_start(LORA[32:64, :], t["rw_a2"][li]).then_inc(sems["par2"], 16)
                q.dma_start(LORA[64:128, :], t["rw_g2"][li]).then_inc(sems["par2"], 16)
                q.dma_start(V1[:, :, :], t["rw_v1"][0].rearrange("(k p) n -> p k n", p=P)).then_inc(sems["par2"], 16)
                q.dma_start(V2[0:32, :], t["rw_v2"][0]).then_inc(sems["par2"], 16)
                q.dma_start(AW2[0:GRANK, :], t["gla_a_w2"][li]).then_inc(sems["par2"], 16)
                q.dma_start(FLAG[:, :], t["flags"][li]).then_inc(sems["par2"], 16)

            NPAR = 12 + 1 + 3 + 3 + 2 + 1 + 3 + 1
            NPAR2 = 7

            @block.sync
            def _(sp):
                views = {"w_in": t["w_in"][li], "w_branch": t["w_branch"][li].rearrange("n w d -> (n w) d"),
                         "w_out": t["w_out"][li], "ffn_up": t["ffn_w_up"][li], "ffn_down": t["ffn_w_down"][li]}
                names = list(STRIP_AT)
                for j, pieces in enumerate(STRIPS):
                    if j >= RING:
                        sp.wait_ge(sems["tile"], last_tile(names[j - RING]) + 1)
                    for at_, kind, col, width, k0, nk in pieces:
                        src = views[kind].rearrange("(k p) n -> p k n", p=P)[:, k0:k0 + nk, col:col + width]
                        sp.dma_start(RG[j % RING][:, 0:nk, at_:at_ + width], src).then_inc(sems[f"ring{j % RING}"], 16)
                    if names[j][0] == "gate":
                        _, d, n = names[j]
                        i = d * NBR + n
                        if i >= 2:
                            sp.wait_ge(sems["tile"], TILE_AT[("br", (i - 2) // NBR, (i - 2) % NBR, 1)] + 1)
                        src = t["w_branch"][li][n].rearrange("(k p) n -> p k n", p=P)[:, :, d * 2 * P:(d + 1) * 2 * P]
                        sp.dma_start(BRG[i % 2][:, :, :], src).then_inc(sems[f"brring{i % 2}"], 16)

            need = []
            cnt = [0] * RING
            for j, pieces in enumerate(STRIPS):
                cnt[j % RING] += 16 * len(pieces)
                need.append(cnt[j % RING])

            @block.tensor
            def _(pe):
                mm = nc.tensor.matmul

                def strip(name):
                    j = STRIP_AT[name]
                    pe.wait_ge(sems[f"ring{j % RING}"], need[j])
                    return RG[j % RING]

                def begin(name):
                    i = TILE_AT[name]
                    if i >= NPJ:
                        e = TILES[i - NPJ][1]
                        pe.wait_ge(sems["out_act" if e == "a" else "out_dve"], taken(i - NPJ))
                    return pj[i % NPJ]

                def fm(name, st, col, width=P, rhs=H, r0=0, nk=KT):
                    b = begin(name)
                    for k in range(nk):
                        ins = mm(b[0:width, :], st[:, k, col:col + width], rhs[:, r0 + k, :], start=k == 0,
                                 stop=k == nk - 1)
                    ins.then_inc(sems["tile"], 1)
                    return ins

                def tokens(tb, g):
                    if g == 0:
                        return lambda k: H[:, k, tb * P:(tb + 1) * P]
                    return lambda k: H[:, k, :].rearrange("p (j r) -> p r j", r=ORDER[g])[:, tb, :]

                def tm(name, st, g=0):
                    for m in range(2):
                        b = begin((*name, m))
                        for j in range(2):
                            tok = tokens(2 * m + j, g)
                            for k in range(KT):
                                ins = mm(b[:, j * 256:(j + 1) * 256], tok(k), st[:, k, :], start=k == 0, stop=k == KT - 1)
                        ins.then_inc(sems["tile"], 1)

                pe.wait_ge(sems["par"], 16 * NPAR)
                nc.tensor.transpose(mx[0][:, 0:P], ROW[:, 0, :], ident)
                nc.tensor.transpose(mx[0][:, P:2 * P], ROW[:, 1, :], ident).then_inc(sems["par_t"], 1)
                pe.wait_ge(sems["par_c"], 1)
                norm_pe(pe, "n1")
                pe.wait_ge(sems["n1_h"], 1)
                pe.wait_ge(sems["par2"], 16 * NPAR2)

                for nm in ("rw_r", "rw_k", "rw_v"):
                    st = strip(nm)
                    for m in range(2):
                        fm((nm, m), st, m * P)
                st = strip("rw_sm")
                fm(("rw_sm", 0), st, 0)
                rwkv_pe(pe)
                for nm in ("hg_q", "hg_f"):
                    st = strip(nm)
                    for m in range(2):
                        fm((nm, m), st, m * P)
                tm(("hg_i",), strip("hg_i"))
                st = strip("hg_g")
                for m in range(2):
                    fm(("hg_g", m), st, m * P)
                linear_pe(pe, "hg", HB, 2, HD)
                st = strip("gl_qk")
                for m in range(2):
                    fm(("gl_qk", m), st, m * P)
                tm(("gl_v",), strip("gl_v"))
                st = strip("gl_g")
                for m in range(2):
                    fm(("gl_g", m), st, m * P)
                fm(("gl_a", 0), strip("gl_a"), 0, GRANK)
                pe.wait_ge(sems["out_act"], taken(TILE_AT[("gl_a", 0)]))
                mm(mx[5][:, :], AW2[0:GRANK, :], GB["al"][0:GRANK, :], start=True, stop=True).then_inc(sems["gl_u"], 1)
                linear_pe(pe, "gl", GB, 1, GDK)
                nrot = 0
                for g in range(N_DIL):
                    for nm in ("at_q", "at_k"):
                        st = strip((nm, g))
                        for m in range(2):
                            fm((nm, g, m), st, m * P)
                            pe.wait_ge(sems["out_act"], taken(TILE_AT[(nm, g, m)]))
                            if nrot >= 2:
                                pe.wait_ge(sems["at_rope"], nrot - 1)
                            mm(mx[nrot % 2][:, :], rot, TZ[:, nrot % 2, :], start=True, stop=True)\
                                .then_inc(sems["at_rot"], 1)
                            nrot += 1
                    tm(("at_v", g), strip(("at_v", g)), g)
                attention_pe(pe)
                pe.wait_ge(sems["at_done"], 2)
                for d in range(D // (2 * P)):
                    for n in range(NBR):
                        sg = strip(("gate", d, n))
                        i = d * NBR + n
                        pe.wait_ge(sems[f"brring{i % 2}"], 16 * (i // 2 + 1))
                        for m in range(2):
                            fm(("gate", d, n, m), sg, m * P)
                            fm(("br", d, n, m), BRG[i % 2], m * P, rhs=OB, r0=2 * n, nk=2)
                pe.wait_ge(sems["mt"], KT)
                for d in range(D // P):
                    fm(("out", d), strip(("out", d // 2)), (d % 2) * P, rhs=MT)
                norm_pe(pe, "n2")
                pe.wait_ge(sems["n2_h"], 1)
                for c in range(FT // 2):
                    su, sg = strip(("up", c)), strip(("gf", c))
                    for m in range(2):
                        fm(("up", 2 * c + m), su, m * P)
                        fm(("gf", 2 * c + m), sg, m * P)
                for d2 in range(D // (2 * P)):
                    ss = [strip(("down", d2, j)) for j in range(3)]
                    for m in range(2):
                        b = begin(("down", 2 * d2 + m))
                        for k in range(FT):
                            if d2 == 0 and m == 0:
                                pe.wait_ge(sems["out_dve"], taken(TILE_AT[("gf", k)]))
                            ins = mm(b[:, :], ss[k // KT][:, k % KT, m * P:(m + 1) * P], HFF[:, k, :], start=k == 0,
                                     stop=k == FT - 1)
                        ins.then_inc(sems["tile"], 1)

            @block.scalar
            def _(act):
                ch = Chain(act, sems, "act_own")
                load_parameters(act)
                act.wait_ge(sems["lb1"], 1)
                ch(A.activation(LBT[:, 2:6], LBT[:, 2:6], ACT.Exp), "lb2")
                norm_act(act, ch, "n1")
                rwkv_act(act, ch)
                hg_act(act, ch)
                gl_act(act, ch)
                at_act(act, ch)
                i = 0
                for d in range(D // (2 * P)):
                    for n in range(NBR):
                        for m in range(2):
                            take_act(act, ("gate", d, n, m))
                            if i >= 4:
                                act.wait_ge(sems["out_dve"], taken(TILE_AT[("br", d, n, m)]) - 4)
                            ch(A.activation(SG[i % 4], pj[TILE_AT[("gate", d, n, m)] % NPJ][:, :], ACT.Sigmoid), "out_act")
                            i += 1
                act.wait_ge(sems["x_mid"], 1)
                norm_act(act, ch, "n2")
                for c in range(FT + 1):
                    if c < FT:
                        take_act(act, ("up", c))
                        if c == 0:
                            act.wait_ge(sems["uppad"], 1)
                        if c >= 2:
                            act.wait_ge(sems["conv"], c - 1)
                        ch(A.activation(UP[c % 2][:, 2:], pj[TILE_AT[("up", c)] % NPJ][:, :], ACT.Copy), "out_act")
                    if c >= 1:
                        act.wait_ge(sems["conv"], c)
                        ch(A.activation(FS[(c - 1) % 2], FC[(c - 1) % 3], ACT.Sigmoid), "fsig")

            @block.vector
            def _(dve):
                ch = Chain(dve, sems, "dve_own")
                dve.wait_ge(sems["par_t"], 1)
                V.tensor_copy(PC_[:, 0:NPA], mx[0][:, 0:NPA])
                ch(V.tensor_copy(PC_[:, NPA:NPA + NPB], mx[0][:, P:P + NPB]), "par_c")
                dve.wait_ge(sems["par2"], 16 * NPAR2)
                t0, t1 = (PC_[:, PA["lb"] + 2 * l:PA["lb"] + 2 * l + 2] for l in range(2))
                ch(V.tensor_tensor(LBT[:, 0:2], t0, t1, ALU.max))
                V.tensor_tensor(LBT[:, 2:4], t0, LBT[:, 0:2], ALU.subtract)
                ch(V.tensor_tensor(LBT[:, 4:6], t1, LBT[:, 0:2], ALU.subtract), "lb1")
                dve.wait_ge(sems["lb2"], 1)
                ch(V.tensor_tensor(LBT[:, 6:8], LBT[:, 2:4], LBT[:, 4:6], ALU.add))
                ch(V.reciprocal(LBT[:, 6:8], LBT[:, 6:8]))
                V.tensor_tensor(LBT[:, 8:10], LBT[:, 2:4], LBT[:, 6:8], ALU.mult)
                ch(V.tensor_tensor(LBT[:, 10:12], LBT[:, 4:6], LBT[:, 6:8], ALU.mult))
                ch(V.scalar_tensor_tensor(LBT[:, 12:14], LBT[:, 10:12], FLAG[:, 0:1], LBT[:, 8:10], ALU.mult, ALU.add))
                ch(V.tensor_tensor(LB[:, :], LBT[:, 12:14], LBT[:, 8:10], ALU.subtract))
                ch(V.tensor_scalar(OMLB[:, :], LB[:, :], -1.0, 1.0, ALU.mult, ALU.add))
                norm_dve(dve, "n1", "norm_mix")
                rwkv_dve(dve, ch)
                hg_dve(dve, ch)
                gl_dve(dve, ch)
                at_dve(dve, ch)

                def tile(name):
                    dve.wait_ge(sems["tile"], TILE_AT[name] + 1)
                    return pj[TILE_AT[name] % NPJ][:, :]

                i = 0
                for d in range(D // (2 * P)):
                    for n in range(NBR):
                        for m in range(2):
                            dve.wait_ge(sems["out_act"], taken(TILE_AT[("gate", d, n, m)]))
                            b = tile(("br", d, n, m))
                            mt = MT[:, 2 * d + m, :]
                            o = mt if n == 0 else MTMP[i % 2]
                            ch(V.tensor_tensor(o, b, SG[i % 4], ALU.mult), "out_dve")
                            if n:
                                ch(V.tensor_tensor(mt, mt, o, ALU.add), "mt" if n == NBR - 1 else None)
                            i += 1
                for d in range(D // P):
                    ch(V.tensor_tensor(X[:, d, :], tile(("out", d)), X[:, d, :], ALU.add), "out_dve")
                dve.sem_inc(sems["x_mid"], 1)
                norm_dve(dve, "n2", "norm_ffn")
                for u in range(2):
                    ins = V.memset(UP[u][:, 0:2], 0.0)
                ch(ins, "uppad")
                for c in range(FT):
                    u, f = UP[c % 2], FC[c % 3]
                    dve.wait_ge(sems["out_act"], taken(TILE_AT[("up", c)]))
                    ch(V.tensor_scalar(f, u[:, 2:], pb_("conv_w", c), pb_("conv_b", c), ALU.mult, ALU.add))
                    ch(V.scalar_tensor_tensor(f, u[:, 1:S + 1], pb_("conv_w", FT + c), f, ALU.mult, ALU.add))
                    ch(V.scalar_tensor_tensor(f, u[:, 0:S], pb_("conv_w", 2 * FT + c), f, ALU.mult, ALU.add), "conv")
                    dve.wait_ge(sems["fsig"], c + 1)
                    ch(V.tensor_tensor(FS[c % 2], FS[c % 2], f, ALU.mult))
                    ch(V.tensor_tensor(HFF[:, c, :], tile(("gf", c)), FS[c % 2], ALU.mult), "out_dve")
                for d in range(D // P):
                    ch(V.tensor_tensor(X[:, d, :], tile(("down", d)), X[:, d, :], ALU.add), "out_dve")

        clear()

    with nc.Block() as block:
        @block.scalar
        def _(act):
            ch = Chain(act, sems, "act_own")
            norm_act(act, ch, "n1")

        @block.vector
        def _(dve):
            norm_dve(dve, "n1", "final")
            for i in range(2 * TB):
                dve.wait_ge(sems["x_t"], i + 1)
                V.tensor_copy(arena[:, i * 512:(i + 1) * 512], pj[i % 2][:, :]).then_inc(sems["x_out"], 1)

        @block.tensor
        def _(pe):
            norm_pe(pe, "n1")
            pe.wait_ge(sems["n1_h"], 1)
            for i in range(2 * TB):
                tb, hf = divmod(i, 2)
                if i >= 2:
                    pe.wait_ge(sems["x_out"], i - 1)
                for k in range(4):
                    ins = tr(pj[i % 2][:, k * P:(k + 1) * P], H[:, 4 * hf + k, tb * P:(tb + 1) * P], ident)
                ins.then_inc(sems["x_t"], 1)

        @block.sync
        def _(sp):
            for tb in range(TB):
                sp.wait_ge(sems["x_out"], 2 * tb + 2)
                sp.dma_start(out[0, tb * P:(tb + 1) * P, :], arena[:, tb * D:(tb + 1) * D]).then_inc(sems["x_in"], 16)
            sp.wait_ge(sems["x_in"], 16 * TB)


CONSTS = (("ident", P), ("ones", P), ("oblk", P), ("rot", P), ("lmask", 8 * P), ("amask", 4 * P), ("rmask", 4 * P),
          ("cos", S), ("sin", S), ("rst64", S), ("rst128", S))


def constants():
    i = np.arange(P)
    row, col = i[:, None], i[None, :]
    c = {"ident": row == col, "ones": np.ones((P, P)), "oblk": row // HD == col // HD}
    hd = HD // 2
    c["rot"] = (row - hd == col) * (row % HD >= hd) * -1.0 + (row + hd == col) * (row % HD < hd) * 1.0
    lv = [(row // (2 * n) == col // (2 * n)) & (row // n % 2 == 0) & (col // n % 2 == 1) for n in LEVELS]
    c["lmask"] = np.concatenate(lv + [row == col], 1)
    neg = lambda ok: np.where(ok, 0.0, -BIG)
    c["amask"] = np.concatenate([neg(col >= row), neg(col <= row), neg(col <= row),
                                 neg(((row - col) % (DILS[2] // DILS[1]) == 0) & (col <= row))], 1)
    same = row // RC == col // RC
    strict, incl = same & (row < col), same & (row <= col)
    c["rmask"] = np.concatenate([strict, incl, strict, incl], 1)
    inv = 10000.0 ** (-np.arange(hd, dtype=np.float32) / np.float32(hd))
    ang = (inv.astype(np.float32)[:, None] * np.arange(S, dtype=np.float32)[None, :]).astype(np.float32)
    c["cos"], c["sin"] = (np.tile(f(ang.astype(np.float64)), (4, 1)) for f in (np.cos, np.sin))
    t_ = np.arange(S)
    c["rst64"], c["rst128"] = (np.tile((t_ % n != 0)[None, :], (P, 1)) for n in (RC, P))
    table = np.concatenate([np.asarray(c[nm], np.float32) for nm, _ in CONSTS], 1)
    cols = np.zeros((P, 8), np.float32)
    cols[:, C_ONE], cols[:, C_EPS], cols[:, C_GN] = 1.0, 1e-6, 64e-5
    cols[:, C_LOG] = LOG_SHIFT / 2 * np.log(2.0)
    cols[:, C_SM] = np.where(i < 32, 2.0, 1.0)
    flags = np.zeros((L, P, 2), np.float32)
    flags[:, :, 0] = (np.arange(L) > 0)[:, None]
    flags[:, :, 1] = 1.0 - flags[:, :, 0]
    return {"consts": np.ascontiguousarray(table), "const_cols": cols, "flags": flags}


INPUTS = ("x", "norm_mix_w", "norm_ffn_w", "norm_final_w", "w_in", "hg_lb_table", "hg_norm_w", "gla_a_w2", "gla_a_b",
          "gla_norm_w", "rw_mu", "rw_w0", "rw_w2", "rw_a0", "rw_a2", "rw_g2", "rw_k_k", "rw_k_a", "rw_r_k", "rw_ln_w",
          "rw_ln_b", "rw_v0", "rw_v1", "rw_v2", "w_branch", "w_out", "ffn_w_up", "ffn_conv_w", "ffn_conv_b",
          "ffn_w_down")


def kernel(**inputs):
    import concourse.bacc as bacc
    from concourse.bass_utils import run_bass_kernel_spmd

    nc = bacc.Bacc("TRN2", target_bir_lowering=False, num_devices=1)
    arrays = {n: np.ascontiguousarray(inputs[n]) for n in INPUTS}
    arrays.update(constants())
    t = {n: nc.dram_tensor(f"in_{n}", a.shape, F32, kind="ExternalInput").ap() for n, a in arrays.items()}
    out = nc.dram_tensor("out", (1, S, D), F32, kind="ExternalOutput").ap()
    build(nc, t, out)
    r = run_bass_kernel_spmd(nc, [{f"in_{n}": a for n, a in arrays.items()}], core_ids=[0])
    return r.results[0]["out"]
```

```python
from itertools import chain

import numpy as np

import concourse.bass as bass
from concourse import mybir

F32 = mybir.dt.float32
U32 = mybir.dt.uint32
ALU = mybir.AluOpType
ACT = mybir.ActivationFunctionType
AX = mybir.AxisListType

P = 128
D = 1024
S = 512
L = 2
KT = D // P
W = D // 4
HD = 64
NH = W // HD
NBR = 4
DFF = 11 * D // 4
FT = DFF // P
GDK = 32
GRANK = 16
TAU = 16.0
N_DIL = 3
DILS = (1, 4, 16)
ORDER = (1, 4, 4)
TB = S // P
RC = 64
NRC = S // RC

HG0 = 0
GL0 = 4 * W
GLW = 2 * NH * GDK + 2 * W + GRANK
RW0 = GL0 + GLW
RWW = 3 * W + 32 + 32 + 64
AT0 = RW0 + RWW
GT0 = AT0 + 9 * W
N_IN = GT0 + NBR * D

BR_ORDER = (2, 0, 1, 3)
GATE_ITEMS = [(n, d) for n in BR_ORDER for d in range(D // (2 * P))]

LEVELS = (64, 32, 16, 8, 4, 2, 1)
RING = 4
NPJ = 2
NMX = 6
BIG = 8.0e9

C_ONE, C_EPS, C_GN, C_LOG, C_SM = range(5)
LOG_SHIFT = 20


def _rows(*items):
    at, n = {}, 0
    for name, rows in items:
        at[name] = n
        n += rows
    return at, n


PA, NPA = _rows(("norm_mix", 8), ("norm_ffn", 8), ("hg_norm", 2), ("gla_norm", 2), ("gla_b", 1), ("w0", 2), ("a0", 2),
                ("k_k", 2), ("k_a", 2), ("r_k", 2), ("ln_w", 2), ("ln_b", 2), ("v0", 2), ("mu_r", 2), ("mu_k", 2),
                ("mu_v", 2), ("mu_sm", 1), ("lb", 4), ("final", 8))
PB, NPB = _rows(("conv_w", 3 * FT), ("conv_b", FT))


def strips():
    out, at = [], {}

    def add(name, *pieces):
        at[name] = len(out)
        out.append(pieces)

    def win(name, col, width=2 * P):
        add(name, (0, "w_in", col, width, 0, KT))

    win("rw_r", RW0)
    win("rw_k", RW0 + W + 32)
    win("rw_v", RW0 + 2 * W + 32)
    add("rw_sm", (0, "w_in", RW0 + W, 32, 0, KT), (32, "w_in", RW0 + 3 * W + 32, 32, 0, KT),
        (64, "w_in", RW0 + 3 * W + 64, 64, 0, KT))
    for n, nm in enumerate(("hg_q", "hg_f", "hg_i", "hg_g")):
        win(nm, HG0 + n * W)
    win("gl_qk", GL0)
    win("gl_v", GL0 + W)
    win("gl_g", GL0 + 2 * W)
    win("gl_a", GL0 + 3 * W, GRANK)
    for g in range(N_DIL):
        win(("at_q", g), AT0 + g * W)
        win(("at_k", g), AT0 + (N_DIL + g) * W)
        win(("at_v", g), AT0 + (2 * N_DIL + g) * W)
    for n in BR_ORDER:
        for d in range(D // (2 * P)):
            win(("gate", d, n), GT0 + n * D + d * 2 * P)
    for d in range(D // (2 * P)):
        add(("out", d), (0, "w_out", d * 2 * P, 2 * P, 0, KT))
    for c in range(FT // 2):
        add(("up", c), (0, "ffn_up", c * 2 * P, 2 * P, 0, KT))
        add(("gf", c), (0, "ffn_up", DFF + c * 2 * P, 2 * P, 0, KT))
    for d in range(D // (2 * P)):
        for j, k0 in enumerate(range(0, FT, KT)):
            add(("down", d, j), (0, "ffn_down", d * 2 * P, 2 * P, k0, min(KT, FT - k0)))
    return out, at


STRIPS, STRIP_AT = strips()


def tiles():
    t = []
    for nm in ("rw_r", "rw_k", "rw_v"):
        t += [((nm, m), "a") for m in range(2)]
    t.append((("rw_sm", 0), "a"))
    for nm in ("hg_q", "hg_f", "hg_i", "hg_g", "gl_qk", "gl_v", "gl_g"):
        t += [((nm, m), "a") for m in range(2)]
    t.append((("gl_a", 0), "a"))
    for g in range(N_DIL):
        for nm in ("at_q", "at_k", "at_v"):
            t += [((nm, g, m), "a") for m in range(2)]
    for n in BR_ORDER:
        for d in range(D // (2 * P)):
            for m in range(2):
                t += [(("gate", d, n, m), "a"), (("br", d, n, m), "d")]
    for d in range(D // P):
        t.append((("out", d), "d"))
    for c in range(FT):
        t += [(("up", c), "a"), (("gf", c), "d")]
    for d in range(D // P):
        t.append((("down", d), "d"))
    return t


TILES = tiles()
TILE_AT = {n: i for i, (n, _) in enumerate(TILES)}


def taken(i):
    return sum(1 for _, e in TILES[:i + 1] if e == TILES[i][1])


def last_tile(name):
    if isinstance(name, str):
        return TILE_AT[(name, 0 if name in ("rw_sm", "gl_a") else 1)]
    if name[0] in ("out", "up", "gf", "down"):
        return TILE_AT[(name[0], 2 * name[1] + 1)]
    return TILE_AT[(*name, 1)]


STORED = [n for n, _ in TILES if n[0][0:3] in ("hg_", "gl_", "at_")]
STORE_AT = {n: i for i, n in enumerate(STORED)}


def run(steps):
    for _ in steps:
        pass


def interleave(main, filler):
    for n in main:
        for _ in range(n):
            next(filler, None)


STAGES = {
    "rw_act": (("rw_sm1", 1), ("rw_sg", 1), ("rw_sig1", 1), ("rw_sig3", 1), ("rw_vm1", 2), ("rw_vm3", 1), ("rw_kn", 1),
               ("rw_em", 1), ("rw_eb", 1), ("rw_en", 1)),
    "rw_dve": (("rw_sm2", 1), ("rw_smx", 1), ("rw_sig2", 1), ("rw_vm2", 1), ("rw_sq", 1), ("rw_ss2", 1),
               ("rw_cum", 1), ("rw_bp", 1), ("rw_em2", 1), ("rw_eb2", 1), ("rw_ready", 1)),
}


class Sems:

    def __init__(self, nc, n):
        self.pool, self.made = [nc.alloc_semaphore(f"sem{i}") for i in range(n)], {}
        nums = [s.num for s in self.pool]
        assert nums == list(range(nums[0], nums[0] + n)), nums
        self.range = range(nums[0], nums[-1] + 1)

    def at(self, name, v):
        for group, stages in STAGES.items():
            before = 0
            for stage, times in stages:
                if stage == name:
                    return self[group], before + v
                before += times
        return self[name], v

    def __getitem__(self, name):
        if name not in self.made:
            self.made[name] = self.pool[len(self.made)]
        return self.made[name]


class Chain:

    def __init__(self, eng, sems, own):
        self.eng, self.sems, self.own, self.n = eng, sems, own, {}

    def __call__(self, ins, name=None):
        name = name or self.own
        self.n[name] = self.n.get(name, 0) + 1
        sem, count = self.sems.at(name, self.n[name])
        ins.then_inc(sem, 1)
        self.eng.wait_ge(sem, count)


def build(nc, t, out):
    sems = Sems(nc, 156)
    z_dram = nc.dram_tensor("z_scratch", (len(STORED), P, S), F32).ap()
    x_dram = nc.dram_tensor("x_scratch", (P, KT, S), F32).ap()

    def sb(name, *shape):
        return nc.alloc_sbuf_tensor(name, [P, *shape], F32)

    X = sb("x_fm", KT, S)
    H = sb("h_fm", KT, S)
    RG = [sb(f"ring{i}", KT, 2 * P) for i in range(RING)]
    BRG = [sb(f"brring{i}", 2, 2 * P) for i in range(2)]
    OB = sb("branch_out", KT, S)
    VF = sb("v_first", 2, S)
    CC = sb("consts", t["consts"].shape[1])
    CST = sb("const_cols", 8)
    ROW = sb("param_rows", 2, P)
    PC_ = sb("param_cols", NPA + NPB)
    LORA = sb("lora", 2 * P)
    V1 = sb("v1", 2, 32)
    V2 = sb("v2", 2 * P)
    AW2 = sb("gla_w2", P)
    FLAG = sb("layer_flag", 2)
    LB = sb("lower_bound", 2)
    OMLB = sb("one_minus_lb", 2)
    LBT = sb("lb_tmp", 16)
    arena = sb("arena", 24900)
    PS = [nc.alloc_psum_tensor(f"ps{i}", [P, 512], F32) for i in range(8)]
    pj, mx = PS[:NPJ], PS[NPJ:]

    ccat = {}
    at = 0
    for nm, n in CONSTS:
        ccat[nm] = at
        at += n
    cc = lambda nm: CC[:, ccat[nm]:ccat[nm] + dict(CONSTS)[nm]]
    ident, ones, oblk, rot = cc("ident"), cc("ones"), cc("oblk"), cc("rot")
    lmask = cc("lmask").rearrange("p (l t) -> p l t", l=8)
    amask, rmask = cc("amask"), cc("rmask")
    cosT, sinT, rst64, rst128 = cc("cos"), cc("sin"), cc("rst64"), cc("rst128")

    def pa(name, i=0):
        return PC_[:, PA[name] + i:PA[name] + i + 1]

    def pb_(name, i=0):
        return PC_[:, NPA + PB[name] + i:NPA + PB[name] + i + 1]

    def cst(i):
        return CST[:, i:i + 1]

    ARENA = 24900
    SG_AT = ARENA - 6 * S

    class Arena:
        def __init__(self):
            self.at = 0

        def __call__(self, *shape):
            n = int(np.prod(shape))
            v = arena[:, self.at:self.at + n]
            self.at += n
            assert self.at <= 24900, self.at
            if len(shape) == 2:
                v = v.rearrange("p (a b) -> p a b", a=shape[0])
            elif len(shape) == 3:
                v = v.rearrange("p (a b c) -> p a b c", a=shape[0], b=shape[1])
            return v

    a = Arena()
    ZT, RS = a(2, S + 1), a(7, S)
    RA, RLW, RB, RG_, RBN, RKT = (a(2, S) for _ in range(6))
    AR = a(2, 2, S)
    RT1, RT2 = a(2, S), a(2, S)
    PCH = a(2, NRC)
    mark = a.at
    TOK = a(4, TB, P)
    G = a(8, 4 * P)
    TM, TTM = a(8, P), a(8, P)
    SH = a(NRC + 1, HD)
    SPR = a(HD)
    as_tiles = lambda v, n: v.rearrange("p (a b) -> p a b", a=n)
    CM = as_tiles(RB.rearrange("p a b -> p (a b)"), 8)
    YM = as_tiles(RS[:, 2:4, :].rearrange("p a b -> p (a b)"), 8)
    W1, TV, U = (as_tiles(RS[:, i, :], 8) for i in (0, 1, 6))
    TAT = RT1[:, 0, :]
    VT = G[:, 0, :]
    YF = RLW

    def lin_buffers(nt):
        a = Arena()
        b = {}
        for nm in ("q", "k", "b", "t1", "t2", "t3"):
            b[nm] = a(nt, S)
        for nm in ("g", "o", "u1", "u2"):
            b[nm] = a(2, S)
        b["v"] = a(TB, 2 * P)
        b["x"] = [a(nt, S) for _ in range(2)]
        b["d"] = [a(nt, S) for _ in range(2)]
        b["a"] = a(NH, TB, P)
        b["kdt"] = a(nt, TB, P)
        b["sh"] = a(TB, nt, HD)
        b["ebl"] = a(nt, TB)
        b["al"] = a(S)
        b["f"] = a(nt, S)
        assert a.at <= SG_AT, a.at
        return b

    HB, GB = lin_buffers(2), lin_buffers(1)

    a = Arena()
    QR, KR = a(6, S), a(6, S)
    VA = a(N_DIL * TB, 2 * P)
    TC, TR = a(S), a(S)
    SMX = a(2, 4 * P)
    PT = a(2, 4 * P)
    PE_ = a(2, 4 * P)
    TZ = [v[:, i, :] for v in (SMX, PT, PE_) for i in range(2)]
    NZ = len(TZ)
    ST = a(2, 3 * 2 * 2 * TB)
    STR = a(P)
    NM = a(2, 4)
    MN = a(3, S)
    CN = a(3, S)
    MG, DN, NU, TP = a(S), a(S), a(S), a(S)
    assert a.at <= SG_AT

    a = Arena()
    a.at = SG_AT
    SG = [a(S) for _ in range(4)]
    MTMP = [a(S) for _ in range(2)]
    MT = X
    a = Arena()
    HFF = a(FT, S)
    UP = [a(S + 2) for _ in range(2)]
    FC = [a(S) for _ in range(3)]
    FS = [a(S) for _ in range(2)]
    SQN = a(2, S)
    RSTD = a(S)
    NTMP = a(S)
    XR = a(KT, S)
    STG = [OB[:, i, :] for i in range(4)]

    with nc.Block() as block:
        @block.sync
        def _(sp):
            sp.dma_start(CC[:, :], t["consts"]).then_inc(sems["c_in"], 16)
            sp.dma_start(CST[:, :], t["const_cols"]).then_inc(sems["c_in"], 16)
            for tb in range(TB):
                sp.dma_start(arena[:, tb * D:(tb + 1) * D], t["x"][0, tb * P:(tb + 1) * P, :]).then_inc(sems["x_in"], 16)

        @block.tensor
        def _(pe):
            pe.wait_ge(sems["c_in"], 32)
            pe.wait_ge(sems["x_in"], 16 * TB)
            for k in range(KT):
                if k >= 2:
                    pe.wait_ge(sems["x_out"], k - 1)
                for tb in range(TB):
                    ins = nc.tensor.transpose(pj[k % 2][:, tb * P:(tb + 1) * P],
                                              arena[:, tb * D + k * P:tb * D + (k + 1) * P], ident)
                ins.then_inc(sems["x_t"], 1)

        @block.vector
        def _(dve):
            nc.vector.memset(VF[:, :, :], 0.0)
            nc.vector.memset(ROW[:, :, :], 0.0).then_inc(sems["row0"], 1)
            for k in range(KT):
                dve.wait_ge(sems["x_t"], k + 1)
                nc.vector.tensor_copy(X[:, k, :], pj[k % 2][:, :]).then_inc(sems["x_out"], 1)

    def clear():
        nc.sync.sem_clear(sems.range)
        nc.all_engine_barrier()

    clear()

    def norm_pe(pe, tag):
        for k in range(KT):
            pe.wait_ge(sems[tag + "_sq"], k + 1)
            ins = nc.tensor.matmul(mx[0][:, :], ones, SQN[:, k % 2, :], start=k == 0, stop=k == KT - 1)
            ins.then_inc(sems[tag + "_ss"], 1)

    def norm_act(act, ch, tag, x=X):
        for k in range(KT):
            if k >= 2:
                act.wait_ge(sems[tag + "_ss"], k - 1)
            nc.scalar.activation(SQN[:, k % 2, :], x[:, k, :], ACT.Square).then_inc(sems[tag + "_sq"], 1)
        act.wait_ge(sems[tag + "_ss"], KT)
        ch(nc.scalar.activation(NTMP[:, :], mx[0][:, :], ACT.Ln, bias=cst(C_EPS), scale=1.0 / D))
        ch(nc.scalar.activation(RSTD[:, :], NTMP[:, :], ACT.Exp, scale=-0.5), tag + "_rstd")

    def norm_dve(dve, tag, wname, x=X):
        dve.wait_ge(sems[tag + "_rstd"], 1)
        for k in range(KT):
            ins = nc.vector.scalar_tensor_tensor(H[:, k, :], x[:, k, :], pa(wname, k), RSTD[:, :], ALU.mult, ALU.mult)
        ins.then_inc(sems[tag + "_h"], 1)

    def sig_act(ch, xs, tmp, src, bias=0.0, scale=1.0, name=None):
        nc.scalar.activation(xs, src, ACT.Identity, bias=bias, scale=scale)
        ch(nc.scalar.activation(tmp, src, ACT.Abs, bias=bias, scale=scale))
        ch(nc.scalar.activation(tmp, tmp, ACT.Exp, scale=-1.0))
        ch(nc.scalar.activation(tmp, tmp, ACT.Ln, bias=cst(C_ONE), scale=1.0), name)

    def sigmoid(ch, dst, src, name):
        ch(nc.scalar.activation(dst, src, ACT.Sigmoid), name)

    def sig_dve(ch, dst, xs, tmp, name=None):
        ch(nc.vector.scalar_tensor_tensor(dst, xs, 0.0, tmp, ALU.min, ALU.subtract), name)

    flat = lambda v: v.rearrange("p a b -> p (a b)")

    mm = nc.tensor.matmul
    tr = nc.tensor.transpose
    V, A = nc.vector, nc.scalar
    TOKN = ("a", "b", "k", "v")
    half = lambda hh: slice(HD * hh, HD * hh + HD)

    def rwkv_pe(pe):
        w = lambda nm, v: pe.wait_ge(*sems.at(nm, v))
        yield 3
        w("rw_smx", 1)
        w("rw_shift", 7)
        for m in range(2):
            mm(mx[m][:, :], LORA[0:32, m * P:(m + 1) * P], RA[0:32, 0, :], start=True, stop=True)
        for m in range(2):
            mm(mx[2 + m][:, :], LORA[32:64, m * P:(m + 1) * P], RA[32:64, 0, :], start=True, stop=True)
        for m in range(2):
            ins = mm(mx[4][0:32, :], V1[:, m, :], RS[:, 4 + m, :], start=m == 0, stop=m == 1)
        ins.then_inc(sems["rw_lora"], 1)
        yield 4
        w("rw_sig1", 1)
        for m in range(2):
            mm(mx[m][:, :], V2[0:32, m * P:(m + 1) * P], VT[0:32, :], start=True, stop=True)
        for m in range(2):
            ins = mm(mx[2 + m][:, :], LORA[64:128, m * P:(m + 1) * P], RBN[64:128, 0, :], start=True, stop=True)
        ins.then_inc(sems["rw_lora2"], 1)
        yield 3
        w("rw_sq", 1)
        for m in range(2):
            ins = mm(mx[4 + m][:, :], oblk, RT1[:, m, :], start=True, stop=True)
        ins.then_inc(sems["rw_ss"], 1)
        yield 3
        w("rw_bp", 1)
        for m in range(2):
            ins = mm(mx[m][:, :], oblk, RT1[:, m, :], start=True, stop=True)
        ins.then_inc(sems["rw_bs"], 1)
        yield 3
        w("rw_ready", 1)
        for p in range(2):
            src = (AR[:, p, 0, :], RA[:, p, :], RKT[:, p, :], RS[:, 4 + p, :])
            for q in range(4):
                for tb in range(TB):
                    ins = tr(mx[q][:, tb * P:(tb + 1) * P], src[q][:, tb * P:(tb + 1) * P], ident)
                ins.then_inc(sems["rw_tr"], 1)
            yield 1
            w("rw_tok", 4 * (p + 1))
            for hh in range(2):
                for tb in range(TB):
                    i = hh * TB + tb
                    if i >= 2:
                        w("rw_g", 8 * p + i - 1)
                    ts = slice(tb * P, (tb + 1) * P)
                    mm(mx[i % 2][:, 0:256], RA[half(hh), p, ts], AR[half(hh), p, :, ts], start=True, stop=True)
                    mm(mx[i % 2][:, 256:512], RKT[half(hh), p, ts], AR[half(hh), p, :, ts], start=True, stop=True)\
                        .then_inc(sems["rw_gp"], 1)
            yield 1
            w("rw_g", 8 * p + 8)
            for l in range(6):
                for g in range(2):
                    n = (p * 6 + l) * 2 + g
                    y, z, zt = mx[3 * g:3 * g + 3]
                    w("rw_cm", n + 1)
                    if l:
                        w("rw_t", n - 1)
                    for j in range(4):
                        ins = mm(y[:, j * P:(j + 1) * P], CM[:, 4 * g + j, :], TM[:, 4 * g + j, :], start=True, stop=True)
                    ins.then_inc(sems["rw_y1"], 1)
                yield 1
                for g in range(2):
                    n = (p * 6 + l) * 2 + g
                    y, z, zt = mx[3 * g:3 * g + 3]
                    w("rw_ym", n + 1)
                    for j in range(4):
                        mm(z[:, j * P:(j + 1) * P], TTM[:, 4 * g + j, :], YM[:, 4 * g + j, :], start=True, stop=True)
                    for j in range(4):
                        ins = mm(zt[:, j * P:(j + 1) * P], YM[:, 4 * g + j, :], TTM[:, 4 * g + j, :], start=True, stop=True)
                    ins.then_inc(sems["rw_z"], 1)
                yield 1
            w("rw_t", (p + 1) * 12)
            for hh in range(2):
                for tb in range(TB):
                    i = hh * TB + tb
                    ins = mm(mx[0][:, i * HD:(i + 1) * HD], G[:, i, 256:384], TOK[:, 3, tb, half(hh)], start=True, stop=True)
            ins.then_inc(sems["rw_w1p"], 1)
            yield 1
            w("rw_w1", p + 1)
            for hh in range(2):
                for tb in range(TB):
                    i = hh * TB + tb
                    mm(mx[1][:, i * HD:(i + 1) * HD], TTM[:, i, :], W1[:, i, :], start=True, stop=True)
            for hh in range(2):
                for tb in range(TB):
                    i = hh * TB + tb
                    ins = mm(mx[2][half(hh), tb * P:(tb + 1) * P], TOK[:, 0, tb, half(hh)], TTM[:, i, :], start=True, stop=True)
            ins.then_inc(sems["rw_tvp"], 1)
            yield 1
            w("rw_tv", 2 * (p + 1))
            for c in range(NRC):
                tb, par = divmod(c, 2)
                rows = slice(RC * par, RC * par + RC)
                w("rw_s", p * NRC + c + 1)
                for hh in range(2):
                    ins = mm(mx[3 + hh][rows, 0:HD], TAT[half(hh), c * RC:(c + 1) * RC], SH[half(hh), c, :],
                             start=True, stop=True)
                ins.then_inc(sems["rw_up"], 1)
                if c % 2 == 0:
                    yield 1
                w("rw_u", p * NRC + c + 1)
                if c < NRC - 1:
                    for hh in range(2):
                        mm(mx[5][half(hh), 0:HD], TOK[rows, 1, tb, half(hh)], U[rows, hh * TB + tb, :],
                           start=True, stop=False)
                        ins = mm(mx[5][half(hh), 0:HD], TOK[rows, 2, tb, half(hh)], TOK[rows, 3, tb, half(hh)],
                                 start=False, stop=True)
                    ins.then_inc(sems["rw_sp"], 1)
            for hh in range(2):
                for tb in range(TB):
                    i = hh * TB + tb
                    o = mx[0][half(hh), tb * P:(tb + 1) * P]
                    mm(o, U[:, i, :], G[:, i, 128:256], start=True, stop=False)
                    mm(o, TOK[:, 3, tb, half(hh)], G[:, i, 384:512], start=False, stop=False)
                    for par in range(2):
                        c = 2 * tb + par
                        ins = mm(mx[0][half(hh), c * RC:(c + 1) * RC], SH[half(hh), c, :],
                                 AR[half(hh), p, 1, c * RC:(c + 1) * RC], start=False, stop=par == 1)
            ins.then_inc(sems["rw_yp"], 1)
            yield 1
            w("rw_yf", p + 1)
        for m in range(2):
            ins = mm(mx[m][:, :], oblk, YF[:, m, :], start=True, stop=True)
        ins.then_inc(sems["rw_mean"], 1)
        yield 1
        w("rw_yc", 1)
        for m in range(2):
            ins = mm(mx[2 + m][:, :], oblk, RT1[:, m, :], start=True, stop=True)
        ins.then_inc(sems["rw_var"], 1)
        yield 2

    def rwkv_act(act, ch):
        w = lambda nm, v: act.wait_ge(*sems.at(nm, v))
        sm_scale = cst(C_SM)
        i = 0
        for nm, m in [(n, m) for n in ("rw_r", "rw_k", "rw_v") for m in range(2)] + [("rw_sm", 0)]:
            take_act(act, (nm, m))
            w("rw_zpad", 1)
            if i >= 2:
                w("rw_shift", i - 1)
            ch(A.activation(ZT[:, i % 2, 1:S + 1], pj[TILE_AT[(nm, m)] % NPJ][:, :], ACT.Copy), "out_act")
            i += 1
        w("rw_shift", 7)
        sig_act(ch, RBN[:, 0, :], RT1[:, 0, :], RS[:, 6, :], scale=sm_scale, name="rw_sm1")
        w("rw_sm2", 1)
        ch(A.activation(RBN[:, 0, :], RBN[:, 0, :], ACT.Exp), "rw_sg")
        yield 3
        w("rw_lora", 1)
        ch(A.activation(VT[0:32, :], mx[4][0:32, :], ACT.Copy))
        w("rw_smx", 1)
        for m in range(2):
            sig_act(ch, RLW[:, m, :], RT1[:, m, :], mx[m][:, :], bias=pa("w0", m))
        for m in range(2):
            sig_act(ch, RKT[:, m, :], RT2[:, m, :], mx[2 + m][:, :], bias=pa("a0", m), name="rw_sig1" if m else None)
        yield 4
        w("rw_sig2", 1)
        A.activation(flat(RLW), flat(RLW), ACT.Exp)
        ch(A.activation(flat(RA), flat(RKT), ACT.Exp), "rw_sig3")
        w("rw_lora2", 1)
        for m in range(2):
            A.activation(RG_[:, m, :], mx[2 + m][:, :], ACT.Copy)
            sig_act(ch, RT2[:, m, :], RT1[:, m, :], mx[m][:, :], bias=pa("v0", m), name="rw_vm1")
        w("rw_vm2", 1)
        ch(A.activation(flat(RT2), flat(RT2), ACT.Exp), "rw_vm3")
        yield 3
        w("rw_ss2", 1)
        ch(A.activation(flat(RT1), flat(RT1), ACT.Ln, scale=float(2 ** LOG_SHIFT)))
        ch(A.activation(flat(RT1), flat(RT1), ACT.Exp, scale=-0.5, bias=cst(C_LOG)), "rw_kn")
        yield 3
        w("rw_cum", 1)
        ch(A.activation(flat(RT2), flat(RT2), ACT.Exp), "rw_em")
        w("rw_em2", 1)
        ch(A.activation(flat(RT2), flat(RB), ACT.Exp), "rw_eb")
        w("rw_eb2", 1)
        ch(A.activation(flat(RT2), flat(RB), ACT.Exp, scale=-1.0), "rw_en")
        yield 3
        for p in range(2):
            for q in (2, 3):
                w("rw_tr", 4 * p + q + 1)
                ch(A.activation(flat(TOK[:, q]), mx[q][:, :], ACT.Copy), "rw_tokx")
            yield 1
            yield 1
            for n in range(12):
                w("rw_y1", p * 12 + n + 1)
                g = n % 2
                ch(A.activation(flat(YM[:, 4 * g:4 * g + 4]), mx[3 * g][:, :], ACT.Copy), "rw_ym")
                if g:
                    yield 1
                    yield 1
            w("rw_w1p", p + 1)
            ch(A.activation(flat(W1), mx[0][:, :], ACT.Copy), "rw_w1")
            yield 1
            w("rw_tvp", p + 1)
            ch(A.activation(flat(TV), mx[1][:, :], ACT.Copy), "rw_tv")
            ch(A.activation(TAT[:, :], mx[2][:, :], ACT.Copy), "rw_tv")
            yield 1
            for _ in range(NRC // 2):
                yield 1
            w("rw_yp", p + 1)
            ch(A.activation(YF[:, p, :], mx[0][:, :], ACT.Copy), "rw_yf")
            yield 1
        yield 1
        w("rw_var", 1)
        for m in range(2):
            ch(A.activation(RT2[:, m, :], mx[2 + m][:, :], ACT.Ln, scale=1.0 / HD, bias=cst(C_GN)))
        ch(A.activation(flat(RT2), flat(RT2), ACT.Exp, scale=-0.5), "rw_rstd")
        yield 2

    def rwkv_dve(dve, ch):
        w = lambda nm, v: dve.wait_ge(*sems.at(nm, v))
        ch(V.memset(ZT[:, :, 0:1], 0.0), "rw_zpad")
        mus = [("mu_r", 0), ("mu_r", 1), ("mu_k", 0), ("mu_k", 1), ("mu_v", 0), ("mu_v", 1), ("mu_sm", 0)]
        for i in range(7):
            w("out_act", i + 1)
            z = ZT[:, i % 2, 1:S + 1]
            ch(V.tensor_tensor(RT1[:, i % 2, :], ZT[:, i % 2, 0:S], z, ALU.subtract))
            ch(V.scalar_tensor_tensor(RS[:, i, :], RT1[:, i % 2, :], pa(*mus[i]), z, ALU.mult, ALU.add), "rw_shift")
        w("rw_sm1", 1)
        sig_dve(ch, RBN[:, 0, :], RBN[:, 0, :], RT1[:, 0, :], "rw_sm2")
        w("rw_sg", 1)
        V.tensor_scalar(RA[0:32, 0, :], RBN[0:32, 0, :], 2.0, -1.0, ALU.mult, ALU.add)
        ch(V.tensor_copy(RA[32:64, 0, :], RS[32:64, 6, :]), "rw_smx")
        yield 3
        yield 4
        w("rw_sig1", 1)
        sig_dve(ch, flat(RLW), flat(RLW), flat(RT1))
        sig_dve(ch, flat(RKT), flat(RKT), flat(RT2), "rw_sig2")
        w("rw_vm1", 2)
        sig_dve(ch, flat(RT2), flat(RT2), flat(RT1), "rw_vm2")
        w("rw_sig3", 1)
        ch(V.tensor_scalar_mul(flat(RLW), flat(RLW), -float(np.exp(np.float64(-0.5)))))
        r, k, v = RS[:, 0:2, :], RS[:, 2:4, :], RS[:, 4:6, :]
        ch(V.tensor_scalar(flat(RT1), flat(v), FLAG[:, 1:2], None, ALU.mult))
        ch(V.scalar_tensor_tensor(flat(VF), flat(VF), FLAG[:, 0:1], flat(RT1), ALU.mult, ALU.add))
        ch(V.tensor_tensor(flat(RT1), flat(VF), flat(v), ALU.subtract))
        w("rw_vm3", 1)
        ch(V.tensor_tensor(flat(RT1), flat(RT1), flat(RT2), ALU.mult))
        ch(V.tensor_tensor(flat(v), flat(v), flat(RT1), ALU.add))
        w("rw_lora2", 1)
        kk = AR[:, :, 0, :]
        for m in range(2):
            ch(V.tensor_scalar(AR[:, m, 0, :], k[:, m, :], pa("k_k", m), None, ALU.mult))
        ch(V.tensor_tensor(RT1, kk, kk, ALU.mult), "rw_sq")
        yield 3
        for m in range(2):
            V.tensor_tensor_scan(RB[:, m, :], rst64, RLW[:, m, :], 0.0, ALU.mult, ALU.add)
        for m in range(2):
            ch(V.tensor_scalar(RT2[:, m, :], RA[:, m, :], -1.0, pa("k_a", m), ALU.add, ALU.mult))
        ch(V.scalar_tensor_tensor(flat(RKT), flat(RT2), 1.0, flat(k), ALU.add, ALU.mult))
        w("rw_ss", 1)
        for m in range(2):
            ins = V.tensor_scalar_max(RT1[:, m, :], mx[4 + m][:, :], 1e-24)
        ch(ins, "rw_ss2")
        ch(V.tensor_tensor(flat(RT2), flat(RB), flat(RLW), ALU.subtract), "rw_cum")
        w("rw_kn", 1)
        ch(V.tensor_tensor(kk, kk, RT1, ALU.mult))
        ch(V.tensor_tensor(RA, RA, kk, ALU.mult))
        ch(V.tensor_tensor(RT1, r, RKT, ALU.mult))
        for m in range(2):
            ins = V.tensor_scalar(RT1[:, m, :], RT1[:, m, :], pa("r_k", m), None, ALU.mult)
        ch(ins, "rw_bp")
        yield 3
        w("rw_bs", 1)
        for m in range(2):
            ins = V.tensor_tensor(RBN[:, m, :], mx[m][:, :], v[:, m, :], ALU.mult)
        ch(ins)
        w("rw_em", 1)
        ch(V.tensor_tensor(kk, kk, RT2, ALU.mult), "rw_em2")
        w("rw_eb", 1)
        V.tensor_copy(PCH, RT2.rearrange("p m (c t) -> p m c t", t=RC)[:, :, :, RC - 1])
        ch(V.tensor_tensor(AR[:, :, 1, :], r, RT2, ALU.mult), "rw_eb2")
        w("rw_en", 1)
        V.tensor_tensor(RA, RA, RT2, ALU.mult)
        ch(V.tensor_tensor(RKT, RKT, RT2, ALU.mult), "rw_ready")
        yield 3
        for p in range(2):
            for q in range(2):
                w("rw_tr", 4 * p + q + 1)
                ch(V.tensor_copy(flat(TOK[:, q]), mx[q][:, :]), "rw_tok")
            w("rw_tokx", 2 * p + 2)
            ch(V.memset(SH[:, 0, :], 0.0), "rw_tok")
            for j in range(8):
                ins = V.tensor_copy(TM[:, j, :], ident)
            for j in range(8):
                ins = V.tensor_copy(TTM[:, j, :], ident)
            ch(ins, "rw_tok")
            yield 1
            for i in range(8):
                w("rw_gp", 8 * p + i + 1)
                ch(V.tensor_tensor(G[:, i, :], mx[i % 2][:, :], rmask, ALU.mult), "rw_g")
            yield 1

            def masked(l):
                for g in range(2):
                    gs = slice(4 * g, 4 * g + 4)
                    if l:
                        w("rw_y1", (p * 6 + l - 1) * 2 + g + 1)
                    ch(V.tensor_tensor(CM[:, gs, :], G[:, gs, 0:P], bc(lmask[:, 6 - l, :], 4), ALU.mult), "rw_cm")

            masked(0)
            for l in range(6):
                if l < 5:
                    masked(l + 1)
                yield 1
                for g in range(2):
                    gs = slice(4 * g, 4 * g + 4)
                    w("rw_z", (p * 6 + l) * 2 + g + 1)
                    V.tensor_tensor(flat(TM[:, gs, :]), flat(TM[:, gs, :]), mx[3 * g + 1][:, :], ALU.subtract)
                    ch(V.tensor_tensor(flat(TTM[:, gs, :]), flat(TTM[:, gs, :]), mx[3 * g + 2][:, :], ALU.subtract), "rw_t")
                yield 1
            yield 1
            yield 1
            w("rw_tv", 2 * (p + 1))
            ch(V.memset(SH[:, 0, :], 0.0), "rw_s")
            for c in range(NRC):
                tb, par = divmod(c, 2)
                rows = slice(RC * par, RC * par + RC)
                pc = PCH[:, p, c:c + 1]
                w("rw_up", p * NRC + c + 1)
                for hh in range(2):
                    i = hh * TB + tb
                    ins = V.scalar_tensor_tensor(U[rows, i, :], mx[3 + hh][rows, 0:HD], -1.0, TV[rows, i, :],
                                                 ALU.mult, ALU.subtract)
                ch(ins, "rw_u")
                if c % 2 == 0:
                    yield 1
                if c < NRC - 1:
                    ch(V.tensor_scalar(SPR[:, :], SH[:, c, :], pc, None, ALU.mult))
                    w("rw_sp", p * (NRC - 1) + c + 1)
                    ch(V.scalar_tensor_tensor(SH[:, c + 1, :], mx[5][:, 0:HD], pc, SPR[:, :], ALU.mult, ALU.add), "rw_s")
            yield 1
        w("rw_mean", 1)
        for m in range(2):
            ins = V.scalar_tensor_tensor(YF[:, m, :], mx[m][:, :], -1.0 / HD, YF[:, m, :], ALU.mult, ALU.add)
        ch(ins)
        ch(V.tensor_tensor(RT1, YF, YF, ALU.mult), "rw_yc")
        yield 1
        w("rw_rstd", 1)
        ch(V.tensor_tensor(YF, YF, RT2, ALU.mult))
        for m in range(2):
            ins = V.tensor_scalar(YF[:, m, :], YF[:, m, :], pa("ln_w", m), pa("ln_b", m), ALU.mult, ALU.add)
        ch(ins)
        ch(V.tensor_tensor(YF, YF, RBN, ALU.add))
        ch(V.tensor_tensor(OB[:, 4:6, :], YF, RG_, ALU.mult), "rw_done")
        yield 2

    def bc(v, n):
        return v.unsqueeze(1).to_broadcast([v.shape[0], n, v.shape[1]])

    def take_act(act, name):
        act.wait_ge(sems["tile"], TILE_AT[name] + 1)

    NL = len(LEVELS)
    HG_LEAVES = dict(d=NL, e=NL, x=NL, sc=(NL + 1) * NH, cp=(NL + 1) * NH, kdt=2)

    def lin_wait(eng, pre, nm, v):
        eng.wait_ge(sems["lin_" + nm], v + (HG_LEAVES.get(nm, 1) if pre == "gl" else 0))

    def linear_pe(pe, pre, b, nt, dk):
        w = lambda nm, v: lin_wait(pe, pre, nm, v)
        hpt = P // dk
        yield 4
        for l in range(len(LEVELS) + 1):
            if l:
                yield 1
            if l < len(LEVELS):
                w("x", l + 1)
                kx = qx = b["x"][l % 2]
            else:
                w("qk", 1)
                kx, qx = b["k"], b["q"]
            for h in range(NH):
                ti, r = divmod(h, hpt)
                rows = slice(dk * r, dk * r + dk)
                if l >= 1:
                    w("cp", (l - 1) * NH + h + 1)
                for c in range(TB):
                    ts = slice(c * P, (c + 1) * P)
                    ins = mm(mx[h][:, ts], kx[rows, ti, ts], qx[rows, ti, ts], start=True, stop=True)
                ins.then_inc(sems["lin_sc"], 1)
        yield 1
        w("kd", 1)
        for ti in range(nt):
            for c in range(TB):
                ins = tr(mx[4 + ti][:, c * P:(c + 1) * P], b["t1"][:, ti, c * P:(c + 1) * P], ident)
        ins.then_inc(sems["lin_kdp"], 1)
        yield 1
        w("kdt", nt)
        for h in range(NH):
            ti, r = divmod(h, hpt)
            rows = slice(dk * r, dk * r + dk)
            for c in range(TB - 1):
                at_ = (ti * (TB - 1) + c) * HD
                ins = mm(mx[4][rows, at_:at_ + HD], b["kdt"][:, ti, c, rows], b["v"][:, c, h * HD:(h + 1) * HD],
                         start=True, stop=True)
        ins.then_inc(sems["lin_kv"], 1)
        yield 1
        w("sh", 1)
        w("qb", 1)
        w("cp", (len(LEVELS) + 1) * NH)
        for h in range(NH):
            ti, r = divmod(h, hpt)
            rows = slice(dk * r, dk * r + dk)
            for c in range(TB):
                o = mx[h // 2][half(h % 2), c * P:(c + 1) * P]
                mm(o, b["v"][:, c, h * HD:(h + 1) * HD], b["a"][:, h, c, :], start=True, stop=False)
                ins = mm(o, b["sh"][rows, c, ti, :], b["t2"][rows, ti, c * P:(c + 1) * P], start=False, stop=True)
        ins.then_inc(sems["lin_op"], 1)
        yield 1
        w("osq", 1)
        for m in range(2):
            ins = mm(mx[2 + m][:, :], oblk, b["u1"][:, m, :], start=True, stop=True)
        ins.then_inc(sems["lin_oss"], 1)
        yield 2

    def blocks(v, n):
        return flat(v).rearrange("p (b h n) -> p b h n", h=2, n=n)

    def linear_act(act, ch, pre, b, nt):
        w = lambda nm, v: lin_wait(act, pre, nm, v)
        for l, n in enumerate(LEVELS):
            if l >= 2:
                yield 4 if l == 2 else 1
            w("d", l + 1)
            d = blocks(b["d"][l % 2], n)
            A.activation(d[:, :, 0, :], d[:, :, 0, :], ACT.Exp, scale=-1.0)
            ch(A.activation(d[:, :, 1, :], d[:, :, 1, :], ACT.Exp), "lin_e")
        for _ in range(3):
            yield 1
        w("db", 1)
        ch(A.activation(flat(b["t1"]), flat(b["t1"]), ACT.Exp, scale=-1.0), "lin_ed")
        ch(A.activation(flat(b["t2"]), flat(b["b"]), ACT.Exp), "lin_eb")
        yield 1
        w("kdp", 1)
        for ti in range(nt):
            ch(A.activation(flat(b["kdt"][:, ti]), mx[4 + ti][:, :], ACT.Copy), "lin_kdt")
        yield 1
        yield 1
        w("op", 1)
        for m in range(2):
            ins = A.activation(b["o"][:, m, :], mx[m][:, :], ACT.Copy)
        ch(ins)
        ch(A.activation(flat(b["u1"]), flat(b["o"]), ACT.Square), "lin_osq")
        yield 1
        w("oss", 1)
        for m in range(2):
            ins = A.activation(b["u2"][:, m, :], mx[2 + m][:, :], ACT.Ln, scale=1.0 / HD, bias=cst(C_EPS))
        ch(ins)
        ch(A.activation(flat(b["u2"]), flat(b["u2"]), ACT.Exp, scale=-0.5), "lin_rs")
        yield 2

    def linear_dve(dve, ch, pre, b, nt, norm, ob):
        w = lambda nm, v: lin_wait(dve, pre, nm, v)
        ch(V.memset(b["a"].rearrange("p a b c -> p (a b c)"), 0.0))
        V.memset(b["sh"][:, 0, :, :], 0.0)
        for m in range(nt):
            ins = V.tensor_tensor_scan(b["b"][:, m, :], rst128, b["f"][:, m, :], 0.0, ALU.mult, ALU.add)
        ch(ins)
        bb = flat(b["b"])

        def diff(l):
            n = LEVELS[l]
            v = bb.rearrange("p (b m) -> p b m", m=2 * n)
            if l >= 2:
                w("x", l - 1)
            ch(V.tensor_tensor(flat(b["d"][l % 2]).rearrange("p (b m) -> p b m", m=2 * n), v,
                               v[:, :, n - 1:n].to_broadcast([P, v.shape[1], 2 * n]), ALU.subtract), "lin_d")

        diff(0)
        for l, n in enumerate(LEVELS):
            if l + 1 < len(LEVELS):
                diff(l + 1)
            w("e", l + 1)
            if l >= 2:
                w("sc", (l - 1) * NH)
            d, x, k, q = (blocks(v, n) for v in (b["d"][l % 2], b["x"][l % 2], b["k"], b["q"]))
            V.tensor_tensor(x[:, :, 0, :], k[:, :, 0, :], d[:, :, 0, :], ALU.mult)
            ch(V.tensor_tensor(x[:, :, 1, :], q[:, :, 1, :], d[:, :, 1, :], ALU.mult), "lin_x")
            if l:
                copy_scores(dve, ch, pre, b, l - 1)
            yield 1 if l else 4
        copy_scores(dve, ch, pre, b, len(LEVELS) - 1)
        yield 1
        v = bb.rearrange("p (b m) -> p b m", m=P)
        ch(V.tensor_tensor(flat(b["t1"]).rearrange("p (b m) -> p b m", m=P), v,
                           v[:, :, P - 1:P].to_broadcast([P, v.shape[1], P]), ALU.subtract), "lin_db")
        w("ed", 1)
        ch(V.tensor_tensor(flat(b["t1"]), flat(b["t1"]), flat(b["k"]), ALU.mult), "lin_kd")
        yield 1
        copy_scores(dve, ch, pre, b, len(LEVELS))
        w("eb", 1)
        ch(V.tensor_copy(b["ebl"], b["t2"].rearrange("p m (c t) -> p m c t", t=P)[:, :, :, P - 1]))
        ch(V.tensor_tensor(flat(b["t2"]), flat(b["t2"]), flat(b["q"]), ALU.mult), "lin_qb")
        yield 1
        w("kv", 1)
        for c in range(TB - 1):
            for ti in range(nt):
                at_ = (ti * (TB - 1) + c) * HD
                ins = V.scalar_tensor_tensor(b["sh"][:, c + 1, ti, :], b["sh"][:, c, ti, :], b["ebl"][:, ti, c:c + 1],
                                             mx[4][:, at_:at_ + HD], ALU.mult, ALU.add)
            ch(ins, "lin_sh" if c == TB - 2 else None)
        yield 1
        yield 1
        w("rs", 1)
        ch(V.tensor_tensor(flat(b["o"]), flat(b["o"]), flat(b["u2"]), ALU.mult))
        for m in range(2):
            ins = V.scalar_tensor_tensor(OB[:, ob + m, :], b["o"][:, m, :], pa(norm, m), b["g"][:, m, :], ALU.mult, ALU.mult)
        ch(ins, "lin_done")
        yield 2

    def copy_scores(dve, ch, pre, b, l):
        for h in range(NH):
            lin_wait(dve, pre, "sc", l * NH + h + 1)
            ch(V.copy_predicated(b["a"][:, h, :, :], bc(lmask[:, l, :], TB).bitcast(U32),
                                 mx[h][:, :].rearrange("p (c t) -> p c t", c=TB)), "lin_cp")

    def store_tile(act, ch, name):
        i = STORE_AT[name]
        width = GRANK if name[0] == "gl_a" else P
        take_act(act, name)
        if i >= len(STG):
            act.wait_ge(sems[f"z_out{i % len(STG)}"], 16 * (i // len(STG)))
        ch(A.activation(STG[i % len(STG)][0:width, :], pj[TILE_AT[name] % NPJ][0:width, :], ACT.Copy), "out_act")
        act.dma_start(z_dram[i][0:width, :], STG[i % len(STG)][0:width, :]).then_inc(sems[f"z_out{i % len(STG)}"], 16)

    def load_tile(act, name, dst, sem):
        i = STORE_AT[name]
        width = GRANK if name[0] == "gl_a" else P
        act.wait_ge(sems[f"z_out{i % len(STG)}"], 16 * (i // len(STG) + 1))
        act.dma_start(dst[0:width], z_dram[i][0:width, :]).then_inc(sems[sem], 16)

    DONE = {2: ("rw_done", 1), 0: ("lin_done", 1), 1: ("lin_done", 2), 3: ("at_done", 2)}

    def gl_pe(pe):
        yield 2
        pe.wait_ge(sems["z_in"], 16 * 15)
        mm(mx[5][:, :], AW2[0:GRANK, :], GB["al"][0:GRANK, :], start=True, stop=True).then_inc(sems["gl_u"], 1)
        yield from linear_pe(pe, "gl", GB, 1, GDK)

    def hg_act(act, ch):
        b = HB
        w = lambda nm, v: act.wait_ge(sems["hg_" + nm], v)
        act.wait_ge(sems["rw_done"], 1)
        for m in range(2):
            load_tile(act, ("hg_q", m), b["q"][:, m, :], "z_in")
            load_tile(act, ("hg_f", m), b["f"][:, m, :], "z_in")
            load_tile(act, ("hg_g", m), b["g"][:, m, :], "z_in")
            load_tile(act, ("hg_i", m), flat(b["v"][:, 2 * m:2 * m + 2, :]), "z_in")
        act.wait_ge(sems["z_in"], 16 * 8)
        sig_act(ch, flat(b["t1"]), flat(b["t2"]), flat(b["q"]), name="hg_s1")
        w("s2", 1)
        ch(A.activation(flat(b["t1"]), flat(b["t1"]), ACT.Exp), "hg_s3")
        sig_act(ch, flat(b["u1"]), flat(b["u2"]), flat(b["g"]), name="hg_g1")
        w("g2", 1)
        ch(A.activation(flat(b["g"]), flat(b["u1"]), ACT.Exp), "hg_g3")
        w("s4", 1)
        sig_act(ch, flat(b["t1"]), flat(b["t2"]), flat(b["f"]), name="hg_f1")
        w("f2", 1)
        ch(A.activation(flat(b["t2"]), flat(b["t2"]), ACT.Exp), "hg_f3")
        w("f4", 1)
        A.activation(flat(b["t2"]), flat(b["t2"]), ACT.Ln, bias=cst(C_ONE), scale=1.0)
        ch(A.activation(flat(b["t3"]), flat(b["t3"]), ACT.Ln, scale=1e-9), "hg_f5")
        ch(A.activation(flat(b["k"]), flat(b["k"]), ACT.Exp), "hg_k1")
        yield from linear_act(act, ch, "hg", b, 2)

    def hg_dve(dve, ch):
        b = HB
        w = lambda nm, v: dve.wait_ge(sems["hg_" + nm], v)
        w("s1", 1)
        sig_dve(ch, flat(b["t1"]), flat(b["t1"]), flat(b["t2"]), "hg_s2")
        w("s3", 1)
        ch(V.tensor_tensor(flat(b["q"]), flat(b["q"]), flat(b["t1"]), ALU.mult), "hg_s4")
        w("g1", 1)
        sig_dve(ch, flat(b["u1"]), flat(b["u1"]), flat(b["u2"]), "hg_g2")
        w("f1", 1)
        sig_dve(ch, flat(b["t1"]), flat(b["t1"]), flat(b["t2"]))
        ch(V.tensor_tensor(flat(b["k"]), flat(b["t1"]), flat(b["f"]), ALU.subtract))
        ch(V.tensor_scalar(flat(b["t2"]), flat(b["f"]), -1.0, 60.0, ALU.mult, ALU.min), "hg_f2")
        w("f3", 1)
        for m in range(2):
            ins = V.tensor_scalar(b["t2"][:, m, :], b["t2"][:, m, :], LB[:, m:m + 1], None, ALU.mult)
        ch(ins)
        V.tensor_scalar_max(flat(b["t3"]), flat(b["t2"]), 1e9)
        ch(V.tensor_scalar_min(flat(b["x"][0]), flat(b["t2"]), 1e9))
        ch(V.tensor_copy(flat(b["t2"]), flat(b["x"][0])), "hg_f4")
        w("f5", 1)
        ch(V.tensor_tensor(flat(b["f"]), flat(b["t1"]), flat(b["t2"]), ALU.add))
        ch(V.tensor_tensor(flat(b["f"]), flat(b["f"]), flat(b["t3"]), ALU.add))
        w("k1", 1)
        for m in range(2):
            ins = V.tensor_scalar(b["k"][:, m, :], b["k"][:, m, :], OMLB[:, m:m + 1], None, ALU.mult)
        ch(ins, "lin_qk")
        yield from linear_dve(dve, ch, "hg", b, 2, "hg_norm", 0)

    def gl_act(act, ch):
        b = GB
        w = lambda nm, v: act.wait_ge(sems["gl_" + nm], v)
        act.wait_ge(sems["lin_done"], 1)
        load_tile(act, ("gl_a", 0), b["al"], "z_in")
        load_tile(act, ("gl_qk", 0), b["q"][:, 0, :], "z_in")
        load_tile(act, ("gl_qk", 1), b["k"][:, 0, :], "z_in")
        for m in range(2):
            load_tile(act, ("gl_g", m), b["g"][:, m, :], "z_in")
            load_tile(act, ("gl_v", m), flat(b["v"][:, 2 * m:2 * m + 2, :]), "z_in")
        yield 2
        act.wait_ge(sems["z_in"], 16 * 15)
        sig_act(ch, flat(b["u1"]), flat(b["u2"]), flat(b["g"]), name="gl_g1")
        w("g2", 1)
        ch(A.activation(flat(b["u1"]), flat(b["u1"]), ACT.Exp), "gl_g3")
        w("u", 1)
        sig_act(ch, flat(b["t1"]), flat(b["t2"]), mx[5][:, :], bias=pa("gla_b"), name="gl_f1")
        yield from linear_act(act, ch, "gl", b, 1)

    def gl_dve(dve, ch):
        b = GB
        w = lambda nm, v: dve.wait_ge(sems["gl_" + nm], v)
        yield 2
        w("g1", 1)
        sig_dve(ch, flat(b["u1"]), flat(b["u1"]), flat(b["u2"]), "gl_g2")
        w("g3", 1)
        ch(V.tensor_tensor(flat(b["g"]), flat(b["g"]), flat(b["u1"]), ALU.mult))
        w("f1", 1)
        sig_dve(ch, flat(b["f"]), flat(b["t1"]), flat(b["t2"]))
        V.tensor_scalar_mul(flat(b["q"]), flat(b["q"]), float(GDK) ** -0.5)
        ch(V.tensor_scalar_mul(flat(b["f"]), flat(b["f"]), 1.0 / TAU), "lin_qk")
        yield from linear_dve(dve, ch, "gl", b, 1, "gla_norm", 2)

    AT_STEPS = [(pr, hh, blk) for pr in range(2) for hh in range(2) for blk in range(TB)]
    ROPE = [(nm, g, m) for g in range(N_DIL) for nm in ("at_q", "at_k") for m in range(2)]

    def rope_loaded(n):
        return ("at_z", 16 * NZ) if n < NZ else (f"at_z{n // 2}", 32)

    def attention_pe(pe):
        w = lambda nm, v: pe.wait_ge(*sems.at(nm, v))
        for n in range(len(ROPE)):
            w(*rope_loaded(n))
            if n >= 2:
                w("at_rope", n - 1)
            mm(mx[n % 2][:, :], rot, TZ[n % NZ], start=True, stop=True).then_inc(sems["at_rot"], 1)
            if n % 2:
                yield 1
        w("at_rope", len(ROPE))

        def scores(n):
            pr, hh, blk = AT_STEPS[n]
            bs = slice(blk * P, (blk + 1) * P)
            if n >= 2:
                w("at_sm", n - 1)
            s = mx[5 * (n % 2)]
            q = lambda g: QR[half(hh), 2 * g + pr, bs]
            if blk:
                mm(s[:, 0:256], q(0), KR[half(hh), pr, (blk - 1) * P:(blk + 1) * P], start=True, stop=True)
            else:
                mm(s[:, 128:256], q(0), KR[half(hh), pr, bs], start=True, stop=True)
            mm(s[:, 256:384], q(1), KR[half(hh), 2 + pr, bs], start=True, stop=True)
            mm(s[:, 384:512], q(2), KR[half(hh), 4 + pr, bs], start=True, stop=True).then_inc(sems["at_s"], 1)

        scores(0)
        for n, (pr, hh, blk) in enumerate(AT_STEPS):
            bs = slice(blk * P, (blk + 1) * P)
            if n + 1 < len(AT_STEPS):
                scores(n + 1)
            yield 1
            w("at_p", n + 1)
            for j in range(0 if blk else 1, 4):
                ins = tr(mx[1][:, j * P:(j + 1) * P], PE_[:, n % 2, j * P:(j + 1) * P], ident)
            ins.then_inc(sems["at_pt"], 1)
            yield 1
            w("at_ptc", n + 1)
            if n == 0:
                w("at_va", 16 * 6)
            if n == 8:
                w("at_num", 1)
            vs = slice((2 * pr + hh) * HD, (2 * pr + hh + 1) * HD)
            pt = PT[:, n % 2, :]
            for g in range(N_DIL):
                o = mx[2 + g][half(hh), bs]
                if g == 0 and blk:
                    mm(o, VA[:, blk - 1, vs], pt[:, 0:P], start=True, stop=False)
                ins = mm(o, VA[:, g * TB + blk, vs], pt[:, (1 + g) * P:(2 + g) * P], start=not (g == 0 and blk),
                         stop=True)
            ins.then_inc(sems["at_n"], 1)
            if n % 8 != 7:
                continue
            w("at_st", pr + 1)
            tr(mx[5][0:48, 0:P], ST[:, pr, :], ident).then_inc(sems["at_str"], 1)
            yield 1
            w("at_strc", pr + 1)
            for q in range(2):
                for g in range(N_DIL):
                    k = q * N_DIL + g
                    if k:
                        w("at_bca" if k <= 3 else "at_bcd", pr * 3 + (k if k <= 3 else k - 3))
                    for hh2 in range(2):
                        for b2 in range(TB):
                            row = ((g * 2 + q) * 2 + hh2) * TB + b2
                            ins = mm(mx[5][half(hh2), b2 * P:(b2 + 1) * P],
                                     ident[0:48, row:row + 1].to_broadcast([48, HD]), STR[0:48, :],
                                     start=True, stop=True)
                    ins.then_inc(sems["at_bcp"], 1)
                    if k == 2:
                        yield 1
            yield 1
            w("at_bcd", pr * 3 + 3)

    def nat(v, g):
        if g == 0:
            return v
        return v.rearrange("p (r j) -> p j r", r=ORDER[g])

    def perm(v, g):
        if g == 0:
            return v
        return v.rearrange("p (j r) -> p j r", r=ORDER[g])

    def at_act(act, ch):
        w = lambda nm, v: act.wait_ge(*sems.at(nm, v))
        w("lin_done", 2)
        for n in range(NZ):
            load_tile(act, ROPE[n], TZ[n], "at_z")
        for g in range(N_DIL):
            for m in range(2):
                load_tile(act, ("at_v", g, m), flat(VA[:, g * TB + 2 * m:g * TB + 2 * m + 2, :]), "at_va")
        for n in range(0, len(ROPE), 2):
            if n + NZ < len(ROPE):
                w("at_rope", n + 2)
                for j in range(2):
                    load_tile(act, ROPE[n + NZ + j], TZ[n + j], rope_loaded(n + NZ)[0])
            yield 1
        scale = float(HD) ** -0.5
        for n, (pr, hh, blk) in enumerate(AT_STEPS):
            w("at_sm", n + 1)
            if n >= 2:
                w("at_pt", n - 1)
            x, e, st = SMX[:, n % 2, :], PE_[:, n % 2, :], ST[:, pr, :]
            c = hh * TB + blk
            lo = 0 if blk else P
            for g, (a0, a1) in enumerate(((lo, 256), (256, 384), (384, 512))):
                col = (g * 2 + 1) * 2 * TB + c
                ins = A.activation(e[:, a0:a1], x[:, a0:a1], ACT.Exp, bias=NM[:, n % 2, g:g + 1], scale=scale,
                                   accum_out=st[:, col:col + 1])
            ch(ins, "at_p")
            yield 1
            w("at_pt", n + 1)
            ch(A.activation(PT[:, n % 2, lo:], mx[1][:, lo:], ACT.Copy), "at_ptc")
            yield 1
            if n % 8 != 7:
                continue
            w("at_str", pr + 1)
            ch(A.activation(STR[0:48, :], mx[5][0:48, 0:P], ACT.Copy), "at_strc")
            yield 1
            for g in range(N_DIL):
                w("at_bcp", pr * 6 + g + 1)
                ch(A.activation(perm(MN[:, g, :], g), nat(mx[5][:, :], g), ACT.Copy), "at_bca")
            w("at_c1", pr + 1)
            ch(A.activation(flat(CN), flat(CN), ACT.Exp, scale=scale), "at_c2")
            yield 1
            w("at_den", pr + 1)
            ch(A.activation(TP, DN, ACT.Ln))
            ch(A.activation(TP, TP, ACT.Exp, scale=-1.0), "at_rd")
            yield 1
        w("at_done", 2)
        w("x_out_d", 16)
        act.dma_start(XR, x_dram).then_inc(sems["x_in_d"], 16)

    def at_dve(dve, ch):
        w = lambda nm, v: dve.wait_ge(*sems.at(nm, v))
        for n, (nm, g, m) in enumerate(ROPE):
            dst = (QR if nm == "at_q" else KR)[:, 2 * g + m, :]
            w("at_rot", n + 1)
            V.tensor_tensor(TC, TZ[n % NZ], cosT, ALU.mult)
            ch(V.tensor_tensor(TR, mx[n % 2][:, :], sinT, ALU.mult))
            ch(V.tensor_tensor(nat(dst, g), perm(TC, g), perm(TR, g), ALU.add), "at_rope")
            if n % 2:
                yield 1
        scale = float(HD) ** -0.5

        def maxima(n):
            pr, hh, blk = AT_STEPS[n]
            lo = 0 if blk else P
            c = hh * TB + blk
            x, s, nm = SMX[:, n % 2, :], mx[5 * (n % 2)], NM[:, n % 2, :]
            w("at_s", n + 1)
            if n >= 2:
                w("at_p", n - 1)
            ch(V.tensor_tensor(x[:, lo:], s[:, lo:], amask[:, lo:], ALU.add))
            st = ST[:, pr, :].rearrange("p (g q c) -> p g q c", g=3, q=2)
            V.tensor_reduce(st[:, 0, 0, c:c + 1], x[:, lo:256], AX.X, ALU.max)
            ch(V.tensor_reduce(st[:, 1:3, 0, c], x[:, 256:512].rearrange("p (g t) -> p g t", g=2), AX.X, ALU.max))
            ch(V.tensor_scalar_mul(nm[:, 0:3], st[:, :, 0, c], -scale), "at_sm")

        maxima(0)
        for n, (pr, hh, blk) in enumerate(AT_STEPS):
            if n + 1 < len(AT_STEPS):
                maxima(n + 1)
            yield 1
            yield 1
            if n % 8 != 7:
                continue
            w("at_p", n + 1)
            w("at_n", n + 1)
            dve.sem_inc(sems["at_st"], 1)
            yield 1
            w("at_bca", pr * 3 + 3)
            ch(V.tensor_tensor(MG, MN[:, 0, :], MN[:, 1, :], ALU.max))
            ch(V.tensor_tensor(MG, MG, MN[:, 2, :], ALU.max))
            ch(V.tensor_tensor(CN, MN, bc(MG, 3), ALU.subtract), "at_c1")
            yield 1
            w("at_c2", pr + 1)
            for g in range(N_DIL):
                w("at_bcp", pr * 6 + 4 + g)
                o = DN if g == 0 else TC
                ch(V.tensor_tensor(perm(o, g), nat(mx[5][:, :], g), perm(CN[:, g, :], g), ALU.mult), "at_bcd")
                if g:
                    ch(V.tensor_tensor(DN, DN, TC, ALU.add), "at_den" if g == 2 else None)
            for g in range(N_DIL):
                o = NU if g == 0 else TC
                ch(V.tensor_tensor(perm(o, g), nat(mx[2 + g][:, :], g), perm(CN[:, g, :], g), ALU.mult),
                   "at_num" if g == 2 else None)
                if g:
                    ch(V.tensor_tensor(NU, NU, TC, ALU.add))
            w("at_rd", pr + 1)
            ch(V.tensor_tensor(OB[:, 6 + pr, :], NU, TP, ALU.mult), "at_done")
            yield 1

    with nc.Fori(0, L) as li:
        with nc.Block() as block:
            def load_parameters(q):
                def row(half, r, src, n):
                    q.dma_start(ROW[r:r + n, half, :], src.rearrange("(a p) -> a p", p=P)).then_inc(sems["par"], 16)
                for nm, src in (("norm_mix", "norm_mix_w"), ("norm_ffn", "norm_ffn_w"), ("hg_norm", "hg_norm_w"),
                                ("gla_norm", "gla_norm_w"), ("gla_b", "gla_a_b"), ("w0", "rw_w0"), ("a0", "rw_a0"),
                                ("k_k", "rw_k_k"), ("k_a", "rw_k_a"), ("r_k", "rw_r_k"), ("ln_w", "rw_ln_w"),
                                ("ln_b", "rw_ln_b")):
                    n = t[src].shape[1] // P
                    row(0, PA[nm], t[src][li], n)
                row(0, PA["v0"], t["rw_v0"][0], 2)
                mu = t["rw_mu"][li]
                row(0, PA["mu_r"], mu[0:W], 2)
                row(0, PA["mu_k"], mu[W + 32:2 * W + 32], 2)
                row(0, PA["mu_v"], mu[2 * W + 32:3 * W + 32], 2)
                r = PA["mu_sm"]
                one = lambda v: v.rearrange("(a p) -> a p", a=1)
                q.dma_start(ROW[r:r + 1, 0, 0:32], one(mu[W:W + 32])).then_inc(sems["par"], 16)
                q.dma_start(ROW[r:r + 1, 0, 32:64], one(mu[3 * W + 32:3 * W + 64])).then_inc(sems["par"], 16)
                q.dma_start(ROW[r:r + 1, 0, 64:128], one(mu[3 * W + 64:3 * W + 128])).then_inc(sems["par"], 16)
                for l in range(L):
                    row(0, PA["lb"] + 2 * l, t["hg_lb_table"][l], 2)
                row(0, PA["final"], t["norm_final_w"], 8)
                for j in range(3):
                    row(1, PB["conv_w"] + j * FT, t["ffn_conv_w"][li, j], FT)
                row(1, PB["conv_b"], t["ffn_conv_b"][li], FT)
                q.dma_start(LORA[0:32, :], t["rw_w2"][li]).then_inc(sems["par2"], 16)
                q.dma_start(LORA[32:64, :], t["rw_a2"][li]).then_inc(sems["par2"], 16)
                q.dma_start(LORA[64:128, :], t["rw_g2"][li]).then_inc(sems["par2"], 16)
                q.dma_start(V1[:, :, :], t["rw_v1"][0].rearrange("(k p) n -> p k n", p=P)).then_inc(sems["par2"], 16)
                q.dma_start(V2[0:32, :], t["rw_v2"][0]).then_inc(sems["par2"], 16)
                q.dma_start(AW2[0:GRANK, :], t["gla_a_w2"][li]).then_inc(sems["par2"], 16)
                q.dma_start(FLAG[:, :], t["flags"][li]).then_inc(sems["par2"], 16)

            NPAR = 12 + 1 + 3 + 3 + 2 + 1 + 3 + 1
            NPAR2 = 7

            @block.sync
            def _(sp):
                views = {"w_in": t["w_in"][li], "w_branch": t["w_branch"][li].rearrange("n w d -> (n w) d"),
                         "w_out": t["w_out"][li], "ffn_up": t["ffn_w_up"][li], "ffn_down": t["ffn_w_down"][li]}
                names = list(STRIP_AT)
                sp.dma_start(x_dram, X[:, :, :]).then_inc(sems["x_out_d"], 16)
                for j, pieces in enumerate(STRIPS):
                    if j >= RING:
                        sp.wait_ge(sems["tile"], last_tile(names[j - RING]) + 1)
                    for at_, kind, col, width, k0, nk in pieces:
                        src = views[kind].rearrange("(k p) n -> p k n", p=P)[:, k0:k0 + nk, col:col + width]
                        sp.dma_start(RG[j % RING][:, 0:nk, at_:at_ + width], src).then_inc(sems[f"ring{j % RING}"], 16)
                    if names[j][0] == "gate":
                        _, d, n = names[j]
                        i = GATE_ITEMS.index((n, d))
                        if i >= 2:
                            n2, d2 = GATE_ITEMS[i - 2]
                            sp.wait_ge(sems["tile"], TILE_AT[("br", d2, n2, 1)] + 1)
                        src = t["w_branch"][li][n].rearrange("(k p) n -> p k n", p=P)[:, :, d * 2 * P:(d + 1) * 2 * P]
                        sp.dma_start(BRG[i % 2][:, :, :], src).then_inc(sems[f"brring{i % 2}"], 16)

            need = []
            cnt = [0] * RING
            for j, pieces in enumerate(STRIPS):
                cnt[j % RING] += 16 * len(pieces)
                need.append(cnt[j % RING])

            @block.tensor
            def _(pe):
                mm = nc.tensor.matmul

                def strip(name):
                    j = STRIP_AT[name]
                    pe.wait_ge(sems[f"ring{j % RING}"], need[j])
                    return RG[j % RING]

                def begin(name):
                    i = TILE_AT[name]
                    if i >= NPJ:
                        e = TILES[i - NPJ][1]
                        pe.wait_ge(sems["out_act" if e == "a" else "out_dve"], taken(i - NPJ))
                    return pj[i % NPJ]

                def fm(name, st, col, width=P, rhs=H, r0=0, nk=KT):
                    b = begin(name)
                    for k in range(nk):
                        ins = mm(b[0:width, :], st[:, k, col:col + width], rhs[:, r0 + k, :], start=k == 0,
                                 stop=k == nk - 1)
                        if k == nk - 1:
                            ins.then_inc(sems["tile"], 1)
                        if k % 4 == 3 or k == nk - 1:
                            yield

                def tm(name, st, g=0):
                    for m in range(2):
                        b = begin((*name, m))
                        for j in range(2):
                            tb = 2 * m + j
                            for k in range(KT):
                                tok = H[:, k, :].rearrange("p (j r) -> p r j", r=4)[:, tb, :] if ORDER[g] == 4 else \
                                    H[:, k, tb * P:(tb + 1) * P]
                                ins = mm(b[:, j * 256:(j + 1) * 256], tok, st[:, k, :], start=k == 0, stop=k == KT - 1)
                            if j:
                                ins.then_inc(sems["tile"], 1)
                            yield

                def stored():
                    for nm in ("hg_q", "hg_f", "hg_i", "hg_g", "gl_qk", "gl_v", "gl_g"):
                        st = strip(nm)
                        if nm in ("hg_i", "gl_v"):
                            yield from tm((nm,), st)
                        else:
                            for m in range(2):
                                yield from fm((nm, m), st, m * P)
                    yield from fm(("gl_a", 0), strip("gl_a"), 0, GRANK)
                    for g in range(N_DIL):
                        for nm in ("at_q", "at_k"):
                            st = strip((nm, g))
                            for m in range(2):
                                yield from fm((nm, g, m), st, m * P)
                        yield from tm(("at_v", g), strip(("at_v", g)), g)

                def merge(n):
                    pe.wait_ge(sems[DONE[n][0]], DONE[n][1])
                    for d in range(D // (2 * P)):
                        i = GATE_ITEMS.index((n, d))
                        sg = strip(("gate", d, n))
                        for m in range(2):
                            yield from fm(("gate", d, n, m), sg, m * P)
                            pe.wait_ge(sems[f"brring{i % 2}"], 16 * (i // 2 + 1))
                            yield from fm(("br", d, n, m), BRG[i % 2], m * P, rhs=OB, r0=2 * n, nk=2)

                pe.wait_ge(sems["par"], 16 * NPAR)
                nc.tensor.transpose(mx[0][:, 0:P], ROW[:, 0, :], ident)
                nc.tensor.transpose(mx[0][:, P:2 * P], ROW[:, 1, :], ident).then_inc(sems["par_t"], 1)
                pe.wait_ge(sems["par_c"], 1)
                norm_pe(pe, "n1")
                pe.wait_ge(sems["n1_h"], 1)
                pe.wait_ge(sems["par2"], 16 * NPAR2)

                for nm in ("rw_r", "rw_k", "rw_v"):
                    st = strip(nm)
                    for m in range(2):
                        run(fm((nm, m), st, m * P))
                run(fm(("rw_sm", 0), strip("rw_sm"), 0))
                filler = stored()
                interleave(rwkv_pe(pe), filler)
                run(filler)
                rest = merge(2)
                interleave(linear_pe(pe, "hg", HB, 2, HD), rest)
                rest = chain(rest, merge(0))
                interleave(gl_pe(pe), rest)
                rest = chain(rest, merge(1))
                interleave(attention_pe(pe), rest)
                run(rest)
                run(merge(3))
                pe.wait_ge(sems["mt"], KT)
                for d in range(D // P):
                    run(fm(("out", d), strip(("out", d // 2)), (d % 2) * P, rhs=MT))
                norm_pe(pe, "n2")
                pe.wait_ge(sems["n2_h"], 1)
                for c in range(FT // 2):
                    su, sg = strip(("up", c)), strip(("gf", c))
                    for m in range(2):
                        run(fm(("up", 2 * c + m), su, m * P))
                        run(fm(("gf", 2 * c + m), sg, m * P))
                for d2 in range(D // (2 * P)):
                    ss = [strip(("down", d2, j)) for j in range(3)]
                    for m in range(2):
                        b = begin(("down", 2 * d2 + m))
                        for k in range(FT):
                            if d2 == 0 and m == 0:
                                pe.wait_ge(sems["out_dve"], taken(TILE_AT[("gf", k)]))
                            ins = mm(b[:, :], ss[k // KT][:, k % KT, m * P:(m + 1) * P], HFF[:, k, :], start=k == 0,
                                     stop=k == FT - 1)
                        ins.then_inc(sems["tile"], 1)

            @block.scalar
            def _(act):
                ch = Chain(act, sems, "act_own")
                load_parameters(act)
                act.wait_ge(sems["lb1"], 1)
                ch(A.activation(LBT[:, 2:6], LBT[:, 2:6], ACT.Exp), "lb2")
                norm_act(act, ch, "n1")

                def stored():
                    for name in STORED:
                        yield
                        store_tile(act, ch, name)
                        yield

                def merge(n):
                    for d in range(D // (2 * P)):
                        for m in range(2):
                            i = GATE_ITEMS.index((n, d)) * 2 + m
                            yield
                            take_act(act, ("gate", d, n, m))
                            if i >= 4:
                                act.wait_ge(sems["out_dve"], taken(TILE_AT[("br", d, n, m)]) - 4)
                            sigmoid(ch, SG[i % 4], pj[TILE_AT[("gate", d, n, m)] % NPJ][:, :], "out_act")
                            yield
                            yield

                filler = stored()
                interleave(rwkv_act(act, ch), filler)
                run(filler)
                rest = merge(2)
                interleave(hg_act(act, ch), rest)
                rest = chain(rest, merge(0))
                interleave(gl_act(act, ch), rest)
                rest = chain(rest, merge(1))
                interleave(at_act(act, ch), rest)
                run(rest)
                run(merge(3))
                act.wait_ge(sems["x_mid"], 1)
                norm_act(act, ch, "n2", XR)
                for c in range(FT + 1):
                    if c < FT:
                        take_act(act, ("up", c))
                        if c == 0:
                            act.wait_ge(sems["uppad"], 1)
                        if c >= 2:
                            act.wait_ge(sems["conv"], c - 1)
                        ch(A.activation(UP[c % 2][:, 2:], pj[TILE_AT[("up", c)] % NPJ][:, :], ACT.Copy), "out_act")
                    if c >= 1:
                        act.wait_ge(sems["conv"], c)
                        ch(A.activation(FS[(c - 1) % 2], FC[(c - 1) % 3], ACT.Sigmoid), "fsig")

            @block.vector
            def _(dve):
                ch = Chain(dve, sems, "dve_own")
                dve.wait_ge(sems["par_t"], 1)
                V.tensor_copy(PC_[:, 0:NPA], mx[0][:, 0:NPA])
                ch(V.tensor_copy(PC_[:, NPA:NPA + NPB], mx[0][:, P:P + NPB]), "par_c")
                dve.wait_ge(sems["par2"], 16 * NPAR2)
                t0, t1 = (PC_[:, PA["lb"] + 2 * l:PA["lb"] + 2 * l + 2] for l in range(2))
                ch(V.tensor_tensor(LBT[:, 0:2], t0, t1, ALU.max))
                V.tensor_tensor(LBT[:, 2:4], t0, LBT[:, 0:2], ALU.subtract)
                ch(V.tensor_tensor(LBT[:, 4:6], t1, LBT[:, 0:2], ALU.subtract), "lb1")
                dve.wait_ge(sems["lb2"], 1)
                ch(V.tensor_tensor(LBT[:, 6:8], LBT[:, 2:4], LBT[:, 4:6], ALU.add))
                ch(V.reciprocal(LBT[:, 6:8], LBT[:, 6:8]))
                V.tensor_tensor(LBT[:, 8:10], LBT[:, 2:4], LBT[:, 6:8], ALU.mult)
                ch(V.tensor_tensor(LBT[:, 10:12], LBT[:, 4:6], LBT[:, 6:8], ALU.mult))
                ch(V.scalar_tensor_tensor(LBT[:, 12:14], LBT[:, 10:12], FLAG[:, 0:1], LBT[:, 8:10], ALU.mult, ALU.add))
                ch(V.tensor_tensor(LB[:, :], LBT[:, 12:14], LBT[:, 8:10], ALU.subtract))
                ch(V.tensor_scalar(OMLB[:, :], LB[:, :], -1.0, 1.0, ALU.mult, ALU.add))
                norm_dve(dve, "n1", "norm_mix")

                def tile(name):
                    dve.wait_ge(sems["tile"], TILE_AT[name] + 1)
                    return pj[TILE_AT[name] % NPJ][:, :]

                def merge(n):
                    for d in range(D // (2 * P)):
                        for m in range(2):
                            i = GATE_ITEMS.index((n, d)) * 2 + m
                            yield
                            yield
                            if i == 0:
                                dve.wait_ge(sems["x_out_d"], 16)
                            dve.wait_ge(sems["out_act"], taken(TILE_AT[("gate", d, n, m)]))
                            b = tile(("br", d, n, m))
                            mt = MT[:, 2 * d + m, :]
                            o = mt if n == BR_ORDER[0] else MTMP[i % 2]
                            ch(V.tensor_tensor(o, b, SG[i % 4], ALU.mult), "out_dve")
                            if n != BR_ORDER[0]:
                                ch(V.tensor_tensor(mt, mt, o, ALU.add), "mt" if n == BR_ORDER[-1] else None)
                            yield

                run(rwkv_dve(dve, ch))
                rest = merge(2)
                interleave(hg_dve(dve, ch), rest)
                rest = chain(rest, merge(0))
                interleave(gl_dve(dve, ch), rest)
                rest = chain(rest, merge(1))
                interleave(at_dve(dve, ch), rest)
                run(rest)
                run(merge(3))
                dve.wait_ge(sems["x_in_d"], 16)
                for d in range(D // P):
                    ch(V.tensor_tensor(XR[:, d, :], tile(("out", d)), XR[:, d, :], ALU.add), "out_dve")
                dve.sem_inc(sems["x_mid"], 1)
                norm_dve(dve, "n2", "norm_ffn", XR)
                for u in range(2):
                    ins = V.memset(UP[u][:, 0:2], 0.0)
                ch(ins, "uppad")
                for c in range(FT):
                    u, f = UP[c % 2], FC[c % 3]
                    dve.wait_ge(sems["out_act"], taken(TILE_AT[("up", c)]))
                    ch(V.tensor_scalar(f, u[:, 2:], pb_("conv_w", c), pb_("conv_b", c), ALU.mult, ALU.add))
                    ch(V.scalar_tensor_tensor(f, u[:, 1:S + 1], pb_("conv_w", FT + c), f, ALU.mult, ALU.add))
                    ch(V.scalar_tensor_tensor(f, u[:, 0:S], pb_("conv_w", 2 * FT + c), f, ALU.mult, ALU.add), "conv")
                    dve.wait_ge(sems["fsig"], c + 1)
                    ch(V.tensor_tensor(FS[c % 2], FS[c % 2], f, ALU.mult))
                    ch(V.tensor_tensor(HFF[:, c, :], tile(("gf", c)), FS[c % 2], ALU.mult), "out_dve")
                for d in range(D // P):
                    ch(V.tensor_tensor(X[:, d, :], tile(("down", d)), XR[:, d, :], ALU.add), "out_dve")

        clear()

    with nc.Block() as block:
        @block.scalar
        def _(act):
            ch = Chain(act, sems, "act_own")
            norm_act(act, ch, "n1")

        @block.vector
        def _(dve):
            norm_dve(dve, "n1", "final")
            for i in range(2 * TB):
                dve.wait_ge(sems["x_t"], i + 1)
                V.tensor_copy(arena[:, i * 512:(i + 1) * 512], pj[i % 2][:, :]).then_inc(sems["x_out"], 1)

        @block.tensor
        def _(pe):
            norm_pe(pe, "n1")
            pe.wait_ge(sems["n1_h"], 1)
            for i in range(2 * TB):
                tb, hf = divmod(i, 2)
                if i >= 2:
                    pe.wait_ge(sems["x_out"], i - 1)
                for k in range(4):
                    ins = tr(pj[i % 2][:, k * P:(k + 1) * P], H[:, 4 * hf + k, tb * P:(tb + 1) * P], ident)
                ins.then_inc(sems["x_t"], 1)

        @block.sync
        def _(sp):
            for tb in range(TB):
                sp.wait_ge(sems["x_out"], 2 * tb + 2)
                sp.dma_start(out[0, tb * P:(tb + 1) * P, :], arena[:, tb * D:(tb + 1) * D]).then_inc(sems["x_in"], 16)
            sp.wait_ge(sems["x_in"], 16 * TB)


CONSTS = (("ident", P), ("ones", P), ("oblk", P), ("rot", P), ("lmask", 8 * P), ("amask", 4 * P), ("rmask", 4 * P),
          ("cos", S), ("sin", S), ("rst64", S), ("rst128", S))


def constants():
    i = np.arange(P)
    row, col = i[:, None], i[None, :]
    c = {"ident": row == col, "ones": np.ones((P, P)), "oblk": row // HD == col // HD}
    hd = HD // 2
    c["rot"] = (row - hd == col) * (row % HD >= hd) * -1.0 + (row + hd == col) * (row % HD < hd) * 1.0
    lv = [(row // (2 * n) == col // (2 * n)) & (row // n % 2 == 0) & (col // n % 2 == 1) for n in LEVELS]
    c["lmask"] = np.concatenate(lv + [row == col], 1)
    neg = lambda ok: np.where(ok, 0.0, -BIG)
    c["amask"] = np.concatenate([neg(col >= row), neg(col <= row), neg(col <= row),
                                 neg(((row - col) % (DILS[2] // DILS[1]) == 0) & (col <= row))], 1)
    same = row // RC == col // RC
    strict, incl = same & (row < col), same & (row <= col)
    c["rmask"] = np.concatenate([strict, incl, strict, incl], 1)
    inv = 10000.0 ** (-np.arange(hd, dtype=np.float32) / np.float32(hd))
    ang = (inv.astype(np.float32)[:, None] * np.arange(S, dtype=np.float32)[None, :]).astype(np.float32)
    c["cos"], c["sin"] = (np.tile(f(ang.astype(np.float64)), (4, 1)) for f in (np.cos, np.sin))
    t_ = np.arange(S)
    c["rst64"], c["rst128"] = (np.tile((t_ % n != 0)[None, :], (P, 1)) for n in (RC, P))
    table = np.concatenate([np.asarray(c[nm], np.float32) for nm, _ in CONSTS], 1)
    cols = np.zeros((P, 8), np.float32)
    cols[:, C_ONE], cols[:, C_EPS], cols[:, C_GN] = 1.0, 1e-6, 64e-5
    cols[:, C_LOG] = LOG_SHIFT / 2 * np.log(2.0)
    cols[:, C_SM] = np.where(i < 32, 2.0, 1.0)
    flags = np.zeros((L, P, 2), np.float32)
    flags[:, :, 0] = (np.arange(L) > 0)[:, None]
    flags[:, :, 1] = 1.0 - flags[:, :, 0]
    return {"consts": np.ascontiguousarray(table), "const_cols": cols, "flags": flags}


INPUTS = ("x", "norm_mix_w", "norm_ffn_w", "norm_final_w", "w_in", "hg_lb_table", "hg_norm_w", "gla_a_w2", "gla_a_b",
          "gla_norm_w", "rw_mu", "rw_w0", "rw_w2", "rw_a0", "rw_a2", "rw_g2", "rw_k_k", "rw_k_a", "rw_r_k", "rw_ln_w",
          "rw_ln_b", "rw_v0", "rw_v1", "rw_v2", "w_branch", "w_out", "ffn_w_up", "ffn_conv_w", "ffn_conv_b",
          "ffn_w_down")


def kernel(**inputs):
    import concourse.bacc as bacc
    from concourse.bass_utils import run_bass_kernel_spmd

    nc = bacc.Bacc("TRN2", target_bir_lowering=False, num_devices=1)
    arrays = {n: np.ascontiguousarray(inputs[n]) for n in INPUTS}
    arrays.update(constants())
    t = {n: nc.dram_tensor(f"in_{n}", a.shape, F32, kind="ExternalInput").ap() for n, a in arrays.items()}
    out = nc.dram_tensor("out", (1, S, D), F32, kind="ExternalOutput").ap()
    build(nc, t, out)
    r = run_bass_kernel_spmd(nc, [{f"in_{n}": a for n, a in arrays.items()}], core_ids=[0])
    return r.results[0]["out"]
```

```python
from itertools import chain

import numpy as np

import concourse.bass as bass
from concourse import mybir

F32 = mybir.dt.float32
F32R = mybir.dt.float32r
U32 = mybir.dt.uint32
ALU = mybir.AluOpType
ACT = mybir.ActivationFunctionType
AX = mybir.AxisListType

P = 128
D = 1024
S = 512
L = 2
KT = D // P
W = D // 4
HD = 64
NH = W // HD
NBR = 4
DFF = 11 * D // 4
FT = DFF // P
GDK = 32
GRANK = 16
TAU = 16.0
N_DIL = 3
DILS = (1, 4, 16)
ORDER = (1, 4, 4)
TB = S // P
RC = 64
NRC = S // RC

HG0 = 0
GL0 = 4 * W
GLW = 2 * NH * GDK + 2 * W + GRANK
RW0 = GL0 + GLW
RWW = 3 * W + 32 + 32 + 64
AT0 = RW0 + RWW
GT0 = AT0 + 9 * W
N_IN = GT0 + NBR * D

BR_ORDER = (2, 0, 1, 3)
GATE_ITEMS = [(n, d) for n in BR_ORDER for d in range(D // (2 * P))]

LEVELS = (64, 32, 16, 8, 4, 2, 1)
RAW = 2
HALF_SLOTS = 2
NPJ = 2
NMX = 6
BIG = 8.0e9
ARENA = 23300
OB_AT = (0, 2, 4, 4)

C_ONE, C_EPS, C_GN, C_LOG, C_SM = range(5)
LOG_SHIFT = 20


def _rows(*items):
    at, n = {}, 0
    for name, rows in items:
        at[name] = n
        n += rows
    return at, n


PA, NPA = _rows(("norm_mix", 8), ("norm_ffn", 8), ("hg_norm", 2), ("gla_norm", 2), ("gla_b", 1), ("w0", 2), ("a0", 2),
                ("k_k", 2), ("k_a", 2), ("r_k", 2), ("ln_w", 2), ("ln_b", 2), ("v0", 2), ("mu_r", 2), ("mu_k", 2),
                ("mu_v", 2), ("mu_sm", 1), ("lb", 4), ("final", 8))
PB, NPB = _rows(("conv_w", 3 * FT), ("conv_b", FT))


PARAMS = (("cols", NPA + NPB), ("lora", W), ("v1", 2 * 32), ("v2", W), ("aw2", P), ("flags", 2))
PARAM_AT = {nm: sum(n for _, n in PARAMS[:i]) for i, (nm, _) in enumerate(PARAMS)}
N_PARAM = sum(n for _, n in PARAMS)


def strips():
    out, at = [], {}

    def add(name, *pieces):
        at[name] = len(out)
        out.append(pieces)

    def win(name, col, width=2 * P):
        add(name, (0, "w_in", col, width, 0, KT))

    win("rw_r", RW0)
    win("rw_k", RW0 + W + 32)
    win("rw_v", RW0 + 2 * W + 32)
    add("rw_sm", (0, "w_in", RW0 + W, 32, 0, KT), (32, "w_in", RW0 + 3 * W + 32, 32, 0, KT),
        (64, "w_in", RW0 + 3 * W + 64, 64, 0, KT))
    win("gl_a", GL0 + 3 * W, P)
    for n, nm in enumerate(("hg_q", "hg_f", "hg_i", "hg_g")):
        win(nm, HG0 + n * W)
    win("gl_qk", GL0)
    win("gl_v", GL0 + W)
    win("gl_g", GL0 + 2 * W)
    for g in range(N_DIL):
        win(("at_q", g), AT0 + g * W)
        win(("at_k", g), AT0 + (N_DIL + g) * W)
        win(("at_v", g), AT0 + (2 * N_DIL + g) * W)
    for n in BR_ORDER:
        for d in range(D // (2 * P)):
            win(("gate", d, n), GT0 + n * D + d * 2 * P)
    for d in range(D // (2 * P)):
        add(("out", d), (0, "w_out", d * 2 * P, 2 * P, 0, KT))
    for c in range(FT // 2):
        add(("up", c), (0, "ffn_up", c * 2 * P, 2 * P, 0, KT))
        add(("gf", c), (0, "ffn_up", DFF + c * 2 * P, 2 * P, 0, KT))
    for d in range(D // (2 * P)):
        for j, k0 in enumerate(range(0, FT, KT)):
            add(("down", d, j), (0, "ffn_down", d * 2 * P, 2 * P, k0, min(KT, FT - k0)))
    return out, at


STRIPS, STRIP_AT = strips()


def tiles():
    t = []
    for nm in ("rw_r", "rw_k", "rw_v"):
        t += [((nm, m), "a") for m in range(2)]
    t += [(("rw_sm", 0), "a"), (("gl_a", 0), "a")]
    for nm in ("hg_q", "hg_f", "hg_i", "hg_g", "gl_qk", "gl_v", "gl_g"):
        t += [((nm, m), "a") for m in range(2)]
    for g in range(N_DIL):
        for nm in ("at_q", "at_k", "at_v"):
            t += [((nm, g, m), "a") for m in range(2)]
    for n in BR_ORDER:
        for d in range(D // (2 * P)):
            for m in range(2):
                t += [(("gate", d, n, m), "a"), (("br", d, n, m), "d")]
    for d in range(D // P):
        t.append((("out", d), "d"))
    for c in range(0, FT, 2):
        t += [(("up", c), "a"), (("up", c + 1), "a"), (("gf", c), "d"), (("gf", c + 1), "d")]
    for d in range(D // P):
        t.append((("down", d), "d"))
    return t


TILES = tiles()
TILE_AT = {n: i for i, (n, _) in enumerate(TILES)}


def taken(i):
    return sum(1 for _, e in TILES[:i + 1] if e == TILES[i][1])


def banks():
    bank, before, last = [], [], {}
    for i in range(len(TILES)):
        b = i % NPJ if i < TILE_AT[("up", 0)] else i % (NPJ + NMX)
        bank.append(b)
        before.append(last.get(b))
        last[b] = i
    return bank, before


BANK, BEFORE = banks()


def token_major(name):
    return name[0] in ("hg_i", "gl_v", "at_v")


def halves():
    half, step = [], []
    for name, _ in TILES:
        if name[0] == "br":
            step.append((name, [], True))
            continue
        if name[0] == "down":
            continue
        strip = (name[0], name[1] // 2) if name[0] in ("out", "up", "gf") else name[:-1] if len(name) > 2 else name[0]
        m = name[-1] % 2
        half.append((strip, m))
        if token_major(name):
            assert len(half) % HALF_SLOTS == (m + 1) % HALF_SLOTS
            step.append((name, half[-2:] if m else [], True))
        else:
            step.append((name, half[-1:], True))
    for d in range(0, D // P, 2):
        for j in range(3):
            for m in range(2):
                half.append((("down", d // 2, j), m))
                step.append((("down", d + m), half[-1:], j == 2))
    return half, step


HALVES, STEPS = halves()
HALF_AT = {h: i for i, h in enumerate(HALVES)}
DONE_AT = {name: i + 1 for i, (name, _, last) in enumerate(STEPS) if last}
USED_AT = {h: i + 1 for i, (_, read, _) in enumerate(STEPS) for h in read}

STORED = [n for n, _ in TILES if n[0][0:3] in ("hg_", "gl_", "at_")]
STORE_AT = {n: i for i, n in enumerate(STORED)}


def run(steps):
    for _ in steps:
        pass


def interleave(main, filler):
    for n in main:
        for _ in range(n):
            next(filler, None)


STAGES = {
    "rw_act": (("rw_sm1", 1), ("rw_sg", 1), ("rw_sig1", 1), ("rw_sig3", 1), ("rw_vm1", 2), ("rw_vm3", 1), ("rw_kn", 1),
               ("rw_em", 1), ("rw_eb", 1), ("rw_en", 1)),
    "rw_dve": (("rw_sm2", 1), ("rw_smx", 1), ("rw_sig2", 1), ("rw_vm2", 1), ("rw_sq", 1), ("rw_ss2", 1),
               ("rw_cum", 1), ("rw_bp", 1), ("rw_em2", 1), ("rw_eb2", 1), ("rw_ready", 1)),
}


class Sems:

    def __init__(self, nc, n):
        self.pool, self.made = [nc.alloc_semaphore(f"sem{i}") for i in range(n)], {}
        nums = [s.num for s in self.pool]
        assert nums == list(range(nums[0], nums[0] + n)), nums
        self.range = range(nums[0], nums[-1] + 1)

    def at(self, name, v):
        for group, stages in STAGES.items():
            before = 0
            for stage, times in stages:
                if stage == name:
                    return self[group], before + v
                before += times
        return self[name], v

    def __getitem__(self, name):
        if name not in self.made:
            self.made[name] = self.pool[len(self.made)]
        return self.made[name]


class Chain:

    def __init__(self, eng, sems, own):
        self.eng, self.sems, self.own, self.n = eng, sems, own, {}

    def __call__(self, ins, name=None):
        name = name or self.own
        self.n[name] = self.n.get(name, 0) + 1
        sem, count = self.sems.at(name, self.n[name])
        ins.then_inc(sem, 1)
        self.eng.wait_ge(sem, count)


def build(nc, t, out):
    sems = Sems(nc, 156)
    z_dram = nc.dram_tensor("z_scratch", (len(STORED), P, S), F32).ap()
    x_dram = nc.dram_tensor("x_scratch", (P, KT, S), F32).ap()

    def sb(name, *shape):
        return nc.alloc_sbuf_tensor(name, [P, *shape], F32)

    X = sb("x_fm", KT, S)
    HH, HL = (nc.alloc_sbuf_tensor(n, [P, KT, S], F32R) for n in ("h_high", "h_low"))
    RG = [sb(f"ring{i}", KT, 2 * P) for i in range(RAW)]
    WH, WL = (nc.alloc_sbuf_tensor(f"w_{n}", [P, KT, HALF_SLOTS * P], F32R) for n in ("high", "low"))
    BRG = [sb(f"brring{i}", 2, 2 * P) for i in range(2)]
    VF = sb("v_first", 2, S)
    CC = sb("consts", N_CONST)
    CST = sb("const_cols", 8)
    PRM = sb("params", N_PARAM)
    PC_, LORA, V1, V2, AW2, FLAG = (PRM[:, PARAM_AT[nm]:PARAM_AT[nm] + n] for nm, n in PARAMS)
    V1 = V1.rearrange("p (k n) -> p k n", k=2)
    LB = sb("lower_bound", 2)
    OMLB = sb("one_minus_lb", 2)
    LBT = sb("lb_tmp", 16)
    arena_at = -(-nc.sbuf_base // 32) * 32
    arena = nc.alloc_sbuf_tensor("arena", [P, ARENA], F32)
    OB = sb("branch_out", 6, S)
    PS = [nc.alloc_psum_tensor(f"ps{i}", [P, 512], F32) for i in range(8)]
    pj, mx = PS[:NPJ], PS[NPJ:]

    ccat = {}
    at = 0
    for nm, n in CONSTS:
        ccat[nm] = at
        at += n
    cc = lambda nm: CC[:, ccat[nm]:ccat[nm] + dict(CONSTS)[nm]]
    ident, ones, oblk, rot = cc("ident"), cc("ones"), cc("oblk"), cc("rot")
    lmask = cc("lmask").rearrange("p (l t) -> p l t", l=8)
    rmask, rst64, rst128 = cc("rmask"), cc("rst64"), cc("rst128")

    def pa(name, i=0):
        return PC_[:, PA[name] + i:PA[name] + i + 1]

    def pb_(name, i=0):
        return PC_[:, NPA + PB[name] + i:NPA + PB[name] + i + 1]

    def cst(i):
        return CST[:, i:i + 1]

    SG_AT = ARENA - 6 * S

    class Arena:
        def __init__(self):
            self.at = 0

        def __call__(self, *shape):
            n = int(np.prod(shape))
            v = arena[:, self.at:self.at + n]
            self.at += n
            assert self.at <= ARENA, self.at
            if len(shape) == 2:
                v = v.rearrange("p (a b) -> p a b", a=shape[0])
            elif len(shape) == 3:
                v = v.rearrange("p (a b c) -> p a b c", a=shape[0], b=shape[1])
            return v

    a = Arena()
    ZT, RS = a(2, S + 1), a(7, S)
    RA, RLW, RB, RG_, RBN, RKT = (a(2, S) for _ in range(6))
    AR = a(2, 2, S)
    RT1, RT2 = a(2, S), a(2, S)
    PCH = a(2, NRC)
    mark = a.at
    TOK = a(4, TB, P)
    G = a(8, 4 * P)
    TM, TTM = (X[:, i:i + 2, :].rearrange("p a (b c) -> p (a b) c", c=P) for i in (0, 2))
    SH = a(NRC + 1, HD)
    SPR = a(HD)
    as_tiles = lambda v, n: v.rearrange("p (a b) -> p a b", a=n)
    CM = as_tiles(RB.rearrange("p a b -> p (a b)"), 8)
    YM = as_tiles(RS[:, 2:4, :].rearrange("p a b -> p (a b)"), 8)
    W1, TV, U = (as_tiles(RS[:, i, :], 8) for i in (0, 1, 6))
    TAT = RT1[:, 0, :]
    VT = G[:, 0, :]
    YF = RLW

    def lin_buffers(nt):
        a = Arena()
        b = {}
        for nm in ("q", "k", "b", "t1", "t2", "t3"):
            b[nm] = a(nt, S)
        for nm in ("g", "o", "u1", "u2"):
            b[nm] = a(2, S)
        b["v"] = a(TB, 2 * P)
        b["x"] = [a(nt, S) for _ in range(2)]
        b["d"] = [a(nt, S) for _ in range(2)]
        b["a"] = a(NH, TB, P)
        b["kdt"] = a(nt, TB, P)
        b["sh"] = a(TB, nt, HD)
        b["ebl"] = a(nt, TB)
        if nt == 1:
            b["al"] = a(S)
        b["f"] = a(nt, S)
        assert a.at <= SG_AT, a.at
        return b

    HB, GB = lin_buffers(2), lin_buffers(1)

    a = Arena()
    QR, KR = a(6, S), a(6, S)
    VA = a(N_DIL * TB, 2 * P)
    TC, TR = a(S), a(S)
    SMX = a(2, 4 * P)
    PT = a(2, 4 * P)
    PE_ = a(2, 4 * P)
    TZ = [v[:, i, :] for v in (SMX, PT, PE_) for i in range(2)]
    NZ = len(TZ)
    ST = a(2, 3 * 2 * 2 * TB)
    STR = a(P)
    NM = a(2, 4)
    MN = a(3, S)
    CN = a(3, S)
    MG, DN, NU, TP = a(S), a(S), a(S), a(S)
    ATC = a(2 * S + 4 * P)
    cosT, sinT, amask = ATC[:, 0:S], ATC[:, S:2 * S], ATC[:, 2 * S:]
    assert a.at <= SG_AT

    a = Arena()
    a.at = SG_AT
    SG = [a(S) for _ in range(4)]
    MTMP = [a(S) for _ in range(2)]
    MT = X
    a = Arena()
    UP = [a(S + 2) for _ in range(2)]
    FC = [a(S) for _ in range(3)]
    FS = [a(S) for _ in range(2)]

    def split_pair(name, at_, *shape):
        n = int(np.prod(shape))
        return (nc.alloc_sbuf_tensor_at(f"{name}_{part}", [P, *shape], F32R, offset=arena_at + 4 * (at_ + i * n))
                for i, part in enumerate(("high", "low")))

    MTH, MTL = split_pair("merged", 0, KT, S)
    ffn_at = -(-a.at // 8) * 8
    HFH, HFL = split_pair("ffn", ffn_at, FT, S)
    assert ffn_at + 2 * FT * S <= ARENA + 6 * S
    a = Arena()
    a.at = 2 * KT * S
    SQN = a(KT, S)
    RSTD = a(S)
    NTMP = a(S)
    HT = [a(S) for _ in range(3)]
    HF = as_tiles(arena[:, KT * S:2 * KT * S], KT)
    STG = [OB[:, i, :] for i in range(4)]

    with nc.Block() as block:
        @block.sync
        def _(sp):
            sp.dma_start(CC[:, :], t["consts"][:, 0:N_CONST]).then_inc(sems["c_in"], 16)
            sp.dma_start(CST[:, :], t["const_cols"]).then_inc(sems["c_in"], 16)
            sp.dma_start(X[:, :, :], t["x_fm"]).then_inc(sems["x_in"], 16)
            sp.wait_ge(sems["c_in"], 32)
            sp.wait_ge(sems["x_in"], 16)

        @block.vector
        def _(dve):
            nc.vector.memset(VF[:, :, :], 0.0).then_inc(sems["vf0"], 1)

    def clear():
        nc.sync.sem_clear(sems.range)
        nc.all_engine_barrier()

    clear()

    table = {"set": None}

    def log_table():
        if table["set"] != "log":
            nc.scalar.preload_act_table_set("natural_log_exp_and_others")
            table["set"] = "log"

    def norm_pe(pe, run_):
        for k in range(KT):
            pe.wait_ge(sems["n_sq"], run_ * KT + k + 1)
            ins = nc.tensor.matmul(mx[0][:, :], ones, SQN[:, k, :], start=k == 0, stop=k == KT - 1)
            if k == KT - 1:
                ins.then_inc(sems["n_ss"], 1)
            yield

    def norm_act(act, ch, run_, x_ready=None, split=True):
        for k in range(KT):
            if x_ready:
                x_ready(k)
            nc.scalar.activation(SQN[:, k, :], X[:, k, :], ACT.Square).then_inc(sems["n_sq"], 1)
        log_table()
        act.wait_ge(sems["n_ss"], run_ + 1)
        ch(nc.scalar.activation(NTMP[:, :], mx[0][:, :], ACT.Ln, bias=cst(C_EPS), scale=1.0 / D))
        ch(nc.scalar.activation(RSTD[:, :], NTMP[:, :], ACT.Exp, scale=-0.5), "n_rstd")
        if split:
            for k in range(KT):
                act.wait_ge(sems["n_h"], run_ * KT + k + 1)
                nc.scalar.activation(HH[:, k, :], HT[k % 3], ACT.Copy).then_inc(sems["n_high"], 1)

    def norm_dve(dve, run_, wname):
        dve.wait_ge(sems["n_rstd"], run_ + 1)
        n = run_ * KT
        for k in range(KT + 1):
            if k < KT:
                if k >= 3:
                    dve.wait_ge(sems["n_low"], n + k - 2)
                nc.vector.scalar_tensor_tensor(HT[k % 3], X[:, k, :], pa(wname, k), RSTD[:, :], ALU.mult, ALU.mult)\
                    .then_inc(sems["n_h"], 1)
            if k:
                dve.wait_ge(sems["n_high"], n + k)
                nc.vector.tensor_tensor(HL[:, k - 1, :], HT[(k - 1) % 3], HH[:, k - 1, :].bitcast(F32), ALU.subtract)\
                    .then_inc(sems["n_low"], 1)

    def sig_act(ch, xs, tmp, src, bias=0.0, scale=1.0, name=None):
        log_table()
        nc.scalar.activation(xs, src, ACT.Identity, bias=bias, scale=scale)
        ch(nc.scalar.activation(tmp, src, ACT.Abs, bias=bias, scale=scale))
        ch(nc.scalar.activation(tmp, tmp, ACT.Exp, scale=-1.0))
        ch(nc.scalar.activation(tmp, tmp, ACT.Ln, bias=cst(C_ONE), scale=1.0), name)

    def sig_dve(ch, dst, xs, tmp, name=None):
        ch(nc.vector.scalar_tensor_tensor(dst, xs, 0.0, tmp, ALU.min, ALU.subtract), name)

    flat = lambda v: v.rearrange("p a b -> p (a b)")

    mm = nc.tensor.matmul
    tr = nc.tensor.transpose
    V, A = nc.vector, nc.scalar
    TOKN = ("a", "b", "k", "v")
    half = lambda hh: slice(HD * hh, HD * hh + HD)

    def rwkv_pe(pe):
        w = lambda nm, v: pe.wait_ge(*sems.at(nm, v))
        yield 3
        w("rw_smx", 1)
        w("rw_shift", 7)
        for m in range(2):
            mm(mx[m][:, :], LORA[0:32, m * P:(m + 1) * P], RA[0:32, 0, :], start=True, stop=True)
        for m in range(2):
            mm(mx[2 + m][:, :], LORA[32:64, m * P:(m + 1) * P], RA[32:64, 0, :], start=True, stop=True)
        for m in range(2):
            ins = mm(mx[4][0:32, :], V1[:, m, :], RS[:, 4 + m, :], start=m == 0, stop=m == 1)
        ins.then_inc(sems["rw_lora"], 1)
        yield 4
        w("rw_sig1", 1)
        for m in range(2):
            mm(mx[m][:, :], V2[0:32, m * P:(m + 1) * P], VT[0:32, :], start=True, stop=True)
        for m in range(2):
            ins = mm(mx[2 + m][:, :], LORA[64:128, m * P:(m + 1) * P], RBN[64:128, 0, :], start=True, stop=True)
        ins.then_inc(sems["rw_lora2"], 1)
        yield 3
        w("rw_sq", 1)
        for m in range(2):
            ins = mm(mx[4 + m][:, :], oblk, RT1[:, m, :], start=True, stop=True)
        ins.then_inc(sems["rw_ss"], 1)
        yield 3
        w("rw_bp", 1)
        for m in range(2):
            ins = mm(mx[m][:, :], oblk, RT1[:, m, :], start=True, stop=True)
        ins.then_inc(sems["rw_bs"], 1)
        yield 3
        w("rw_ready", 1)
        for p in range(2):
            src = (AR[:, p, 0, :], RA[:, p, :], RKT[:, p, :], RS[:, 4 + p, :])
            for q in range(4):
                for tb in range(TB):
                    ins = tr(mx[q][:, tb * P:(tb + 1) * P], src[q][:, tb * P:(tb + 1) * P], ident)
                ins.then_inc(sems["rw_tr"], 1)
            yield 1
            w("rw_tok", 3 * (p + 1))
            for hh in range(2):
                for tb in range(TB):
                    i = hh * TB + tb
                    if i >= 2:
                        w("rw_g", 8 * p + i - 1)
                    ts = slice(tb * P, (tb + 1) * P)
                    mm(mx[i % 2][:, 0:256], RA[half(hh), p, ts], AR[half(hh), p, :, ts], start=True, stop=True)
                    mm(mx[i % 2][:, 256:512], RKT[half(hh), p, ts], AR[half(hh), p, :, ts], start=True, stop=True)\
                        .then_inc(sems["rw_gp"], 1)
            yield 1
            w("rw_g", 8 * p + 8)
            for g in range(2):
                w("rw_cm", p * 12 + g + 1)
                for j in range(4):
                    ins = tr(mx[3 * g][:, j * P:(j + 1) * P], CM[:, 4 * g + j, :], ident)
                ins.then_inc(sems["rw_y1"], 1)
            yield 1
            for l in range(1, 6):
                for g in range(2):
                    n = (p * 6 + l) * 2 + g
                    w("rw_cm", n + 1)
                    w("rw_t", n - 1)
                    for j in range(4):
                        ins = mm(mx[3 * g][:, j * P:(j + 1) * P], CM[:, 4 * g + j, :], TM[:, 4 * g + j, :], start=True,
                                 stop=True)
                    ins.then_inc(sems["rw_y1"], 1)
                yield 1
                for g in range(2):
                    z, zt = mx[3 * g + 1:3 * g + 3]
                    w("rw_ym", (p * 5 + l - 1) * 2 + g + 1)
                    for j in range(4) if l < 5 else ():
                        mm(z[:, j * P:(j + 1) * P], TTM[:, 4 * g + j, :], YM[:, 4 * g + j, :], start=True, stop=True)
                    for j in range(4):
                        ins = mm(zt[:, j * P:(j + 1) * P], YM[:, 4 * g + j, :], TTM[:, 4 * g + j, :], start=True, stop=True)
                    ins.then_inc(sems["rw_z"], 1)
                yield 1
            w("rw_t", (p + 1) * 12)
            for hh in range(2):
                for tb in range(TB):
                    i = hh * TB + tb
                    ins = mm(mx[0][:, i * HD:(i + 1) * HD], G[:, i, 256:384], TOK[:, 3, tb, half(hh)], start=True, stop=True)
            ins.then_inc(sems["rw_w1p"], 1)
            yield 1
            w("rw_w1", p + 1)
            for hh in range(2):
                for tb in range(TB):
                    i = hh * TB + tb
                    mm(mx[1][:, i * HD:(i + 1) * HD], TTM[:, i, :], W1[:, i, :], start=True, stop=True)
            for hh in range(2):
                for tb in range(TB):
                    i = hh * TB + tb
                    ins = mm(mx[2][half(hh), tb * P:(tb + 1) * P], TOK[:, 0, tb, half(hh)], TTM[:, i, :], start=True, stop=True)
            ins.then_inc(sems["rw_tvp"], 1)
            yield 1
            w("rw_tv", 2 * (p + 1))
            for c in range(NRC):
                tb, par = divmod(c, 2)
                rows = slice(RC * par, RC * par + RC)
                w("rw_s", p * NRC + c + 1)
                for hh in range(2):
                    ins = mm(mx[3 + hh][rows, 0:HD], TAT[half(hh), c * RC:(c + 1) * RC], SH[half(hh), c, :],
                             start=True, stop=True)
                ins.then_inc(sems["rw_up"], 1)
                if c % 2 == 0:
                    yield 1
                w("rw_u", p * NRC + c + 1)
                if c < NRC - 1:
                    for hh in range(2):
                        mm(mx[5][half(hh), 0:HD], TOK[rows, 1, tb, half(hh)], U[rows, hh * TB + tb, :],
                           start=True, stop=False)
                        ins = mm(mx[5][half(hh), 0:HD], TOK[rows, 2, tb, half(hh)], TOK[rows, 3, tb, half(hh)],
                                 start=False, stop=True)
                    ins.then_inc(sems["rw_sp"], 1)
            for hh in range(2):
                for tb in range(TB):
                    i = hh * TB + tb
                    o = mx[0][half(hh), tb * P:(tb + 1) * P]
                    mm(o, U[:, i, :], G[:, i, 128:256], start=True, stop=False)
                    mm(o, TOK[:, 3, tb, half(hh)], G[:, i, 384:512], start=False, stop=False)
                    for par in range(2):
                        c = 2 * tb + par
                        ins = mm(mx[0][half(hh), c * RC:(c + 1) * RC], SH[half(hh), c, :],
                                 AR[half(hh), p, 1, c * RC:(c + 1) * RC], start=False, stop=par == 1)
            ins.then_inc(sems["rw_yp"], 1)
            yield 1
            w("rw_yf", p + 1)
        for m in range(2):
            ins = mm(mx[m][:, :], oblk, YF[:, m, :], start=True, stop=True)
        ins.then_inc(sems["rw_mean"], 1)
        yield 1
        w("rw_yc", 1)
        for m in range(2):
            ins = mm(mx[2 + m][:, :], oblk, RT1[:, m, :], start=True, stop=True)
        ins.then_inc(sems["rw_var"], 1)
        yield 2

    def rwkv_act(act, ch):
        w = lambda nm, v: act.wait_ge(*sems.at(nm, v))
        sm_scale = cst(C_SM)
        i = 0
        for nm, m in [(n, m) for n in ("rw_r", "rw_k", "rw_v") for m in range(2)] + [("rw_sm", 0)]:
            take_act(act, (nm, m))
            w("rw_zpad", 1)
            if i >= 2:
                w("rw_shift", i - 1)
            ch(A.activation(ZT[:, i % 2, 1:S + 1], tile_bank((nm, m))[:, :], ACT.Copy), "out_act")
            i += 1
        w("rw_shift", 7)
        sig_act(ch, RBN[:, 0, :], RT1[:, 0, :], RS[:, 6, :], scale=sm_scale, name="rw_sm1")
        w("rw_sm2", 1)
        ch(A.activation(RBN[:, 0, :], RBN[:, 0, :], ACT.Exp), "rw_sg")
        yield 3
        w("rw_lora", 1)
        ch(A.activation(VT[0:32, :], mx[4][0:32, :], ACT.Copy))
        w("rw_smx", 1)
        for m in range(2):
            sig_act(ch, RLW[:, m, :], RT1[:, m, :], mx[m][:, :], bias=pa("w0", m))
        for m in range(2):
            sig_act(ch, RKT[:, m, :], RT2[:, m, :], mx[2 + m][:, :], bias=pa("a0", m), name="rw_sig1" if m else None)
        yield 4
        w("rw_sig2", 1)
        A.activation(flat(RLW), flat(RLW), ACT.Exp)
        ch(A.activation(flat(RA), flat(RKT), ACT.Exp), "rw_sig3")
        w("rw_lora2", 1)
        for m in range(2):
            A.activation(RG_[:, m, :], mx[2 + m][:, :], ACT.Copy)
            sig_act(ch, RT2[:, m, :], RT1[:, m, :], mx[m][:, :], bias=pa("v0", m), name="rw_vm1")
        w("rw_vm2", 1)
        ch(A.activation(flat(RT2), flat(RT2), ACT.Exp), "rw_vm3")
        yield 3
        w("rw_ss2", 1)
        ch(A.activation(flat(RT1), flat(RT1), ACT.Ln, scale=float(2 ** LOG_SHIFT)))
        ch(A.activation(flat(RT1), flat(RT1), ACT.Exp, scale=-0.5, bias=cst(C_LOG)), "rw_kn")
        yield 3
        w("rw_cum", 1)
        ch(A.activation(flat(RT2), flat(RT2), ACT.Exp), "rw_em")
        w("rw_em2", 1)
        ch(A.activation(flat(RT2), flat(RB), ACT.Exp), "rw_eb")
        w("rw_eb2", 1)
        ch(A.activation(flat(RT2), flat(RB), ACT.Exp, scale=-1.0), "rw_en")
        yield 3
        for p in range(2):
            for q in (2, 3):
                w("rw_tr", 4 * p + q + 1)
                ch(A.activation(flat(TOK[:, q]), mx[q][:, :], ACT.Copy), "rw_tokx")
            yield 1
            yield 1
            yield 1
            for n in range(2, 12):
                w("rw_y1", p * 12 + n + 1)
                g = n % 2
                ch(A.activation(flat(YM[:, 4 * g:4 * g + 4]), mx[3 * g][:, :], ACT.Copy), "rw_ym")
                if g:
                    yield 1
                    yield 1
            w("rw_w1p", p + 1)
            ch(A.activation(flat(W1), mx[0][:, :], ACT.Copy), "rw_w1")
            yield 1
            w("rw_tvp", p + 1)
            ch(A.activation(flat(TV), mx[1][:, :], ACT.Copy), "rw_tv")
            ch(A.activation(TAT[:, :], mx[2][:, :], ACT.Copy), "rw_tv")
            yield 1
            for _ in range(NRC // 2):
                yield 1
            w("rw_yp", p + 1)
            ch(A.activation(YF[:, p, :], mx[0][:, :], ACT.Copy), "rw_yf")
            yield 1
        yield 1
        w("rw_var", 1)
        for m in range(2):
            ch(A.activation(RT2[:, m, :], mx[2 + m][:, :], ACT.Ln, scale=1.0 / HD, bias=cst(C_GN)))
        ch(A.activation(flat(RT2), flat(RT2), ACT.Exp, scale=-0.5), "rw_rstd")
        yield 2

    def rwkv_dve(dve, ch):
        w = lambda nm, v: dve.wait_ge(*sems.at(nm, v))
        ch(V.memset(ZT[:, :, 0:1], 0.0), "rw_zpad")
        mus = [("mu_r", 0), ("mu_r", 1), ("mu_k", 0), ("mu_k", 1), ("mu_v", 0), ("mu_v", 1), ("mu_sm", 0)]
        for i in range(7):
            w("out_act", i + 1)
            z = ZT[:, i % 2, 1:S + 1]
            ch(V.tensor_tensor(RT1[:, i % 2, :], ZT[:, i % 2, 0:S], z, ALU.subtract))
            ch(V.scalar_tensor_tensor(RS[:, i, :], RT1[:, i % 2, :], pa(*mus[i]), z, ALU.mult, ALU.add), "rw_shift")
        w("rw_sm1", 1)
        sig_dve(ch, RBN[:, 0, :], RBN[:, 0, :], RT1[:, 0, :], "rw_sm2")
        w("rw_sg", 1)
        V.tensor_scalar(RA[0:32, 0, :], RBN[0:32, 0, :], 2.0, -1.0, ALU.mult, ALU.add)
        ch(V.tensor_copy(RA[32:64, 0, :], RS[32:64, 6, :]), "rw_smx")
        yield 3
        yield 4
        w("rw_sig1", 1)
        sig_dve(ch, flat(RLW), flat(RLW), flat(RT1))
        sig_dve(ch, flat(RKT), flat(RKT), flat(RT2), "rw_sig2")
        w("rw_vm1", 2)
        sig_dve(ch, flat(RT2), flat(RT2), flat(RT1), "rw_vm2")
        w("rw_sig3", 1)
        ch(V.tensor_scalar_mul(flat(RLW), flat(RLW), -float(np.exp(np.float64(-0.5)))))
        r, k, v = RS[:, 0:2, :], RS[:, 2:4, :], RS[:, 4:6, :]
        ch(V.tensor_scalar(flat(RT1), flat(v), FLAG[:, 1:2], None, ALU.mult))
        ch(V.scalar_tensor_tensor(flat(VF), flat(VF), FLAG[:, 0:1], flat(RT1), ALU.mult, ALU.add))
        ch(V.tensor_tensor(flat(RT1), flat(VF), flat(v), ALU.subtract))
        w("rw_vm3", 1)
        ch(V.tensor_tensor(flat(RT1), flat(RT1), flat(RT2), ALU.mult))
        ch(V.tensor_tensor(flat(v), flat(v), flat(RT1), ALU.add))
        w("rw_lora2", 1)
        kk = AR[:, :, 0, :]
        for m in range(2):
            ch(V.tensor_scalar(AR[:, m, 0, :], k[:, m, :], pa("k_k", m), None, ALU.mult))
        ch(V.tensor_tensor(RT1, kk, kk, ALU.mult), "rw_sq")
        yield 3
        for m in range(2):
            V.tensor_tensor_scan(RB[:, m, :], rst64, RLW[:, m, :], 0.0, ALU.mult, ALU.add)
        for m in range(2):
            ch(V.tensor_scalar(RT2[:, m, :], RA[:, m, :], -1.0, pa("k_a", m), ALU.add, ALU.mult))
        ch(V.scalar_tensor_tensor(flat(RKT), flat(RT2), 1.0, flat(k), ALU.add, ALU.mult))
        w("rw_ss", 1)
        for m in range(2):
            ins = V.tensor_scalar_max(RT1[:, m, :], mx[4 + m][:, :], 1e-24)
        ch(ins, "rw_ss2")
        ch(V.tensor_tensor(flat(RT2), flat(RB), flat(RLW), ALU.subtract), "rw_cum")
        w("rw_kn", 1)
        ch(V.tensor_tensor(kk, kk, RT1, ALU.mult))
        ch(V.tensor_tensor(RA, RA, kk, ALU.mult))
        ch(V.tensor_tensor(RT1, r, RKT, ALU.mult))
        for m in range(2):
            ins = V.tensor_scalar(RT1[:, m, :], RT1[:, m, :], pa("r_k", m), None, ALU.mult)
        ch(ins, "rw_bp")
        yield 3
        w("rw_bs", 1)
        for m in range(2):
            ins = V.tensor_tensor(RBN[:, m, :], mx[m][:, :], v[:, m, :], ALU.mult)
        ch(ins)
        w("rw_em", 1)
        ch(V.tensor_tensor(kk, kk, RT2, ALU.mult), "rw_em2")
        w("rw_eb", 1)
        V.tensor_copy(PCH, RT2.rearrange("p m (c t) -> p m c t", t=RC)[:, :, :, RC - 1])
        ch(V.tensor_tensor(AR[:, :, 1, :], r, RT2, ALU.mult), "rw_eb2")
        w("rw_en", 1)
        V.tensor_tensor(RA, RA, RT2, ALU.mult)
        ch(V.tensor_tensor(RKT, RKT, RT2, ALU.mult), "rw_ready")
        yield 3
        for p in range(2):
            for q in range(2):
                w("rw_tr", 4 * p + q + 1)
                ch(V.tensor_copy(flat(TOK[:, q]), mx[q][:, :]), "rw_tok")
            w("rw_tokx", 2 * p + 2)
            ch(V.memset(SH[:, 0, :], 0.0), "rw_tok")
            yield 1
            for i in range(8):
                w("rw_gp", 8 * p + i + 1)
                ch(V.tensor_tensor(G[:, i, :], mx[i % 2][:, :], rmask, ALU.mult), "rw_g")
            yield 1

            def masked(l):
                for g in range(2):
                    gs = slice(4 * g, 4 * g + 4)
                    if l:
                        w("rw_y1", (p * 6 + l - 1) * 2 + g + 1)
                    ch(V.tensor_tensor(CM[:, gs, :], G[:, gs, 0:P], bc(lmask[:, 6 - l, :], 4), ALU.mult), "rw_cm")

            masked(0)
            yield 1
            dve.wait_ge(sems["x_out_d"], 16)
            for g in range(2):
                gs = slice(4 * g, 4 * g + 4)
                V.tensor_tensor(TTM[:, gs, :], bc(ident, 4), CM[:, gs, :], ALU.subtract)
                w("rw_y1", p * 12 + g + 1)
                ch(V.tensor_tensor(TM[:, gs, :], bc(ident, 4), as_tiles(mx[3 * g][:, :], 4), ALU.subtract), "rw_t")
            masked(1)
            for l in range(1, 6):
                if l < 5:
                    masked(l + 1)
                yield 1
                for g in range(2):
                    gs = slice(4 * g, 4 * g + 4)
                    w("rw_z", (p * 5 + l - 1) * 2 + g + 1)
                    if l < 5:
                        V.tensor_tensor(flat(TM[:, gs, :]), flat(TM[:, gs, :]), mx[3 * g + 1][:, :], ALU.subtract)
                    ch(V.tensor_tensor(flat(TTM[:, gs, :]), flat(TTM[:, gs, :]), mx[3 * g + 2][:, :], ALU.subtract), "rw_t")
                yield 1
            yield 1
            yield 1
            w("rw_tv", 2 * (p + 1))
            ch(V.memset(SH[:, 0, :], 0.0), "rw_s")
            for c in range(NRC):
                tb, par = divmod(c, 2)
                rows = slice(RC * par, RC * par + RC)
                pc = PCH[:, p, c:c + 1]
                w("rw_up", p * NRC + c + 1)
                for hh in range(2):
                    i = hh * TB + tb
                    ins = V.scalar_tensor_tensor(U[rows, i, :], mx[3 + hh][rows, 0:HD], -1.0, TV[rows, i, :],
                                                 ALU.mult, ALU.subtract)
                ch(ins, "rw_u")
                if c % 2 == 0:
                    yield 1
                if c < NRC - 1:
                    ch(V.tensor_scalar(SPR[:, :], SH[:, c, :], pc, None, ALU.mult))
                    w("rw_sp", p * (NRC - 1) + c + 1)
                    ch(V.scalar_tensor_tensor(SH[:, c + 1, :], mx[5][:, 0:HD], pc, SPR[:, :], ALU.mult, ALU.add), "rw_s")
            yield 1
        w("rw_mean", 1)
        for m in range(2):
            ins = V.scalar_tensor_tensor(YF[:, m, :], mx[m][:, :], -1.0 / HD, YF[:, m, :], ALU.mult, ALU.add)
        ch(ins)
        ch(V.tensor_tensor(RT1, YF, YF, ALU.mult), "rw_yc")
        yield 1
        w("rw_rstd", 1)
        ch(V.tensor_tensor(YF, YF, RT2, ALU.mult))
        for m in range(2):
            ins = V.tensor_scalar(YF[:, m, :], YF[:, m, :], pa("ln_w", m), pa("ln_b", m), ALU.mult, ALU.add)
        ch(ins)
        ch(V.tensor_tensor(YF, YF, RBN, ALU.add))
        ch(V.tensor_tensor(OB[:, 4:6, :], YF, RG_, ALU.mult), "rw_done")
        yield 2

    def bc(v, n):
        return v.unsqueeze(1).to_broadcast([v.shape[0], n, v.shape[1]])

    def tile_bank(name):
        return PS[BANK[TILE_AT[name]]]

    def take_act(act, name):
        act.wait_ge(sems["step"], DONE_AT[name])

    NL = len(LEVELS)
    HG_LEAVES = dict(d=NL, e=NL, x=NL, sc=(NL + 1) * NH, cp=(NL + 1) * NH, kdt=2)

    def lin_wait(eng, pre, nm, v):
        eng.wait_ge(sems["lin_" + nm], v + (HG_LEAVES.get(nm, 1) if pre == "gl" else 0))

    def linear_pe(pe, pre, b, nt, dk):
        w = lambda nm, v: lin_wait(pe, pre, nm, v)
        hpt = P // dk
        yield 14 if pre == "hg" else 7
        for l in range(len(LEVELS) + 1):
            if l:
                yield 1
            if l < len(LEVELS):
                w("x", l + 1)
                kx = qx = b["x"][l % 2]
            else:
                w("qk", 1)
                kx, qx = b["k"], b["q"]
            for h in range(NH):
                ti, r = divmod(h, hpt)
                rows = slice(dk * r, dk * r + dk)
                if l >= 1:
                    w("cp", (l - 1) * NH + h + 1)
                for c in range(TB):
                    ts = slice(c * P, (c + 1) * P)
                    ins = mm(mx[h][:, ts], kx[rows, ti, ts], qx[rows, ti, ts], start=True, stop=True)
                ins.then_inc(sems["lin_sc"], 1)
        yield 1
        w("kd", 1)
        for ti in range(nt):
            for c in range(TB):
                ins = tr(mx[4 + ti][:, c * P:(c + 1) * P], b["t1"][:, ti, c * P:(c + 1) * P], ident)
        ins.then_inc(sems["lin_kdp"], 1)
        yield 1
        w("kdt", nt)
        for h in range(NH):
            ti, r = divmod(h, hpt)
            rows = slice(dk * r, dk * r + dk)
            for c in range(TB - 1):
                at_ = (ti * (TB - 1) + c) * HD
                ins = mm(mx[4][rows, at_:at_ + HD], b["kdt"][:, ti, c, rows], b["v"][:, c, h * HD:(h + 1) * HD],
                         start=True, stop=True)
        ins.then_inc(sems["lin_kv"], 1)
        yield 1
        w("sh", 1)
        w("qb", 1)
        w("cp", (len(LEVELS) + 1) * NH)
        for h in range(NH):
            ti, r = divmod(h, hpt)
            rows = slice(dk * r, dk * r + dk)
            for c in range(TB):
                o = mx[h // 2][half(h % 2), c * P:(c + 1) * P]
                mm(o, b["v"][:, c, h * HD:(h + 1) * HD], b["a"][:, h, c, :], start=True, stop=False)
                ins = mm(o, b["sh"][rows, c, ti, :], b["t2"][rows, ti, c * P:(c + 1) * P], start=False, stop=True)
        ins.then_inc(sems["lin_op"], 1)
        yield 1
        w("osq", 1)
        for m in range(2):
            ins = mm(mx[2 + m][:, :], oblk, b["u1"][:, m, :], start=True, stop=True)
        ins.then_inc(sems["lin_oss"], 1)
        yield 2

    def blocks(v, n):
        return flat(v).rearrange("p (b h n) -> p b h n", h=2, n=n)

    def linear_act(act, ch, pre, b, nt):
        w = lambda nm, v: lin_wait(act, pre, nm, v)
        for l, n in enumerate(LEVELS):
            if l >= 2:
                yield 4 if l == 2 else 1
            w("d", l + 1)
            d = blocks(b["d"][l % 2], n)
            A.activation(d[:, :, 0, :], d[:, :, 0, :], ACT.Exp, scale=-1.0)
            ch(A.activation(d[:, :, 1, :], d[:, :, 1, :], ACT.Exp), "lin_e")
        for _ in range(3):
            yield 1
        w("db", 1)
        ch(A.activation(flat(b["t1"]), flat(b["t1"]), ACT.Exp, scale=-1.0), "lin_ed")
        ch(A.activation(flat(b["t2"]), flat(b["b"]), ACT.Exp), "lin_eb")
        yield 1
        w("kdp", 1)
        for ti in range(nt):
            ch(A.activation(flat(b["kdt"][:, ti]), mx[4 + ti][:, :], ACT.Copy), "lin_kdt")
        yield 1
        yield 1
        w("op", 1)
        for m in range(2):
            ins = A.activation(b["o"][:, m, :], mx[m][:, :], ACT.Copy)
        ch(ins)
        ch(A.activation(flat(b["u1"]), flat(b["o"]), ACT.Square), "lin_osq")
        yield 1
        log_table()
        w("oss", 1)
        for m in range(2):
            ins = A.activation(b["u2"][:, m, :], mx[2 + m][:, :], ACT.Ln, scale=1.0 / HD, bias=cst(C_EPS))
        ch(ins)
        ch(A.activation(flat(b["u2"]), flat(b["u2"]), ACT.Exp, scale=-0.5), "lin_rs")
        yield 2

    def linear_dve(dve, ch, pre, b, nt, norm, ob):
        w = lambda nm, v: lin_wait(dve, pre, nm, v)
        ch(V.memset(b["a"].rearrange("p a b c -> p (a b c)"), 0.0))
        V.memset(b["sh"][:, 0, :, :], 0.0)
        for m in range(nt):
            ins = V.tensor_tensor_scan(b["b"][:, m, :], rst128, b["f"][:, m, :], 0.0, ALU.mult, ALU.add)
        ch(ins)
        bb = flat(b["b"])

        def diff(l):
            n = LEVELS[l]
            v = bb.rearrange("p (b m) -> p b m", m=2 * n)
            if l >= 2:
                w("x", l - 1)
            ch(V.tensor_tensor(flat(b["d"][l % 2]).rearrange("p (b m) -> p b m", m=2 * n), v,
                               v[:, :, n - 1:n].to_broadcast([P, v.shape[1], 2 * n]), ALU.subtract), "lin_d")

        diff(0)
        for l, n in enumerate(LEVELS):
            if l + 1 < len(LEVELS):
                diff(l + 1)
            w("e", l + 1)
            if l >= 2:
                w("sc", (l - 1) * NH)
            d, x, k, q = (blocks(v, n) for v in (b["d"][l % 2], b["x"][l % 2], b["k"], b["q"]))
            V.tensor_tensor(x[:, :, 0, :], k[:, :, 0, :], d[:, :, 0, :], ALU.mult)
            ch(V.tensor_tensor(x[:, :, 1, :], q[:, :, 1, :], d[:, :, 1, :], ALU.mult), "lin_x")
            if l:
                copy_scores(dve, ch, pre, b, l - 1)
            yield 1 if l else 4
        copy_scores(dve, ch, pre, b, len(LEVELS) - 1)
        yield 1
        v = bb.rearrange("p (b m) -> p b m", m=P)
        ch(V.tensor_tensor(flat(b["t1"]).rearrange("p (b m) -> p b m", m=P), v,
                           v[:, :, P - 1:P].to_broadcast([P, v.shape[1], P]), ALU.subtract), "lin_db")
        w("ed", 1)
        ch(V.tensor_tensor(flat(b["t1"]), flat(b["t1"]), flat(b["k"]), ALU.mult), "lin_kd")
        yield 1
        copy_scores(dve, ch, pre, b, len(LEVELS))
        w("eb", 1)
        ch(V.tensor_copy(b["ebl"], b["t2"].rearrange("p m (c t) -> p m c t", t=P)[:, :, :, P - 1]))
        ch(V.tensor_tensor(flat(b["t2"]), flat(b["t2"]), flat(b["q"]), ALU.mult), "lin_qb")
        yield 1
        w("kv", 1)
        for c in range(TB - 1):
            for ti in range(nt):
                at_ = (ti * (TB - 1) + c) * HD
                ins = V.scalar_tensor_tensor(b["sh"][:, c + 1, ti, :], b["sh"][:, c, ti, :], b["ebl"][:, ti, c:c + 1],
                                             mx[4][:, at_:at_ + HD], ALU.mult, ALU.add)
            ch(ins, "lin_sh" if c == TB - 2 else None)
        yield 1
        yield 1
        w("rs", 1)
        ch(V.tensor_tensor(flat(b["o"]), flat(b["o"]), flat(b["u2"]), ALU.mult))
        for m in range(2):
            if ob == 0 and m == 0:
                for i in range(len(STG)):
                    dve.wait_ge(sems[f"z_out{i}"], 16 * len(STORED[i::len(STG)]))
            ins = V.scalar_tensor_tensor(OB[:, ob + m, :], b["o"][:, m, :], pa(norm, m), b["g"][:, m, :], ALU.mult, ALU.mult)
        ch(ins, "lin_done")
        yield 2

    def copy_scores(dve, ch, pre, b, l):
        for h in range(NH):
            lin_wait(dve, pre, "sc", l * NH + h + 1)
            ch(V.copy_predicated(b["a"][:, h, :, :], bc(lmask[:, l, :], TB).bitcast(U32),
                                 mx[h][:, :].rearrange("p (c t) -> p c t", c=TB)), "lin_cp")

    def store_tile(act, ch, name):
        i = STORE_AT[name]
        width = GRANK if name[0] == "gl_a" else P
        take_act(act, name)
        if i >= len(STG):
            act.wait_ge(sems[f"z_out{i % len(STG)}"], 16 * (i // len(STG)))
        ch(A.activation(STG[i % len(STG)][0:width, :], tile_bank(name)[0:width, :], ACT.Copy), "out_act")
        act.dma_start(z_dram[i][0:width, :], STG[i % len(STG)][0:width, :]).then_inc(sems[f"z_out{i % len(STG)}"], 16)

    def load_tile(act, name, dst, sem):
        i = STORE_AT[name]
        width = GRANK if name[0] == "gl_a" else P
        act.wait_ge(sems[f"z_out{i % len(STG)}"], 16 * (i // len(STG) + 1))
        src = z_dram[i][0:width, :]
        act.dma_start(dst[0:width], src).then_inc(sems[sem], 16)

    DONE = {2: ("rw_done", 1), 0: ("lin_done", 1), 1: ("lin_done", 2), 3: ("at_done", 2)}

    def gl_pe(pe):
        yield 2
        pe.wait_ge(sems["z_in"], 16 * 15)
        mm(mx[5][:, :], AW2[0:GRANK, :], GB["al"][0:GRANK, :], start=True, stop=True).then_inc(sems["gl_u"], 1)
        yield from linear_pe(pe, "gl", GB, 1, GDK)

    def hg_act(act, ch):
        b = HB
        w = lambda nm, v: act.wait_ge(sems["hg_" + nm], v)
        act.wait_ge(sems["rw_done"], 1)
        for m in range(2):
            load_tile(act, ("hg_q", m), b["q"][:, m, :], "z_in")
            load_tile(act, ("hg_f", m), b["f"][:, m, :], "z_in")
            load_tile(act, ("hg_g", m), b["g"][:, m, :], "z_in")
            load_tile(act, ("hg_i", m), flat(b["v"][:, 2 * m:2 * m + 2, :]), "z_in")
        yield 4
        act.wait_ge(sems["z_in"], 16 * 8)
        sig_act(ch, flat(b["t1"]), flat(b["t2"]), flat(b["q"]), name="hg_s1")
        w("s2", 1)
        ch(A.activation(flat(b["t1"]), flat(b["t1"]), ACT.Exp), "hg_s3")
        yield 2
        sig_act(ch, flat(b["u1"]), flat(b["u2"]), flat(b["g"]), name="hg_g1")
        w("g2", 1)
        ch(A.activation(flat(b["g"]), flat(b["u1"]), ACT.Exp), "hg_g3")
        yield 2
        w("s4", 1)
        sig_act(ch, flat(b["t1"]), flat(b["t2"]), flat(b["f"]), name="hg_f1")
        yield 2
        w("f2", 1)
        ch(A.activation(flat(b["t2"]), flat(b["t2"]), ACT.Exp), "hg_f3")
        log_table()
        w("f4", 1)
        A.activation(flat(b["t2"]), flat(b["t2"]), ACT.Ln, bias=cst(C_ONE), scale=1.0)
        ch(A.activation(flat(b["t3"]), flat(b["t3"]), ACT.Ln, scale=1e-9), "hg_f5")
        ch(A.activation(flat(b["k"]), flat(b["k"]), ACT.Exp), "hg_k1")
        yield from linear_act(act, ch, "hg", b, 2)

    def hg_dve(dve, ch):
        b = HB
        w = lambda nm, v: dve.wait_ge(sems["hg_" + nm], v)
        yield 4
        w("s1", 1)
        sig_dve(ch, flat(b["t1"]), flat(b["t1"]), flat(b["t2"]), "hg_s2")
        w("s3", 1)
        ch(V.tensor_tensor(flat(b["q"]), flat(b["q"]), flat(b["t1"]), ALU.mult), "hg_s4")
        yield 2
        w("g1", 1)
        sig_dve(ch, flat(b["u1"]), flat(b["u1"]), flat(b["u2"]), "hg_g2")
        yield 2
        w("f1", 1)
        sig_dve(ch, flat(b["t1"]), flat(b["t1"]), flat(b["t2"]))
        ch(V.tensor_tensor(flat(b["k"]), flat(b["t1"]), flat(b["f"]), ALU.subtract))
        ch(V.tensor_scalar(flat(b["t2"]), flat(b["f"]), -1.0, 60.0, ALU.mult, ALU.min), "hg_f2")
        yield 2
        w("f3", 1)
        for m in range(2):
            ins = V.tensor_scalar(b["t2"][:, m, :], b["t2"][:, m, :], LB[:, m:m + 1], None, ALU.mult)
        ch(ins)
        V.tensor_scalar_max(flat(b["t3"]), flat(b["t2"]), 1e9)
        ch(V.tensor_scalar_min(flat(b["x"][0]), flat(b["t2"]), 1e9))
        ch(V.tensor_copy(flat(b["t2"]), flat(b["x"][0])), "hg_f4")
        w("f5", 1)
        ch(V.tensor_tensor(flat(b["f"]), flat(b["t1"]), flat(b["t2"]), ALU.add))
        ch(V.tensor_tensor(flat(b["f"]), flat(b["f"]), flat(b["t3"]), ALU.add))
        w("k1", 1)
        for m in range(2):
            ins = V.tensor_scalar(b["k"][:, m, :], b["k"][:, m, :], OMLB[:, m:m + 1], None, ALU.mult)
        ch(ins, "lin_qk")
        yield from linear_dve(dve, ch, "hg", b, 2, "hg_norm", 0)

    def gl_act(act, ch):
        b = GB
        w = lambda nm, v: act.wait_ge(sems["gl_" + nm], v)
        act.wait_ge(sems["lin_done"], 1)
        load_tile(act, ("gl_a", 0), b["al"], "z_in")
        load_tile(act, ("gl_qk", 0), b["q"][:, 0, :], "z_in")
        load_tile(act, ("gl_qk", 1), b["k"][:, 0, :], "z_in")
        for m in range(2):
            load_tile(act, ("gl_g", m), b["g"][:, m, :], "z_in")
            load_tile(act, ("gl_v", m), flat(b["v"][:, 2 * m:2 * m + 2, :]), "z_in")
        yield 2
        act.wait_ge(sems["z_in"], 16 * 15)
        sig_act(ch, flat(b["u1"]), flat(b["u2"]), flat(b["g"]), name="gl_g1")
        yield 1
        w("g2", 1)
        ch(A.activation(flat(b["u1"]), flat(b["u1"]), ACT.Exp), "gl_g3")
        yield 2
        w("u", 1)
        sig_act(ch, flat(b["t1"]), flat(b["t2"]), mx[5][:, :], bias=pa("gla_b"), name="gl_f1")
        yield from linear_act(act, ch, "gl", b, 1)

    def gl_dve(dve, ch):
        b = GB
        w = lambda nm, v: dve.wait_ge(sems["gl_" + nm], v)
        yield 2
        w("g1", 1)
        sig_dve(ch, flat(b["u1"]), flat(b["u1"]), flat(b["u2"]), "gl_g2")
        yield 1
        w("g3", 1)
        ch(V.tensor_tensor(flat(b["g"]), flat(b["g"]), flat(b["u1"]), ALU.mult))
        yield 2
        w("f1", 1)
        sig_dve(ch, flat(b["f"]), flat(b["t1"]), flat(b["t2"]))
        V.tensor_scalar_mul(flat(b["q"]), flat(b["q"]), float(GDK) ** -0.5)
        ch(V.tensor_scalar_mul(flat(b["f"]), flat(b["f"]), 1.0 / TAU), "lin_qk")
        yield from linear_dve(dve, ch, "gl", b, 1, "gla_norm", 2)

    AT_STEPS = [(pr, hh, blk) for pr in range(2) for hh in range(2) for blk in range(TB)]
    ROPE = [(nm, g, m) for g in range(N_DIL) for nm in ("at_q", "at_k") for m in range(2)]

    def rope_loaded(n):
        return ("at_z", 16 * NZ) if n < NZ else (f"at_z{n // 2}", 32)

    def attention_pe(pe):
        w = lambda nm, v: pe.wait_ge(*sems.at(nm, v))
        yield 3
        for n in range(len(ROPE)):
            w(*rope_loaded(n))
            if n >= 2:
                w("at_rope", n - 1)
            mm(mx[n % 2][:, :], rot, TZ[n % NZ], start=True, stop=True).then_inc(sems["at_rot"], 1)
            if n % 2:
                yield 1
        w("at_rope", len(ROPE))

        def scores(n):
            pr, hh, blk = AT_STEPS[n]
            bs = slice(blk * P, (blk + 1) * P)
            if n >= 2:
                w("at_sm", n - 1)
            s = mx[5 * (n % 2)]
            q = lambda g: QR[half(hh), 2 * g + pr, bs]
            if blk:
                mm(s[:, 0:256], q(0), KR[half(hh), pr, (blk - 1) * P:(blk + 1) * P], start=True, stop=True)
            else:
                mm(s[:, 128:256], q(0), KR[half(hh), pr, bs], start=True, stop=True)
            mm(s[:, 256:384], q(1), KR[half(hh), 2 + pr, bs], start=True, stop=True)
            mm(s[:, 384:512], q(2), KR[half(hh), 4 + pr, bs], start=True, stop=True).then_inc(sems["at_s"], 1)

        scores(0)
        for n, (pr, hh, blk) in enumerate(AT_STEPS):
            bs = slice(blk * P, (blk + 1) * P)
            if n + 1 < len(AT_STEPS):
                scores(n + 1)
            yield 1
            w("at_p", n + 1)
            for j in range(0 if blk else 1, 4):
                ins = tr(mx[1][:, j * P:(j + 1) * P], PE_[:, n % 2, j * P:(j + 1) * P], ident)
            ins.then_inc(sems["at_pt"], 1)
            yield 1
            w("at_ptc", n + 1)
            if n == 0:
                w("at_va", 16 * 6)
            if n == 8:
                w("at_num", 1)
            vs = slice((2 * pr + hh) * HD, (2 * pr + hh + 1) * HD)
            pt = PT[:, n % 2, :]
            for g in range(N_DIL):
                o = mx[2 + g][half(hh), bs]
                if g == 0 and blk:
                    mm(o, VA[:, blk - 1, vs], pt[:, 0:P], start=True, stop=False)
                ins = mm(o, VA[:, g * TB + blk, vs], pt[:, (1 + g) * P:(2 + g) * P], start=not (g == 0 and blk),
                         stop=True)
            ins.then_inc(sems["at_n"], 1)
            if n % 8 != 7:
                continue
            w("at_st", pr + 1)
            tr(mx[5][0:48, 0:P], ST[:, pr, :], ident).then_inc(sems["at_str"], 1)
            yield 1
            w("at_strc", pr + 1)
            for q in range(2):
                for g in range(N_DIL):
                    k = q * N_DIL + g
                    if k:
                        w("at_bca" if k <= 3 else "at_bcd", pr * 3 + (k if k <= 3 else k - 3))
                    for hh2 in range(2):
                        for b2 in range(TB):
                            row = ((g * 2 + q) * 2 + hh2) * TB + b2
                            ins = mm(mx[5][half(hh2), b2 * P:(b2 + 1) * P],
                                     ident[0:48, row:row + 1].to_broadcast([48, HD]), STR[0:48, :],
                                     start=True, stop=True)
                    ins.then_inc(sems["at_bcp"], 1)
                    if k == 2:
                        yield 1
            yield 1
            w("at_bcd", pr * 3 + 3)

    def nat(v, g):
        if g == 0:
            return v
        return v.rearrange("p (r j) -> p j r", r=ORDER[g])

    def perm(v, g):
        if g == 0:
            return v
        return v.rearrange("p (j r) -> p j r", r=ORDER[g])

    def at_act(act, ch):
        w = lambda nm, v: act.wait_ge(*sems.at(nm, v))
        w("lin_done", 2)
        act.dma_start(ATC, t["consts"][:, N_CONST:]).then_inc(sems["at_cst"], 16)
        for n in range(NZ):
            load_tile(act, ROPE[n], TZ[n], "at_z")
        for g in range(N_DIL):
            for m in range(2):
                load_tile(act, ("at_v", g, m), flat(VA[:, g * TB + 2 * m:g * TB + 2 * m + 2, :]), "at_va")
        yield 3
        for n in range(0, len(ROPE), 2):
            if n + NZ < len(ROPE):
                w("at_rope", n + 2)
                for j in range(2):
                    load_tile(act, ROPE[n + NZ + j], TZ[n + j], rope_loaded(n + NZ)[0])
            yield 1
        scale = float(HD) ** -0.5
        for n, (pr, hh, blk) in enumerate(AT_STEPS):
            w("at_sm", n + 1)
            if n >= 2:
                w("at_pt", n - 1)
            x, e, st = SMX[:, n % 2, :], PE_[:, n % 2, :], ST[:, pr, :]
            c = hh * TB + blk
            lo = 0 if blk else P
            for g, (a0, a1) in enumerate(((lo, 256), (256, 384), (384, 512))):
                col = (g * 2 + 1) * 2 * TB + c
                ins = A.activation(e[:, a0:a1], x[:, a0:a1], ACT.Exp, bias=NM[:, n % 2, g:g + 1], scale=scale,
                                   accum_out=st[:, col:col + 1])
            ch(ins, "at_p")
            yield 1
            w("at_pt", n + 1)
            ch(A.activation(PT[:, n % 2, lo:], mx[1][:, lo:], ACT.Copy), "at_ptc")
            yield 1
            if n % 8 != 7:
                continue
            w("at_str", pr + 1)
            ch(A.activation(STR[0:48, :], mx[5][0:48, 0:P], ACT.Copy), "at_strc")
            yield 1
            for g in range(N_DIL):
                w("at_bcp", pr * 6 + g + 1)
                ch(A.activation(perm(MN[:, g, :], g), nat(mx[5][:, :], g), ACT.Copy), "at_bca")
            w("at_c1", pr + 1)
            ch(A.activation(flat(CN), flat(CN), ACT.Exp, scale=scale), "at_c2")
            yield 1
            log_table()
            w("at_den", pr + 1)
            ch(A.activation(TP, DN, ACT.Ln))
            ch(A.activation(TP, TP, ACT.Exp, scale=-1.0), "at_rd")
            yield 1

    def at_dve(dve, ch):
        w = lambda nm, v: dve.wait_ge(*sems.at(nm, v))
        yield 3
        w("at_cst", 16)
        for n, (nm, g, m) in enumerate(ROPE):
            dst = (QR if nm == "at_q" else KR)[:, 2 * g + m, :]
            w("at_rot", n + 1)
            V.tensor_tensor(TC, TZ[n % NZ], cosT, ALU.mult)
            ch(V.tensor_tensor(TR, mx[n % 2][:, :], sinT, ALU.mult))
            ch(V.tensor_tensor(nat(dst, g), perm(TC, g), perm(TR, g), ALU.add), "at_rope")
            if n % 2:
                yield 1
        scale = float(HD) ** -0.5

        def maxima(n):
            pr, hh, blk = AT_STEPS[n]
            lo = 0 if blk else P
            c = hh * TB + blk
            x, s, nm = SMX[:, n % 2, :], mx[5 * (n % 2)], NM[:, n % 2, :]
            w("at_s", n + 1)
            if n >= 2:
                w("at_p", n - 1)
            ch(V.tensor_tensor(x[:, lo:], s[:, lo:], amask[:, lo:], ALU.add))
            st = ST[:, pr, :].rearrange("p (g q c) -> p g q c", g=3, q=2)
            V.tensor_reduce(st[:, 0, 0, c:c + 1], x[:, lo:256], AX.X, ALU.max)
            ch(V.tensor_reduce(st[:, 1:3, 0, c], x[:, 256:512].rearrange("p (g t) -> p g t", g=2), AX.X, ALU.max))
            ch(V.tensor_scalar_mul(nm[:, 0:3], st[:, :, 0, c], -scale), "at_sm")

        maxima(0)
        for n, (pr, hh, blk) in enumerate(AT_STEPS):
            if n + 1 < len(AT_STEPS):
                maxima(n + 1)
            yield 1
            yield 1
            if n % 8 != 7:
                continue
            w("at_p", n + 1)
            w("at_n", n + 1)
            dve.sem_inc(sems["at_st"], 1)
            yield 1
            w("at_bca", pr * 3 + 3)
            ch(V.tensor_tensor(MG, MN[:, 0, :], MN[:, 1, :], ALU.max))
            ch(V.tensor_tensor(MG, MG, MN[:, 2, :], ALU.max))
            ch(V.tensor_tensor(CN, MN, bc(MG, 3), ALU.subtract), "at_c1")
            yield 1
            w("at_c2", pr + 1)
            for g in range(N_DIL):
                w("at_bcp", pr * 6 + 4 + g)
                o = DN if g == 0 else TC
                ch(V.tensor_tensor(perm(o, g), nat(mx[5][:, :], g), perm(CN[:, g, :], g), ALU.mult), "at_bcd")
                if g:
                    ch(V.tensor_tensor(DN, DN, TC, ALU.add), "at_den" if g == 2 else None)
            for g in range(N_DIL):
                o = NU if g == 0 else TC
                ch(V.tensor_tensor(perm(o, g), nat(mx[2 + g][:, :], g), perm(CN[:, g, :], g), ALU.mult),
                   "at_num" if g == 2 else None)
                if g:
                    ch(V.tensor_tensor(NU, NU, TC, ALU.add))
            w("at_rd", pr + 1)
            w("step", DONE_AT[("br", D // (2 * P) - 1, 2, 1)])
            ch(V.tensor_tensor(OB[:, OB_AT[3] + pr, :], NU, TP, ALU.mult), "at_done")
            yield 1

    with nc.Fori(0, L) as li:
        with nc.Block() as block:
            @block.sync
            def _(sp):
                views = {"w_in": t["w_in"][li], "w_branch": t["w_branch"][li].rearrange("n w d -> (n w) d"),
                         "w_out": t["w_out"][li], "ffn_up": t["ffn_w_up"][li], "ffn_down": t["ffn_w_down"][li]}
                names = list(STRIP_AT)
                sp.dma_start(x_dram, X[:, :, :]).then_inc(sems["x_out_d"], 16)
                split = 0
                for j, pieces in enumerate(STRIPS):
                    if j >= RAW:
                        split += sum(1 for name, _ in HALVES if name == names[j - RAW])
                        sp.wait_ge(sems["split"], split)
                    if names[j] == ("out", 2):
                        sp.wait_ge(sems["x_out_d"], 16)
                        sp.wait_ge(sems["mt"], KT)
                        sp.dma_start(X[:, :, :], x_dram).then_inc(sems["x_in_d"], 16)
                    for at_, kind, col, width, k0, nk in pieces:
                        src = views[kind].rearrange("(k p) n -> p k n", p=P)[:, k0:k0 + nk, col:col + width]
                        sp.dma_start(RG[j % RAW][:, 0:nk, at_:at_ + width], src).then_inc(sems[f"ring{j % RAW}"], 16)
                    if names[j][0] == "gate":
                        _, d, n = names[j]
                        i = GATE_ITEMS.index((n, d))
                        if i >= 2:
                            n2, d2 = GATE_ITEMS[i - 2]
                            sp.wait_ge(sems["step"], DONE_AT[("br", d2, n2, 1)])
                        src = t["w_branch"][li][n].rearrange("(k p) n -> p k n", p=P)[:, :, d * 2 * P:(d + 1) * 2 * P]
                        sp.dma_start(BRG[i % 2][:, :, :], src).then_inc(sems[f"brring{i % 2}"], 16)

            need = []
            cnt = [0] * RAW
            for j, pieces in enumerate(STRIPS):
                cnt[j % RAW] += 16 * len(pieces)
                need.append(cnt[j % RAW])

            @block.gpsimd
            def _(pool):
                for h, (name, m) in enumerate(HALVES):
                    j, i = STRIP_AT[name], h % HALF_SLOTS
                    nk, cols = STRIPS[j][0][5], slice(m * P, (m + 1) * P)
                    raw, high, low = RG[j % RAW][:, 0:nk, cols], *(w[:, 0:nk, i * P:(i + 1) * P] for w in (WH, WL))
                    pool.wait_ge(sems[f"ring{j % RAW}"], need[j])
                    if h >= HALF_SLOTS:
                        pool.wait_ge(sems["step"], USED_AT[HALVES[h - HALF_SLOTS]])
                    nc.gpsimd.tensor_scalar(high, raw, 1.0, 0.0, ALU.mult, ALU.add).then_inc(sems["split_high"], 1)
                    pool.wait_ge(sems["split_high"], h + 1)
                    nc.gpsimd.tensor_tensor(low, raw, high.bitcast(F32), ALU.subtract).then_inc(sems["split"], 1)

            @block.tensor
            def _(pe):
                mm = nc.tensor.matmul

                def weights(strip, m):
                    h = HALF_AT[(strip, m)]
                    pe.wait_ge(sems["split"], h + 1)
                    at_ = h % HALF_SLOTS * P
                    return WH[:, :, at_:at_ + P], WL[:, :, at_:at_ + P]

                def begin(name):
                    i = TILE_AT[name]
                    if BEFORE[i] is not None:
                        e = TILES[BEFORE[i]][1]
                        pe.wait_ge(sems["out_act" if e == "a" else "out_dve"], taken(BEFORE[i]))
                    return PS[BANK[i]]

                def product(o, lhs, rhs, start, stop):
                    mm(o, lhs[1], rhs[0], start=start, stop=False)
                    mm(o, lhs[0], rhs[1], start=False, stop=False)
                    return mm(o, lhs[0], rhs[0], start=False, stop=stop)

                def fm(name, strip, m, rhs=(HH, HL), ready=None):
                    b = begin(name)
                    ws = weights(strip, m)
                    for k in range(KT):
                        if ready:
                            pe.wait_ge(sems[ready[0]], ready[1] + k + 1)
                        ins = product(b[:, :], [w[:, k, :] for w in ws], [x[:, k, :] for x in rhs], k == 0, k == KT - 1)
                        if k == KT - 1:
                            ins.then_inc(sems["step"], 1)
                        if k % 4 == 3:
                            yield

                def tm(name, strip, g=0):
                    for m in range(2):
                        b = begin((*name, m))
                        weights(strip, 1)
                        for j in range(2):
                            tb = 2 * m + j
                            for k in range(KT):
                                tok = [h[:, k, :].rearrange("p (j r) -> p r j", r=4)[:, tb, :] if ORDER[g] == 4 else
                                       h[:, k, tb * P:(tb + 1) * P] for h in (HH, HL)]
                                ins = product(b[:, j * 2 * P:(j + 1) * 2 * P], tok, (WH[:, k, :], WL[:, k, :]), k == 0,
                                              k == KT - 1)
                            if j:
                                ins.then_inc(sems["step"], 1)
                            yield

                def br(d, n, m):
                    i = GATE_ITEMS.index((n, d))
                    b = begin(("br", d, n, m))
                    pe.wait_ge(sems[f"brring{i % 2}"], 16 * (i // 2 + 1))
                    for k in range(2):
                        ins = mm(b[:, :], BRG[i % 2][:, k, m * P:(m + 1) * P], OB[:, OB_AT[n] + k, :], start=k == 0,
                                 stop=k == 1)
                    ins.then_inc(sems["step"], 1)
                    yield

                def stored():
                    yield from fm(("gl_a", 0), "gl_a", 0)
                    for nm in ("hg_q", "hg_f", "hg_i", "hg_g", "gl_qk", "gl_v", "gl_g"):
                        if token_major((nm,)):
                            yield from tm((nm,), nm)
                        else:
                            for m in range(2):
                                yield from fm((nm, m), nm, m)
                    for g in range(N_DIL):
                        for nm in ("at_q", "at_k"):
                            for m in range(2):
                                yield from fm((nm, g, m), (nm, g), m)
                        yield from tm(("at_v", g), ("at_v", g), g)

                def merge(n):
                    pe.wait_ge(sems[DONE[n][0]], DONE[n][1])
                    for d in range(D // (2 * P)):
                        for m in range(2):
                            yield from fm(("gate", d, n, m), ("gate", d, n), m)
                            yield from br(d, n, m)

                run(norm_pe(pe, 0))
                pe.wait_ge(sems["par"], 16)

                for nm in ("rw_r", "rw_k", "rw_v"):
                    for m in range(2):
                        run(fm((nm, m), nm, m, ready=("n_low", 0)))
                run(fm(("rw_sm", 0), "rw_sm", 0))
                filler = stored()
                interleave(rwkv_pe(pe), filler)
                rest = chain(filler, merge(2))
                interleave(linear_pe(pe, "hg", HB, 2, HD), rest)
                rest = chain(rest, merge(0))
                interleave(gl_pe(pe), rest)
                rest = chain(rest, merge(1))
                interleave(attention_pe(pe), rest)
                run(rest)
                run(merge(3))
                sums = norm_pe(pe, 1)
                for d in range(D // P):
                    run(fm(("out", d), ("out", d // 2), d % 2, rhs=(MTH, MTL), ready=("mt", 0) if d == 0 else None))
                    if d >= 2:
                        next(sums)
                run(sums)
                for c in range(0, FT, 2):
                    for nm in ("up", "gf"):
                        for m in range(2):
                            run(fm((nm, c + m), (nm, c // 2), m, ready=("n_low", KT) if c + m == 0 else None))
                for d in range(0, D // P, 2):
                    b = [begin(("down", d + m)) for m in range(2)]
                    for j in range(3):
                        for m in range(2):
                            ws = weights(("down", d // 2, j), m)
                            for k in range(KT * j, min(KT * (j + 1), FT)):
                                if d == 0 and m == 0:
                                    pe.wait_ge(sems["hff"], k + 1)
                                ins = product(b[m][:, :], [w[:, k % KT, :] for w in ws], (HFH[:, k, :], HFL[:, k, :]),
                                              k == 0, k == FT - 1)
                            ins.then_inc(sems["step"], 1)

            @block.scalar
            def _(act):
                ch = Chain(act, sems, "act_own")
                table["set"] = None
                log_table()
                act.dma_start(PRM[:, :], t["params"][li]).then_inc(sems["par"], 16)
                norm_act(act, ch, 0)
                act.wait_ge(sems["lb1"], 1)
                ch(A.activation(LBT[:, 2:6], LBT[:, 2:6], ACT.Exp), "lb2")

                def stored():
                    for name in STORED:
                        yield
                        yield
                        store_tile(act, ch, name)

                def merge(n):
                    for d in range(D // (2 * P)):
                        for m in range(2):
                            i = GATE_ITEMS.index((n, d)) * 2 + m
                            yield
                            yield
                            take_act(act, ("gate", d, n, m))
                            if i >= 4:
                                act.wait_ge(sems["out_dve"], taken(TILE_AT[("br", d, n, m)]) - 4)
                            table["set"] = "exp"
                            ch(A.activation(SG[i % 4], tile_bank(("gate", d, n, m))[:, :], ACT.Tanh, scale=0.5),
                               "out_act")
                            yield

                filler = stored()
                interleave(rwkv_act(act, ch), filler)
                rest = chain(filler, merge(2))
                interleave(hg_act(act, ch), rest)
                rest = chain(rest, merge(0))
                interleave(gl_act(act, ch), rest)
                rest = chain(rest, merge(1))
                interleave(at_act(act, ch), rest)
                run(rest)
                run(merge(3))
                norm_act(act, ch, 1, lambda k: act.wait_ge(sems["out_dve"], taken(TILE_AT[("out", k)])))
                for c in range(FT + 1):
                    if c < FT:
                        take_act(act, ("up", c))
                        if c == 0:
                            act.wait_ge(sems["uppad"], 1)
                        if c >= 2:
                            act.wait_ge(sems["conv"], c - 1)
                        ch(A.activation(UP[c % 2][:, 2:], tile_bank(("up", c))[:, :], ACT.Copy), "out_act")
                    if c >= 1:
                        act.wait_ge(sems["conv"], c)
                        ch(A.activation(FS[(c - 1) % 2], FC[(c - 1) % 3], ACT.Sigmoid), "fsig")

            @block.vector
            def _(dve):
                ch = Chain(dve, sems, "dve_own")
                dve.wait_ge(sems["par"], 16)
                norm_dve(dve, 0, "norm_mix")
                t0, t1 = (PC_[:, PA["lb"] + 2 * l:PA["lb"] + 2 * l + 2] for l in range(2))
                ch(V.tensor_tensor(LBT[:, 0:2], t0, t1, ALU.max))
                V.tensor_tensor(LBT[:, 2:4], t0, LBT[:, 0:2], ALU.subtract)
                ch(V.tensor_tensor(LBT[:, 4:6], t1, LBT[:, 0:2], ALU.subtract), "lb1")
                dve.wait_ge(sems["lb2"], 1)
                ch(V.tensor_tensor(LBT[:, 6:8], LBT[:, 2:4], LBT[:, 4:6], ALU.add))
                ch(V.reciprocal(LBT[:, 6:8], LBT[:, 6:8]))
                V.tensor_tensor(LBT[:, 8:10], LBT[:, 2:4], LBT[:, 6:8], ALU.mult)
                ch(V.tensor_tensor(LBT[:, 10:12], LBT[:, 4:6], LBT[:, 6:8], ALU.mult))
                ch(V.scalar_tensor_tensor(LBT[:, 12:14], LBT[:, 10:12], FLAG[:, 0:1], LBT[:, 8:10], ALU.mult, ALU.add))
                ch(V.tensor_tensor(LB[:, :], LBT[:, 12:14], LBT[:, 8:10], ALU.subtract))
                ch(V.tensor_scalar(OMLB[:, :], LB[:, :], -1.0, 1.0, ALU.mult, ALU.add))

                def tile(name):
                    dve.wait_ge(sems["step"], DONE_AT[name])
                    return tile_bank(name)[:, :]

                def merge(n):
                    for d in range(D // (2 * P)):
                        for m in range(2):
                            i = GATE_ITEMS.index((n, d)) * 2 + m
                            yield
                            yield
                            yield
                            if i == 0:
                                dve.wait_ge(sems["x_out_d"], 16)
                            dve.wait_ge(sems["out_act"], taken(TILE_AT[("gate", d, n, m)]))
                            b = tile(("br", d, n, m))
                            mt = MT[:, 2 * d + m, :]
                            o = mt if n == BR_ORDER[0] else MTMP[i % 2]
                            ch(V.scalar_tensor_tensor(o, SG[i % 4], 1.0, b, ALU.add, ALU.mult), "out_dve")
                            if n != BR_ORDER[0]:
                                ch(V.tensor_tensor(mt, mt, o, ALU.add))
                            if n == BR_ORDER[-1]:
                                high = MTH[:, 2 * d + m, :]
                                ch(V.tensor_scalar(high, mt, 0.5, 0.0, ALU.mult, ALU.add))
                                ch(V.scalar_tensor_tensor(MTL[:, 2 * d + m, :], mt, 0.5, high.bitcast(F32), ALU.mult,
                                                          ALU.subtract), "mt")

                filler = (None for _ in range(2 * len(STORED)))
                interleave(rwkv_dve(dve, ch), filler)
                rest = chain(filler, merge(2))
                interleave(hg_dve(dve, ch), rest)
                rest = chain(rest, merge(0))
                interleave(gl_dve(dve, ch), rest)
                rest = chain(rest, merge(1))
                interleave(at_dve(dve, ch), rest)
                run(rest)
                run(merge(3))
                dve.wait_ge(sems["x_in_d"], 16)
                for d in range(D // P):
                    ch(V.tensor_tensor(X[:, d, :], tile(("out", d)), X[:, d, :], ALU.add), "out_dve")
                norm_dve(dve, 1, "norm_ffn")
                for u in range(2):
                    ins = V.memset(UP[u][:, 0:2], 0.0)
                ch(ins, "uppad")
                for c in range(FT):
                    u, f = UP[c % 2], FC[c % 3]
                    dve.wait_ge(sems["out_act"], taken(TILE_AT[("up", c)]))
                    ch(V.tensor_scalar(f, u[:, 2:], pb_("conv_w", c), pb_("conv_b", c), ALU.mult, ALU.add))
                    ch(V.scalar_tensor_tensor(f, u[:, 1:S + 1], pb_("conv_w", FT + c), f, ALU.mult, ALU.add))
                    ch(V.scalar_tensor_tensor(f, u[:, 0:S], pb_("conv_w", 2 * FT + c), f, ALU.mult, ALU.add), "conv")
                    dve.wait_ge(sems["fsig"], c + 1)
                    ch(V.tensor_tensor(FS[c % 2], FS[c % 2], f, ALU.mult))
                    ch(V.tensor_tensor(FS[c % 2], tile(("gf", c)), FS[c % 2], ALU.mult), "out_dve")
                    high = HFH[:, c, :]
                    ch(V.tensor_copy(high, FS[c % 2]))
                    ch(V.tensor_tensor(HFL[:, c, :], FS[c % 2], high.bitcast(F32), ALU.subtract), "hff")
                for d in range(D // P):
                    ch(V.tensor_tensor(X[:, d, :], tile(("down", d)), X[:, d, :], ALU.add), "out_dve")

        clear()

    with nc.Block() as block:
        @block.scalar
        def _(act):
            ch = Chain(act, sems, "act_own")
            table["set"] = None
            norm_act(act, ch, 0, split=False)

        @block.vector
        def _(dve):
            dve.wait_ge(sems["n_rstd"], 1)
            for k in range(KT):
                ins = V.scalar_tensor_tensor(HF[:, k, :], X[:, k, :], pa("final", k), RSTD[:, :], ALU.mult, ALU.mult)
            ins.then_inc(sems["n_h"], 1)

        @block.tensor
        def _(pe):
            run(norm_pe(pe, 0))

        @block.sync
        def _(sp):
            sp.wait_ge(sems["n_h"], 1)
            sp.dma_start(out, HF).then_inc(sems["x_out"], 16)
            sp.wait_ge(sems["x_out"], 16)


CONSTS = (("ident", P), ("ones", P), ("oblk", P), ("rot", P), ("lmask", 8 * P), ("rmask", 4 * P),
          ("rst64", S), ("rst128", S), ("cos", S), ("sin", S), ("amask", 4 * P))
N_CONST = sum(n for _, n in CONSTS[:8])


def constants():
    i = np.arange(P)
    row, col = i[:, None], i[None, :]
    c = {"ident": row == col, "ones": np.ones((P, P)), "oblk": row // HD == col // HD}
    hd = HD // 2
    c["rot"] = (row - hd == col) * (row % HD >= hd) * -1.0 + (row + hd == col) * (row % HD < hd) * 1.0
    lv = [(row // (2 * n) == col // (2 * n)) & (row // n % 2 == 0) & (col // n % 2 == 1) for n in LEVELS]
    c["lmask"] = np.concatenate(lv + [row == col], 1)
    neg = lambda ok: np.where(ok, 0.0, -BIG)
    c["amask"] = np.concatenate([neg(col >= row), neg(col <= row), neg(col <= row),
                                 neg(((row - col) % (DILS[2] // DILS[1]) == 0) & (col <= row))], 1)
    same = row // RC == col // RC
    strict, incl = same & (row < col), same & (row <= col)
    c["rmask"] = np.concatenate([strict, incl, strict, incl], 1)
    inv = 10000.0 ** (-np.arange(hd, dtype=np.float32) / np.float32(hd))
    ang = (inv.astype(np.float32)[:, None] * np.arange(S, dtype=np.float32)[None, :]).astype(np.float32)
    c["cos"], c["sin"] = (np.tile(f(ang.astype(np.float64)), (4, 1)) for f in (np.cos, np.sin))
    t_ = np.arange(S)
    c["rst64"], c["rst128"] = (np.tile((t_ % n != 0)[None, :], (P, 1)) for n in (RC, P))
    table = np.concatenate([np.asarray(c[nm], np.float32) for nm, _ in CONSTS], 1)
    cols = np.zeros((P, 8), np.float32)
    cols[:, C_ONE], cols[:, C_EPS], cols[:, C_GN] = 1.0, 1e-6, 64e-5
    cols[:, C_LOG] = LOG_SHIFT / 2 * np.log(2.0)
    cols[:, C_SM] = np.where(i < 32, 2.0, 1.0)
    return {"consts": np.ascontiguousarray(table), "const_cols": cols}


def parameters(v):
    out = np.zeros((L, P, N_PARAM), np.float32)
    for li in range(L):
        def put(half, name, src):
            c = (PA[name] if half == 0 else NPA + PB[name])
            out[li, :, c:c + src.size // P] = src.reshape(-1, P).T
        for nm, src in (("norm_mix", "norm_mix_w"), ("norm_ffn", "norm_ffn_w"), ("hg_norm", "hg_norm_w"),
                        ("gla_norm", "gla_norm_w"), ("gla_b", "gla_a_b"), ("w0", "rw_w0"), ("a0", "rw_a0"),
                        ("k_k", "rw_k_k"), ("k_a", "rw_k_a"), ("r_k", "rw_r_k"), ("ln_w", "rw_ln_w"),
                        ("ln_b", "rw_ln_b")):
            put(0, nm, v[src][li])
        put(0, "v0", v["rw_v0"][0])
        mu = v["rw_mu"][li]
        put(0, "mu_r", mu[0:W])
        put(0, "mu_k", mu[W + 32:2 * W + 32])
        put(0, "mu_v", mu[2 * W + 32:3 * W + 32])
        put(0, "mu_sm", np.concatenate([mu[W:W + 32], mu[3 * W + 32:]]))
        put(0, "lb", v["hg_lb_table"])
        put(0, "final", v["norm_final_w"])
        put(1, "conv_w", v["ffn_conv_w"][li])
        put(1, "conv_b", v["ffn_conv_b"][li])
        for nm, r0, src in (("lora", 0, v["rw_w2"][li]), ("lora", 32, v["rw_a2"][li]), ("lora", 64, v["rw_g2"][li]),
                            ("v1", 0, v["rw_v1"][0][:P]), ("v2", 0, v["rw_v2"][0]), ("aw2", 0, v["gla_a_w2"][li])):
            c = PARAM_AT[nm]
            out[li, r0:r0 + src.shape[0], c:c + src.shape[1]] = src
        out[li, :, PARAM_AT["v1"] + 32:PARAM_AT["v1"] + 64] = v["rw_v1"][0][P:]
        out[li, :, PARAM_AT["flags"]] = float(li > 0)
        out[li, :, PARAM_AT["flags"] + 1] = float(li == 0)
    return out


WEIGHTS = ("w_in", "w_branch", "w_out", "ffn_w_up", "ffn_w_down")


def kernel(**inputs):
    import concourse.bacc as bacc
    from concourse.bass_utils import run_bass_kernel_spmd

    nc = bacc.Bacc("TRN2", target_bir_lowering=False, num_devices=1)
    arrays = {n: np.ascontiguousarray(inputs[n]) for n in WEIGHTS}
    arrays["params"] = parameters({n: np.asarray(a) for n, a in inputs.items()
                                   if n not in WEIGHTS and n != "x"})
    arrays["x_fm"] = np.ascontiguousarray(np.asarray(inputs["x"])[0].T.reshape(KT, P, S).transpose(1, 0, 2))
    arrays.update(constants())
    t = {n: nc.dram_tensor(f"in_{n}", a.shape, F32, kind="ExternalInput").ap() for n, a in arrays.items()}
    out = nc.dram_tensor("out", (P, KT, S), F32, kind="ExternalOutput").ap()
    build(nc, t, out)
    r = run_bass_kernel_spmd(nc, [{f"in_{n}": a for n, a in arrays.items()}], core_ids=[0])
    return np.ascontiguousarray(np.asarray(r.results[0]["out"]).transpose(2, 1, 0).reshape(1, S, D))
```
